# Optimizing a Trainium2 kernel written in Bass

```python
import math
import jax, jax.numpy as jnp
from jax import lax
import numpy as np

D_MODEL = 1024
BATCH = 1
SEQ = 512
DEPTH = 2

N_MEM = 256
N_MIXERS = 2
N_A = (DEPTH + 1) // 2
N_B = DEPTH // 2
MIX_WIDTH = D_MODEL
MEM_HEADS = 4
MEM_HEAD_DIM = MIX_WIDTH // 4 // MEM_HEADS
MEM_WIDTH = MEM_HEADS * MEM_HEAD_DIM
MIXER_WIDTH = MIX_WIDTH - MEM_WIDTH

GLA_HEADS = 4
GLA_DV = MIXER_WIDTH // GLA_HEADS
GLA_DK = GLA_DV // 2
GLA_HK = GLA_HEADS * GLA_DK
GLA_GATE_RANK = 16
GLA_GATE_TAU = 16.0
GLA_CHUNK = 64
GLA_IN = 2 * GLA_HK + MIXER_WIDTH + GLA_GATE_RANK + MEM_WIDTH + MIX_WIDTH

DIL_GROUPS = ((128, 1), (512, 4), (2048, 16))
DIL_HEADS = 6
DIL_HEAD_DIM = MIXER_WIDTH // DIL_HEADS
DIL_IN = len(DIL_GROUPS) * 3 * MIXER_WIDTH + MEM_WIDTH + MIX_WIDTH

ROPE_THETA = 500000.0
ROPE_DIM = DIL_HEAD_DIM // 4
NORM_EPS = 1e-6


def rmsnorm(x, w):
    xf = x.astype(jnp.float32)
    y = xf * lax.rsqrt(jnp.mean(xf * xf, axis=-1, keepdims=True) + NORM_EPS)
    return (y * w.astype(jnp.float32)).astype(x.dtype)

def partial_rope(x, pos):
    half = ROPE_DIM // 2
    inv = ROPE_THETA ** (-jnp.arange(half, dtype=jnp.float32) / half)
    ang = pos.astype(jnp.float32)[:, None] * inv[None, :]
    cos = jnp.cos(ang)[None, :, None, :]
    sin = jnp.sin(ang)[None, :, None, :]
    xr = x[..., :ROPE_DIM].astype(jnp.float32)
    x1, x2 = xr[..., :half], xr[..., half:]
    rot = jnp.concatenate([x1 * cos - x2 * sin, x1 * sin + x2 * cos], axis=-1).astype(x.dtype)
    return jnp.concatenate([rot, x[..., ROPE_DIM:]], axis=-1)

def memory_attention(q, mem_n, w_memkv):
    B, T, _ = q.shape
    kv = mem_n @ w_memkv
    k, v = jnp.split(kv, 2, axis=-1)
    q = q.reshape(B, T, MEM_HEADS, MEM_HEAD_DIM)
    k = k.reshape(B, N_MEM, MEM_HEADS, MEM_HEAD_DIM)
    v = v.reshape(B, N_MEM, MEM_HEADS, MEM_HEAD_DIM)
    s = jnp.einsum('bthd,bnhd->bhtn', q, k).astype(jnp.float32) * (MEM_HEAD_DIM ** -0.5)
    p = jax.nn.softmax(s, axis=-1).astype(v.dtype)
    o = jnp.einsum('bhtn,bnhd->bthd', p, v)
    return o.reshape(B, T, MEM_WIDTH)

def gla_chunked(q, k, v, log_a):
    B, T, H, Dk = q.shape
    Dv = v.shape[-1]
    C = GLA_CHUNK
    N = T // C
    f32 = jnp.float32
    q = (q.astype(f32) * (Dk ** -0.5)).reshape(B, N, C, H, Dk)
    k = k.astype(f32).reshape(B, N, C, H, Dk)
    v = v.astype(f32).reshape(B, N, C, H, Dv)
    b = jnp.cumsum(log_a.astype(f32).reshape(B, N, C, H, Dk), axis=2)
    b_last = b[:, :, -1:]
    q_in = q * jnp.exp(b)
    k_in = k * jnp.exp(-b)
    k_out = k * jnp.exp(b_last - b)
    A = jnp.einsum('bnihd,bnjhd->bnhij', q_in, k_in)
    causal = jnp.tril(jnp.ones((C, C), dtype=bool))
    A = jnp.where(causal, A, 0.0)
    o_intra = jnp.einsum('bnhij,bnjhe->bnihe', A, v)
    dS = jnp.einsum('bnjhd,bnjhe->nbhde', k_out, v)
    decay = jnp.exp(b_last[:, :, 0]).transpose(1, 0, 2, 3)

    def step(S, inp):
        dS_c, dec_c = inp
        return dec_c[..., None] * S + dS_c, S

    S0 = jnp.zeros((B, H, Dk, Dv), f32)
    _, S_prev = lax.scan(step, S0, (dS, decay))
    o_inter = jnp.einsum('bnihd,nbhde->bnihe', q_in, S_prev)
    return (o_intra + o_inter).reshape(B, T, H, Dv)

def gla_mixer(h, w_in, w_gate_up, b_gate, gla_norm_w):
    B, T, _ = h.shape
    proj = h @ w_in
    cuts = np.cumsum([GLA_HK, GLA_HK, MIXER_WIDTH, GLA_GATE_RANK, MEM_WIDTH]).tolist()
    q, k, v, g_low, q_mem, gate = jnp.split(proj, cuts, axis=-1)
    log_a = jax.nn.log_sigmoid((g_low @ w_gate_up + b_gate).astype(jnp.float32)) / GLA_GATE_TAU
    o = gla_chunked(q.reshape(B, T, GLA_HEADS, GLA_DK),
                    k.reshape(B, T, GLA_HEADS, GLA_DK),
                    v.reshape(B, T, GLA_HEADS, GLA_DV),
                    log_a.reshape(B, T, GLA_HEADS, GLA_DK))
    o = rmsnorm(o, gla_norm_w).astype(h.dtype).reshape(B, T, MIXER_WIDTH)
    return o, q_mem, gate

def dilated_group(q, k, v, window, dilation):
    B, T, H, Dh = q.shape
    r = dilation
    n = window // dilation
    L = T // r
    nb = -(-L // n)
    Lp = nb * n

    def phase_blocks(x):
        x = x.reshape(B, L, r, H, Dh).transpose(0, 2, 3, 1, 4)
        x = jnp.pad(x, ((0, 0), (0, 0), (0, 0), (0, Lp - L), (0, 0)))
        return x.reshape(B, r, H, nb, n, Dh)

    def with_prev(x):
        prev = jnp.pad(x, ((0, 0), (0, 0), (0, 0), (1, 0), (0, 0), (0, 0)))[:, :, :, :-1]
        return jnp.concatenate([prev, x], axis=4)

    qb = phase_blocks(q)
    kw = with_prev(phase_blocks(k))
    vw = with_prev(phase_blocks(v))
    s = jnp.einsum('bphjqd,bphjkd->bphjqk', qb, kw).astype(jnp.float32) * (Dh ** -0.5)
    qi = jnp.arange(n)[:, None] + n
    ki = jnp.arange(2 * n)[None, :]
    dist = qi - ki
    key_abs = jnp.arange(nb)[:, None, None] * n + ki[None] - n
    mask = (dist >= 0)[None] & (dist <= n)[None] & (key_abs >= 0)
    s = jnp.where(mask, s, -jnp.inf)
    m = jnp.max(s, axis=-1, keepdims=True)
    p = jnp.exp(s - m)
    den = jnp.sum(p, axis=-1, keepdims=True)
    o = jnp.einsum('bphjqk,bphjkd->bphjqd', (p / den).astype(v.dtype), vw)
    lse = (m + jnp.log(den))[..., 0]
    o = o.reshape(B, r, H, Lp, Dh)[:, :, :, :L].transpose(0, 3, 1, 2, 4).reshape(B, T, H, Dh)
    lse = lse.reshape(B, r, H, Lp)[..., :L].transpose(0, 3, 1, 2).reshape(B, T, H)
    return o, lse

def dilated_mixer(h, w_in):
    B, T, _ = h.shape
    pos = jnp.arange(T)
    outs, lses = [], []
    for g, (window, dil) in enumerate(DIL_GROUPS):
        base = g * 3 * MIXER_WIDTH
        qkv = (h @ w_in[:, base:base + 3 * MIXER_WIDTH]).reshape(B, T, 3, DIL_HEADS, DIL_HEAD_DIM)
        q = partial_rope(qkv[:, :, 0], pos)
        k = partial_rope(qkv[:, :, 1], pos)
        o, lse = dilated_group(q, k, qkv[:, :, 2], window, dil)
        outs.append(o)
        lses.append(lse)
    wts = jax.nn.softmax(jnp.stack(lses, axis=0), axis=0)
    o = jnp.einsum('gbth,gbthd->bthd', wts, jnp.stack(outs, axis=0).astype(jnp.float32))
    o = o.astype(h.dtype).reshape(B, T, MIXER_WIDTH)
    rest = h @ w_in[:, len(DIL_GROUPS) * 3 * MIXER_WIDTH:]
    q_mem, gate = jnp.split(rest, [MEM_WIDTH], axis=-1)
    return o, q_mem, gate

def first_inputs(seed: int = 0) -> dict:
    key = jax.random.key(seed)
    ks = jax.random.split(key, 16)
    f32 = jnp.float32
    nrm = lambda k, shape, scale: jax.random.normal(k, shape, f32) * scale
    return {
        "x": nrm(ks[0], (BATCH, SEQ, D_MODEL), 1.0),
        "mem": nrm(ks[1], (BATCH, N_MEM, D_MODEL), 1.0),
        "mem_norm_w": 1.0 + nrm(ks[2], (D_MODEL,), 0.02),
        "norm_w": 1.0 + nrm(ks[3], (DEPTH, D_MODEL), 0.02),
        "w_memkv": nrm(ks[4], (DEPTH, D_MODEL, 2 * MEM_WIDTH), D_MODEL ** -0.5),
        "w_out": nrm(ks[5], (DEPTH, MIX_WIDTH, D_MODEL), MIX_WIDTH ** -0.5),
        "w_in_a": nrm(ks[6], (N_A, D_MODEL, GLA_IN), D_MODEL ** -0.5),
        "w_gate_up": nrm(ks[7], (N_A, GLA_GATE_RANK, GLA_HK), GLA_GATE_RANK ** -0.5),
        "b_gate": nrm(ks[8], (N_A, GLA_HK), 0.1),
        "gla_norm_w": 1.0 + nrm(ks[9], (N_A, GLA_DV), 0.02),
        "w_in_b": nrm(ks[10], (N_B, D_MODEL, DIL_IN), D_MODEL ** -0.5),
        "final_norm_w": 1.0 + nrm(ks[11], (D_MODEL,), 0.02),
    }

def first_block(x, mem, mem_norm_w, norm_w, w_memkv, w_out, w_in_a, w_gate_up, b_gate,
              gla_norm_w, w_in_b, final_norm_w):
    mem_n = rmsnorm(mem, mem_norm_w)
    for i in range(DEPTH):
        h = rmsnorm(x, norm_w[i])
        j = i // N_MIXERS
        if i % N_MIXERS == 0:
            mix, q_mem, gate = gla_mixer(h, w_in_a[j], w_gate_up[j], b_gate[j], gla_norm_w[j])
        else:
            mix, q_mem, gate = dilated_mixer(h, w_in_b[j])
        mem_o = memory_attention(q_mem, mem_n, w_memkv[i])
        branch = jnp.concatenate([mix, mem_o], axis=-1) * jax.nn.silu(gate)
        x = x + branch @ w_out[i]
    return rmsnorm(x, final_norm_w)


GRID_W = 64
CTX_LEN = 256
HEAD_DIM = 64
ROPE_THETA_2 = 10000.0
Q_BLOCK = 128
RMS_EPS = 1e-6
H_A = 8
NOPE_A = 64
ROPE_A = 32
V_A = 64
Q_LORA = 384
KV_LORA = 256
H_B = 8
KV_B = 2
G_B = H_B // KV_B
AB_IN = Q_LORA + KV_LORA + ROPE_A + H_B * HEAD_DIM + 2 * KV_B * HEAD_DIM
AB_OUT = H_A * V_A + H_B * HEAD_DIM
H_C = 16
WIN_R = 8
WIN_C = 16
C_WIDTH = H_C * HEAD_DIM
N_GROUPS = 4
EXPERTS_PER_GROUP = 8
N_EXPERTS = N_GROUPS * EXPERTS_PER_GROUP
TOP_K = 2
D_EXPERT = 512
MOE_BLOCK = 128
N_EVEN = (DEPTH + 1) // 2
N_ODD = DEPTH // 2


def rmsnorm_2(x, g):
    xf = x.astype(jnp.float32)
    y = xf * lax.rsqrt(jnp.mean(xf * xf, axis=-1, keepdims=True) + RMS_EPS)
    return (y * g.astype(jnp.float32)).astype(x.dtype)

def modulate(x, g, shift, scale):
    return rmsnorm_2(x, g) * (1 + scale) + shift

def axial_rope_table(rows, cols, rot_dim):
    n = rot_dim // 4
    inv = ROPE_THETA_2 ** (-jnp.arange(n, dtype=jnp.float32) / n)
    ang = jnp.concatenate([rows[:, None] * inv, cols[:, None] * inv], axis=-1)
    return jnp.cos(ang), jnp.sin(ang)

def apply_rope(x, rope):
    cos, sin = rope
    cos = cos.astype(x.dtype)
    sin = sin.astype(x.dtype)
    x1 = x[..., 0::2]
    x2 = x[..., 1::2]
    return jnp.stack([x1 * cos - x2 * sin, x1 * sin + x2 * cos], axis=-1).reshape(x.shape)

def heads_to_tokens(o):
    b, h, t, d = o.shape
    return o.transpose(0, 2, 1, 3).reshape(b, t, h * d)

def attend(q, k, v):
    s = jnp.einsum('bhgqd,bhkd->bhgqk', q, k, preferred_element_type=jnp.float32)
    p = jax.nn.softmax(s, axis=-1).astype(v.dtype)
    return jnp.einsum('bhgqk,bhkd->bhgqd', p, v)

def prefix_attention(q, k_lat, v_lat, k_ctx, v_ctx):
    b, hk, g, s, d = q.shape
    nb = s // Q_BLOCK
    k_all = jnp.concatenate([k_ctx, k_lat], axis=2)
    v_all = jnp.concatenate([v_ctx, v_lat], axis=2)
    qb = q.reshape(b, hk, g, nb, Q_BLOCK, d).transpose(3, 0, 1, 2, 4, 5)
    o = lax.map(lambda qblk: attend(qblk, k_all, v_all), qb)
    return o.transpose(1, 2, 3, 0, 4, 5).reshape(b, hk, g, s, v_all.shape[-1])

def mixer_ab(h_ctx, h_lat, rope_a, rope_b, w_in, w_out, q_norm, w_q_up, kv_norm, w_kv_up, gq_norm, gk_norm, need_ctx):
    def project(h, ra, rb):
        bsz, t, _ = h.shape
        p = h @ w_in
        o0 = Q_LORA
        o1 = o0 + KV_LORA
        o2 = o1 + ROPE_A
        o3 = o2 + H_B * HEAD_DIM
        o4 = o3 + KV_B * HEAD_DIM
        cq, ckv, kr = p[..., :o0], p[..., o0:o1], p[..., o1:o2]
        gq, gk, gv = p[..., o2:o3], p[..., o3:o4], p[..., o4:]
        qa = (rmsnorm_2(cq, q_norm) @ w_q_up).reshape(bsz, t, H_A, NOPE_A + ROPE_A).transpose(0, 2, 1, 3)
        kva = (rmsnorm_2(ckv, kv_norm) @ w_kv_up).reshape(bsz, t, H_A, NOPE_A + V_A).transpose(0, 2, 1, 3)
        q_nope, q_rope = qa[..., :NOPE_A], qa[..., NOPE_A:]
        k_nope, va = kva[..., :NOPE_A], kva[..., NOPE_A:]
        k_rope = kr[:, None]
        if ra is not None:
            q_rope = apply_rope(q_rope, ra)
            k_rope = apply_rope(k_rope, ra)
        qa = jnp.concatenate([q_nope, q_rope], axis=-1) * ((NOPE_A + ROPE_A) ** -0.5)
        ka = jnp.concatenate([k_nope, jnp.broadcast_to(k_rope, (bsz, H_A, t, ROPE_A))], axis=-1)
        qb = rmsnorm_2(gq.reshape(bsz, t, H_B, HEAD_DIM).transpose(0, 2, 1, 3), gq_norm)
        kb = rmsnorm_2(gk.reshape(bsz, t, KV_B, HEAD_DIM).transpose(0, 2, 1, 3), gk_norm)
        vb = gv.reshape(bsz, t, KV_B, HEAD_DIM).transpose(0, 2, 1, 3)
        if rb is not None:
            qb = apply_rope(qb, rb)
            kb = apply_rope(kb, rb)
        qb = qb.reshape(bsz, KV_B, G_B, t, HEAD_DIM) * (HEAD_DIM ** -0.5)
        return qa[:, :, None], ka, va, qb, kb, vb

    qa_l, ka_l, va_l, qb_l, kb_l, vb_l = project(h_lat, rope_a, rope_b)
    qa_c, ka_c, va_c, qb_c, kb_c, vb_c = project(h_ctx, None, None)
    bsz, s = h_lat.shape[0], h_lat.shape[1]
    oa = prefix_attention(qa_l, ka_l, va_l, ka_c, va_c).reshape(bsz, H_A, s, V_A)
    ob = prefix_attention(qb_l, kb_l, vb_l, kb_c, vb_c).reshape(bsz, H_B, s, HEAD_DIM)
    out_lat = jnp.concatenate([heads_to_tokens(oa), heads_to_tokens(ob)], axis=-1) @ w_out
    out_ctx = None
    if need_ctx:
        t = h_ctx.shape[1]
        oa_c = attend(qa_c, ka_c, va_c).reshape(bsz, H_A, t, V_A)
        ob_c = attend(qb_c, kb_c, vb_c).reshape(bsz, H_B, t, HEAD_DIM)
        out_ctx = jnp.concatenate([heads_to_tokens(oa_c), heads_to_tokens(ob_c)], axis=-1) @ w_out
    return out_ctx, out_lat

def mixer_na(h_ctx, h_lat, nbr_idx, rel_idx, w_in, w_out, rpb, need_ctx):
    def project(h):
        bsz, t, _ = h.shape
        p = (h @ w_in).reshape(bsz, t, 3, H_C, HEAD_DIM).transpose(2, 0, 3, 1, 4)
        return p[0] * (HEAD_DIM ** -0.5), p[1], p[2]

    q_l, k_l, v_l = project(h_lat)
    q_c, k_c, v_c = project(h_ctx)
    bsz, s = h_lat.shape[0], h_lat.shape[1]
    nk = nbr_idx.shape[1]
    nb = s // Q_BLOCK
    rpb_flat = rpb.reshape(H_C, -1)
    qb = q_l.reshape(bsz, H_C, nb, Q_BLOCK, HEAD_DIM).transpose(2, 0, 1, 3, 4)
    idx_b = nbr_idx.reshape(nb, Q_BLOCK, nk)
    rel_b = rel_idx.reshape(nb, Q_BLOCK, nk)

    def one_block(args):
        qblk, ib, rb = args
        kg = jnp.take(k_l, ib, axis=2)
        vg = jnp.take(v_l, ib, axis=2)
        s_n = jnp.einsum('bhqd,bhqnd->bhqn', qblk, kg, preferred_element_type=jnp.float32) + rpb_flat[:, rb].astype(jnp.float32)
        s_c = jnp.einsum('bhqd,bhcd->bhqc', qblk, k_c, preferred_element_type=jnp.float32)
        p = jax.nn.softmax(jnp.concatenate([s_n, s_c], axis=-1), axis=-1).astype(v_l.dtype)
        return jnp.einsum('bhqn,bhqnd->bhqd', p[..., :nk], vg) + jnp.einsum('bhqc,bhcd->bhqd', p[..., nk:], v_c)

    o = lax.map(one_block, (qb, idx_b, rel_b))
    out_lat = o.transpose(1, 0, 3, 2, 4).reshape(bsz, s, C_WIDTH) @ w_out
    out_ctx = None
    if need_ctx:
        oc = attend(q_c[:, :, None], k_c, v_c)[:, :, 0]
        out_ctx = heads_to_tokens(oc) @ w_out
    return out_ctx, out_lat

def hier_moe(h, w_rg, b_rg, w_re, b_re, w_gate, w_up, w_down):
    n, d = h.shape
    hf = h.astype(jnp.float32)
    pg = jax.nn.softmax(hf @ w_rg.astype(jnp.float32) + b_rg.astype(jnp.float32), axis=-1)
    g_sel = jnp.argmax(pg, axis=-1)
    p_gsel = jnp.take_along_axis(pg, g_sel[:, None], axis=-1)
    le = (hf @ w_re.astype(jnp.float32) + b_re.astype(jnp.float32)).reshape(n, N_GROUPS, EXPERTS_PER_GROUP)
    le_sel = jnp.take_along_axis(le, g_sel[:, None, None], axis=1)[:, 0]
    top_p, top_i = lax.top_k(jax.nn.softmax(le_sel, axis=-1), TOP_K)
    gate_w = p_gsel * top_p / jnp.sum(top_p, axis=-1, keepdims=True)
    experts = g_sel[:, None] * EXPERTS_PER_GROUP + top_i

    nkk = n * TOP_K
    flat_e = experts.reshape(-1).astype(jnp.int32)
    flat_w = gate_w.reshape(-1)
    order = jnp.argsort(flat_e)
    sorted_e = flat_e[order]
    tok_sorted = (jnp.arange(nkk, dtype=jnp.int32) // TOP_K)[order]
    w_sorted = flat_w[order]
    counts = jnp.bincount(flat_e, length=N_EXPERTS)
    padded = ((counts + MOE_BLOCK - 1) // MOE_BLOCK) * MOE_BLOCK
    ends = jnp.cumsum(padded)
    pad_start = ends - padded
    start = jnp.cumsum(counts) - counts
    rank = jnp.arange(nkk, dtype=jnp.int32) - start[sorted_e]
    dest = pad_start[sorted_e] + rank
    total = -(-(nkk + N_EXPERTS * (MOE_BLOCK - 1)) // MOE_BLOCK) * MOE_BLOCK
    nblk = total // MOE_BLOCK
    buf_tok = jnp.full((total,), n, jnp.int32).at[dest].set(tok_sorted)
    h_pad = jnp.concatenate([h, jnp.zeros((1, d), h.dtype)], axis=0)
    x_buf = h_pad[buf_tok].reshape(nblk, MOE_BLOCK, d)
    blk_e = jnp.clip(jnp.searchsorted(ends, jnp.arange(nblk, dtype=ends.dtype) * MOE_BLOCK, side='right'), 0, N_EXPERTS - 1)

    def run_block(args):
        xb, e = args
        return (jax.nn.silu(xb @ w_gate[e]) * (xb @ w_up[e])) @ w_down[e]

    y = lax.map(run_block, (x_buf, blk_e)).reshape(total, d)
    return jnp.zeros((n, d), h.dtype).at[tok_sorted].add(y[dest] * w_sorted[:, None].astype(h.dtype))

def second_inputs(seed: int = 0) -> dict:
    key = jax.random.key(seed)
    ks = jax.random.split(key, 32)

    def nrm(k, shape, scale):
        return jax.random.normal(k, shape, jnp.float32) * scale

    def gain(k, shape):
        return 1.0 + nrm(k, shape, 0.1)

    D = D_MODEL
    return {
        "x": nrm(ks[0], (BATCH, SEQ, D), 1.0),
        "c": nrm(ks[1], (BATCH, D), 1.0),
        "ctx": nrm(ks[2], (BATCH, CTX_LEN, D), 1.0),
        "c_ctx": nrm(ks[3], (D,), 1.0),
        "w_ada": nrm(ks[4], (DEPTH, D, 6 * D), 0.02),
        "b_ada": nrm(ks[5], (DEPTH, 6 * D), 0.02),
        "norm_mix": gain(ks[6], (DEPTH, D)),
        "norm_ffn": gain(ks[7], (DEPTH, D)),
        "norm_final": gain(ks[8], (D,)),
        "ab_w_in": nrm(ks[9], (N_EVEN, D, AB_IN), D ** -0.5),
        "ab_w_out": nrm(ks[10], (N_EVEN, AB_OUT, D), AB_OUT ** -0.5),
        "mla_q_norm": gain(ks[11], (N_EVEN, Q_LORA)),
        "mla_w_q_up": nrm(ks[12], (N_EVEN, Q_LORA, H_A * (NOPE_A + ROPE_A)), Q_LORA ** -0.5),
        "mla_kv_norm": gain(ks[13], (N_EVEN, KV_LORA)),
        "mla_w_kv_up": nrm(ks[14], (N_EVEN, KV_LORA, H_A * (NOPE_A + V_A)), KV_LORA ** -0.5),
        "gqa_q_norm": gain(ks[15], (N_EVEN, HEAD_DIM)),
        "gqa_k_norm": gain(ks[16], (N_EVEN, HEAD_DIM)),
        "na_w_in": nrm(ks[17], (N_ODD, D, 3 * C_WIDTH), D ** -0.5),
        "na_w_out": nrm(ks[18], (N_ODD, C_WIDTH, D), C_WIDTH ** -0.5),
        "na_rpb": nrm(ks[19], (N_ODD, H_C, 2 * WIN_R - 1, 2 * WIN_C - 1), 0.1),
        "moe_w_rg": nrm(ks[20], (DEPTH, D, N_GROUPS), D ** -0.5),
        "moe_b_rg": nrm(ks[21], (DEPTH, N_GROUPS), 0.01),
        "moe_w_re": nrm(ks[22], (DEPTH, D, N_EXPERTS), D ** -0.5),
        "moe_b_re": nrm(ks[23], (DEPTH, N_EXPERTS), 0.01),
        "moe_w_gate": nrm(ks[24], (DEPTH, N_EXPERTS, D, D_EXPERT), D ** -0.5),
        "moe_w_up": nrm(ks[25], (DEPTH, N_EXPERTS, D, D_EXPERT), D ** -0.5),
        "moe_w_down": nrm(ks[26], (DEPTH, N_EXPERTS, D_EXPERT, D), D_EXPERT ** -0.5),
    }

def second_block(x, c, ctx, c_ctx, w_ada, b_ada, norm_mix, norm_ffn, norm_final, ab_w_in, ab_w_out, mla_q_norm, mla_w_q_up, mla_kv_norm, mla_w_kv_up, gqa_q_norm, gqa_k_norm, na_w_in, na_w_out, na_rpb, moe_w_rg, moe_b_rg, moe_w_re, moe_b_re, moe_w_gate, moe_w_up, moe_w_down):
    bsz, s, d = x.shape
    n_ctx = ctx.shape[1]
    rows_n = s // GRID_W
    wr = min(WIN_R, rows_n)
    t = jnp.arange(s, dtype=jnp.int32)
    r = t // GRID_W
    col = t % GRID_W
    rope_a = axial_rope_table(r.astype(jnp.float32), col.astype(jnp.float32), ROPE_A)
    rope_b = axial_rope_table(r.astype(jnp.float32), col.astype(jnp.float32), HEAD_DIM)
    rs = jnp.clip(r - wr // 2, 0, rows_n - wr)
    cs = jnp.clip(col - WIN_C // 2, 0, GRID_W - WIN_C)
    key_r = rs[:, None] + jnp.arange(wr, dtype=jnp.int32)[None]
    key_c = cs[:, None] + jnp.arange(WIN_C, dtype=jnp.int32)[None]
    nbr_idx = (key_r[:, :, None] * GRID_W + key_c[:, None, :]).reshape(s, wr * WIN_C)
    rel_idx = ((key_r - r[:, None] + WIN_R - 1)[:, :, None] * (2 * WIN_C - 1)
               + (key_c - col[:, None] + WIN_C - 1)[:, None, :]).reshape(s, wr * WIN_C)

    x_lat = x
    x_ctx = ctx
    silu_c = jax.nn.silu(c)
    silu_cc = jax.nn.silu(c_ctx)
    for l in range(DEPTH):
        last = l == DEPTH - 1
        mod_l = (silu_c @ w_ada[l] + b_ada[l])[:, None, :]
        mod_c = (silu_cc @ w_ada[l] + b_ada[l])[None, None, :]
        sh1, sc1, g1, sh2, sc2, g2 = jnp.split(mod_l, 6, axis=-1)
        sh1c, sc1c, g1c, sh2c, sc2c, g2c = jnp.split(mod_c, 6, axis=-1)
        h_l = modulate(x_lat, norm_mix[l], sh1, sc1)
        h_c = modulate(x_ctx, norm_mix[l], sh1c, sc1c)
        if l % 2 == 0:
            i = l // 2
            o_c, o_l = mixer_ab(h_c, h_l, rope_a, rope_b, ab_w_in[i], ab_w_out[i], mla_q_norm[i], mla_w_q_up[i],
                                mla_kv_norm[i], mla_w_kv_up[i], gqa_q_norm[i], gqa_k_norm[i], not last)
        else:
            i = l // 2
            o_c, o_l = mixer_na(h_c, h_l, nbr_idx, rel_idx, na_w_in[i], na_w_out[i], na_rpb[i], not last)
        x_lat = x_lat + g1 * o_l
        h_l = modulate(x_lat, norm_ffn[l], sh2, sc2)
        if not last:
            x_ctx = x_ctx + g1c * o_c
            h_c = modulate(x_ctx, norm_ffn[l], sh2c, sc2c)
            tokens = jnp.concatenate([h_c.reshape(-1, d), h_l.reshape(-1, d)], axis=0)
            y = hier_moe(tokens, moe_w_rg[l], moe_b_rg[l], moe_w_re[l], moe_b_re[l], moe_w_gate[l], moe_w_up[l], moe_w_down[l])
            n_c = bsz * n_ctx
            x_ctx = x_ctx + g2c * y[:n_c].reshape(bsz, n_ctx, d)
            x_lat = x_lat + g2 * y[n_c:].reshape(bsz, s, d)
        else:
            y = hier_moe(h_l.reshape(-1, d), moe_w_rg[l], moe_b_rg[l], moe_w_re[l], moe_b_re[l], moe_w_gate[l], moe_w_up[l], moe_w_down[l])
            x_lat = x_lat + g2 * y.reshape(bsz, s, d)
    return rmsnorm_2(x_lat, norm_final)


def setup_inputs(seed=0):
    out = dict(first_inputs(seed))
    for name, value in second_inputs(seed + 1).items():
        if name != "x":
            out[name + "_2"] = value
    return out


def reference(
    x, mem, mem_norm_w, norm_w, w_memkv, w_out, w_in_a, w_gate_up, b_gate, gla_norm_w, w_in_b,
    final_norm_w, c_2, ctx_2, c_ctx_2, w_ada_2, b_ada_2, norm_mix_2, norm_ffn_2, norm_final_2,
    ab_w_in_2, ab_w_out_2, mla_q_norm_2, mla_w_q_up_2, mla_kv_norm_2, mla_w_kv_up_2,
    gqa_q_norm_2, gqa_k_norm_2, na_w_in_2, na_w_out_2, na_rpb_2, moe_w_rg_2, moe_b_rg_2,
    moe_w_re_2, moe_b_re_2, moe_w_gate_2, moe_w_up_2, moe_w_down_2,
):
    x = first_block(
        x, mem, mem_norm_w, norm_w, w_memkv, w_out, w_in_a, w_gate_up, b_gate, gla_norm_w,
        w_in_b, final_norm_w,
    )
    return second_block(
        x, c_2, ctx_2, c_ctx_2, w_ada_2, b_ada_2, norm_mix_2, norm_ffn_2, norm_final_2,
        ab_w_in_2, ab_w_out_2, mla_q_norm_2, mla_w_q_up_2, mla_kv_norm_2, mla_w_kv_up_2,
        gqa_q_norm_2, gqa_k_norm_2, na_w_in_2, na_w_out_2, na_rpb_2, moe_w_rg_2, moe_b_rg_2,
        moe_w_re_2, moe_b_re_2, moe_w_gate_2, moe_w_up_2, moe_w_down_2,
    )


_drawn_inputs = setup_inputs


def setup_inputs(seed=0):
    import zlib

    import numpy as np

    out = dict(_drawn_inputs(seed))
    spreads = {}
    factors = {'mem_norm_w': 8.0,
     'gla_norm_w': 3.603,
     'norm_mix_2': 3.303,
     'mla_q_norm_2': 8.0,
     'mla_kv_norm_2': 3.005,
     'gqa_q_norm_2': 8.0,
     'gqa_k_norm_2': 7.578,
     'na_rpb_2': 6.588,
     'moe_b_rg_2': 5.02,
     'moe_b_re_2': 5.18}
    for name, (base, spread) in spreads.items():
        noise = np.random.default_rng([zlib.crc32(name.encode()), seed]).standard_normal(out[name].shape)
        drawn = base * np.exp(spread * noise) if base else spread * noise
        out[name] = __import__('jax').numpy.asarray(drawn.astype(out[name].dtype))
    for name, factor in factors.items():
        out[name] = (out[name] * factor).astype(out[name].dtype)
    return out
```

```python
from contextlib import ExitStack, contextmanager

import numpy as np
import concourse.bass as bass
from concourse import mybir

F32 = mybir.dt.float32
U32 = mybir.dt.uint32
ALU = mybir.AluOpType
ACT = mybir.ActivationFunctionType
AX = mybir.AxisListType.X

P = 128
D = 1024
KT = D // P
SEQ, CTX, NMEM = 512, 256, 256
LT, CT = SEQ // P, CTX // P
ALLT = SEQ + CTX
NT = LT + CT
EPS = 1e-6
NEG = -1.0e30
NEXP, DEXP = 32, 512
MAXJ = ALLT // P - 1
NBLK = NEXP + 2 * ALLT // P - 1
NSPAN = 384




class Token:
    def __init__(self, ctr, loop, shift, off):
        self.ctr, self.loop, self.shift, self.off = ctr, loop, shift, off

    def total(self):
        if self.loop is None:
            return self.off
        lp = self.loop
        return lp.base[self.ctr] + (lp.n - 1 + self.shift) * lp.rate.get(self.ctr.name, 0) + self.off


class Counter:
    def __init__(self, prog, name, unit, by_pool=False, prefix=False):
        self.prog, self.name, self.unit, self.by_pool, self.prefix = prog, name, unit, by_pool, prefix
        self.sem = prog.ctx.enter_context(prog.nc.semaphore("s_" + name))
        self.count = 0
        self.local = 0
        prog.counters.append(self)

    def counted(self, ins):
        ins.then_inc(self.sem, self.unit)
        if self.prog.loop is None:
            self.count += 1
            return Token(self, None, 0, self.count)
        self.local += 1
        return Token(self, self.prog.loop, 0, self.local)


class Slot:

    def __init__(self, prog, name, ap=None):
        self.name, self.ap, self.fill, self.free = f"{name}.{len(prog.slots)}", ap, [], []
        prog.slots.append(self)

    def put(self, *toks):
        self.fill += toks

    def got(self, *toks):
        self.free += toks


class Loop:
    def __init__(self, name, n, i, base, rate):
        self.name, self.n, self.i, self.base, self.rate = name, n, i, base, rate


class Engine:
    def __init__(self, prog, name, eng, signals=True, anchor=False):
        self.prog, self.name, self.eng = prog, name, eng
        self.ctr = Counter(prog, name, 1) if signals else None
        self.seen = {}
        self.anchor = prog.ctx.enter_context(prog.nc.semaphore(f"s_{name}_anchor")) if anchor else None

    def wait(self, *toks):
        for t in toks:
            if t is None:
                continue
            lp = self.prog.loop
            if t.loop is not lp or lp is None:
                if lp is not None:
                    continue
                v = t.total()
                if self.seen.get(t.ctr, (0, 0))[1] >= v:
                    continue
                self.seen[t.ctr] = (0, v)
                self.eng.wait_ge(t.ctr.sem, v * t.ctr.unit)
                continue
            key = (t.shift, t.off)
            if self.seen.get(t.ctr, (-9, 0)) >= key:
                continue
            self.seen[t.ctr] = key
            r = lp.rate.get(t.ctr.name, 0)
            const = (lp.base[t.ctr] + t.shift * r + t.off) * t.ctr.unit
            assert self.prog.plan is None or const > 0, (t.ctr.name, const)
            self.eng.wait_ge(t.ctr.sem, lp.i * (r * t.ctr.unit) + const if r else max(const, 1))
            if self.anchor is not None:
                self.eng.sem_inc(self.anchor, 1)

    def take(self, *slots):
        for s in slots:
            self.wait(*(s.free or s.fill))

    def need(self, *slots):
        for s in slots:
            self.wait(*s.fill)

    def __call__(self, method, *args, after=(), sig=True, **kw):
        self.wait(*after)
        ins = method(*args, **kw)
        return self.ctr.counted(ins) if sig else None

    def dma(self, stream, out, in_, after=()):
        self.wait(*after)
        return stream.counted(self.eng.dma_start(out, in_))


def renew(*slots):
    for s in slots:
        s.fill, s.free = [], []


class Prog:
    def __init__(self, nc, ctx, plan):
        self.nc, self.ctx, self.plan, self.found = nc, ctx, plan, {}
        self.counters, self.slots, self.loop = [], [], None
        self.pe = Engine(self, "pe", nc.tensor)
        self.act = Engine(self, "act", nc.scalar)
        self.dve = Engine(self, "dve", nc.vector)
        self.pool = Engine(self, "pool", nc.gpsimd, anchor=True)
        self.sp = Engine(self, "sp", nc.sync, signals=False, anchor=True)
        self.engines = [self.pe, self.act, self.dve, self.pool, self.sp]

    def everything(self):
        return [Token(c, None, 0, c.count) for c in self.counters if c.count and not c.prefix]

    def barrier(self):
        for e in self.engines:
            e.wait(*self.everything())

    @contextmanager
    def repeat(self, name, n):
        plan = (self.plan or {}).get(name, {"rate": {}, "slots": {}})
        rate = plan["rate"]
        for c in self.counters:
            lack = rate.get(c.name, 0) - c.count
            if lack > 0 and not c.by_pool:
                self.nc.sync.sem_inc(c.sem, lack * c.unit)
                c.count += lack
        self.barrier()
        byname = {c.name: c for c in self.counters}
        with self.nc.Fori(0, n) as i:
            lp = self.loop = Loop(name, n, i, {c: c.count for c in self.counters}, rate)
            for c in self.counters:
                c.local = 0
            for e in self.engines:
                e.seen = {}
            for s in self.slots:
                fill, free = plan["slots"].get(s.name, ([], []))
                s.fill = [Token(byname[c], lp, -1, o) for c, o in fill]
                s.free = [Token(byname[c], lp, -1, o) for c, o in free]
            yield i

            def left(toks):
                return [(t.ctr.name, t.off) for t in toks if t.loop is lp and t.shift == 0]
            self.found[name] = {"rate": {c.name: c.local for c in self.counters if c.local},
                                "slots": {s.name: (left(s.fill), left(s.free)) for s in self.slots}}
            if self.plan is not None:
                assert self.found[name]["rate"] == rate, (name, rate, self.found[name]["rate"])
        self.loop = None
        for e in self.engines:
            e.seen = {}
        for c in self.counters:
            c.count += n * rate.get(c.name, c.local)
            c.local = 0
        for s in self.slots:
            s.fill, s.free = [], []
        self.barrier()

    @contextmanager
    def only_if(self, cond):
        before = {c: c.local for c in self.counters}
        owner = {e.ctr: e for e in self.engines if e.ctr}
        seen = [dict(e.seen) for e in self.engines]
        with self.nc.If(cond):
            yield
        with self.nc.Else():
            for c in self.counters:
                if c.local > before[c] and not c.prefix:
                    e = owner.get(c, self.sp)
                    e.wait(Token(c, self.loop, 0, 0))
                    e.eng.sem_inc(c.sem, (c.local - before[c]) * c.unit)
        for e, s in zip(self.engines, seen):
            e.seen = s


def shape_constants():
    c = {}
    r = np.arange(P)
    q, k = r[:, None], r[None, :]
    c["ident"] = np.eye(P, dtype=np.float32)
    c["gla_mask"] = ((q // 64 == k // 64) & (q <= k)).astype(np.float32)
    c["chunk_reset"] = np.broadcast_to((np.arange(SEQ) % 64 != 0).astype(np.float32), (96, SEQ)).copy()
    neg = np.float32(NEG)

    def block(ok):
        return np.where(ok, np.float32(0), neg).astype(np.float32)
    blocks = [block(k >= q), block(k <= q)]
    for dil in (4, 16):
        same = (q - k) % dil == 0
        blocks += [block(same)] * (LT - 1) + [block(same & (k <= q))]
    c["dil_mask"] = np.concatenate(blocks, axis=1)
    half = 16
    inv = np.float32(500000.0) ** (-np.arange(half, dtype=np.float32) / np.float32(half))
    ang = inv[:, None].astype(np.float32) * np.arange(SEQ, dtype=np.float32)[None, :]
    c["dil_cos"] = np.concatenate([np.cos(ang)] * 2).astype(np.float32)
    c["dil_sin"] = np.concatenate([np.sin(ang)] * 2).astype(np.float32)
    rot = np.zeros((P, P), np.float32)
    for m in range(16):
        rot[m + 16, m], rot[m, m + 16] = -1, 1
    c["dil_rot"] = rot
    t = np.arange(SEQ)
    rows, cols = (t // 64).astype(np.float32), (t % 64).astype(np.float32)

    def axial(dim):
        n = dim // 4
        inv = np.float32(10000.0) ** (-np.arange(n, dtype=np.float32) / np.float32(n))
        ang = np.concatenate([inv[:, None] * rows, inv[:, None] * cols]).astype(np.float32)
        cos = np.ones((dim, ALLT), np.float32)
        sin = np.zeros((dim, ALLT), np.float32)
        cos[:, CTX:] = np.repeat(np.cos(ang), 2, axis=0)
        sin[:, CTX:] = np.repeat(np.sin(ang), 2, axis=0)
        return cos, sin
    cb, sb = axial(64)
    c["gqa_cos"], c["gqa_sin"] = np.concatenate([cb, cb]), np.concatenate([sb, sb])
    ca, sa = axial(32)
    c["mla_cos"], c["mla_sin"] = np.zeros((96, ALLT), np.float32), np.zeros((96, ALLT), np.float32)
    c["mla_cos"][64:], c["mla_sin"][64:] = ca, sa
    pair = np.zeros((P, P), np.float32)
    for m in range(0, P, 2):
        pair[m + 1, m], pair[m, m + 1] = -1, 1
    c["pair_rot"] = pair
    c["head_sum"] = (q // 64 == k // 64).astype(np.float32)
    pick = np.zeros((64, 64, P), np.float32)
    for kc in range(64):
        for cc in range(64):
            cs = min(max(cc - 8, 0), 48)
            for half_ in range(2):
                if cs <= kc < cs + 16:
                    pick[32 * half_ + kc - cc + 15, kc, 64 * half_ + cc] = 1
                else:
                    pick[32 * half_ + 31, kc, 64 * half_ + cc] = 1
    c["na_pick"] = pick.reshape(64, 64 * P)
    c["before"] = (q < k).astype(np.float32)
    c["iota32"] = np.broadcast_to(np.arange(32, dtype=np.float32), (P, 32)).copy()
    c["token_ids"] = (r[:, None] + P * np.arange(NT)[None, :]).astype(np.uint32)
    c["zero_table"] = np.zeros((P, NBLK), np.uint32)
    return c


def build(nc, A, out, plan):
    ctx = ExitStack()
    with ctx:
        p = Prog(nc, ctx, plan)
        pe, act, dve, pool, sp = p.pe, p.act, p.dve, p.pool, p.sp
        T, S, V, G = nc.tensor, nc.scalar, nc.vector, nc.gpsimd

        def ctr(name):
            return Counter(p, name, 16)

        uses = {}

        def sb(stack, name, shape, dt=F32):
            uses[name] = uses.get(name, -1) + 1
            name = f"{name}_{uses[name]}" if uses[name] else name
            return stack.enter_context(nc.sbuf_tensor(name, shape, dt))

        PS = ctx.enter_context(nc.psum_tensor("PS", [P, 8, 512], F32))
        PF = PS[:, :, :].rearrange("p b c -> p (b c)")
        B = [Slot(p, f"bank{b}", PS[:, b, :]) for b in range(8)]

        d_const, d_w = ctr("d_const"), [ctr("d_w0"), ctr("d_w1")]
        d_bc, d_wo, d_st, d_g, d_ada = (ctr("d_bc"), ctr("d_wo"), ctr("d_st"), ctr("d_g"),
                                        [ctr("d_ada0"), ctr("d_ada1")])
        d_y, d_h, d_mo = ([ctr(f"{n}{j}") for j in range(2)] for n in ("d_y", "d_h", "d_mo"))
        d_x, d_yg = ([Counter(p, f"{n}{j}", 16, by_pool=True) for j in range(2)] for n in ("d_x", "d_yg"))
        d_idx = Counter(p, "d_idx", 16, by_pool=True)
        d_xo = [Counter(p, f"d_xo{j}", 16, by_pool=True, prefix=True) for j in range(2)]

        X = sb(ctx, "X", [P, NT, D])
        hT = sb(ctx, "hT", [P, KT, ALLT])
        OT = sb(ctx, "OT", [P, NT, D])
        s_hT = Slot(p, "hT")
        s_OT = Slot(p, "OT")
        s_X = [Slot(p, f"X{t}") for t in range(NT)]
        ident = sb(ctx, "ident", [P, P])
        ones = sb(ctx, "ones", [P, P])
        small = sb(ctx, "small", [P, 64])
        s_small = Slot(p, "small")
        hrow = [sb(ctx, f"hrow{n}", [P, D]) for n in range(2)]
        s_hrow = [Slot(p, f"hrow{n}") for n in range(2)]
        eps_c = sb(ctx, "eps_c", [P, 1])

        mods = nc.dram_tensor("mods", [2, 2, 6 * D], F32, kind="Internal").ap()
        h_dram = nc.dram_tensor("h_dram", [ALLT, D], F32, kind="Internal").ap()
        y_dram = nc.dram_tensor("y_dram", [NBLK * P, D], F32, kind="Internal").ap()
        table = [nc.dram_tensor(f"table{n}", [P * NBLK, 1], U32, kind="Internal").ap() for n in range(2)]

        def bcast(row_ap, n):
            return row_ap.rearrange("(a n) -> a n", a=1).to_broadcast([P, n])

        sp.dma(d_const, ident[:], A["c_ident"])
        sp.dma(d_const, X[:, CT:, :], A["x"][0].rearrange("(t p) d -> p t d", p=P))
        t = sp.dma(d_const, X[:, :CT, :], A["ctx_2"][0].rearrange("(t p) d -> p t d", p=P))
        t1 = dve(V.memset, ones[:], 1.0)
        t2 = dve(V.memset, eps_c[:], EPS)
        for s in s_X:
            s.put(t)
        consts_ready = [t, t1, t2]
        for e in (pe, act, dve, pool):
            e.wait(*consts_ready)

        t = dve(V.memset, hrow[0][:], 0.0)
        for b in range(NEXP, NBLK):
            tz = sp.dma(d_st, y_dram[b * P:(b + 1) * P, :], hrow[0][:], after=[t])
        s_hrow[0].got(tz)

        def rstd_of(sums, width, n, after, scratch):
            t = act(S.activation, scratch, sums, ACT.Ln, bias=eps_c[0:n, :], scale=1.0 / width, after=after)
            return act(S.activation, scratch, scratch, ACT.Exp, scale=-0.5, after=[t])

        def transpose_tile(src, k_tiles, dst_T, col, banks, src_fill, src_slot, dst_slot):
            for g0 in range(0, k_tiles, 4):
                b = banks[(g0 // 4) % len(banks)]
                pe.take(B[b])
                pe.wait(*src_fill)
                renew(B[b])
                for j in range(4):
                    tk = pe(T.transpose, PS[:, b, j * P:(j + 1) * P], src[:, (g0 + j) * P:(g0 + j + 1) * P],
                            ident[:], sig=(j == 3))
                B[b].put(tk)
                src_slot.got(tk)
                ev, cp = (act, S.copy) if (g0 // 4) % 2 else (dve, V.tensor_copy)
                tk = ev(cp, dst_T[:, g0:g0 + 4, col:col + P],
                        PS[:, b, :].rearrange("p (j c) -> p j c", j=4), after=[tk])
                B[b].got(tk)
                dst_slot.put(tk)

        def norm_to_T(tiles, gains, shifts, dst_T, dst_slot, cols, to_dram=None):
            n = len(tiles)
            act.take(s_small)
            for t in s_hrow:
                act.take(t)
            renew(s_small)
            for j, (x_ap, x_slot) in enumerate(tiles):
                act.need(x_slot)
                tk = act(S.activation, hrow[j % 2][:], x_ap, ACT.Square, accum_out=small[:, j:j + 1],
                         after=[tk] if j else [])
                x_slot.got(tk)
            tk = rstd_of(small[:, 0:n], D, P, [tk], small[:, 8:8 + n])
            for s in s_hrow:
                s.free = [tk]
                s.fill = []
            for e in (pe, act, dve):
                e.take(dst_slot)
            renew(dst_slot)
            for j, (x_ap, x_slot) in enumerate(tiles):
                s = s_hrow[j % 2]
                dve.take(s)
                renew(s)
                a = dve(V.scalar_tensor_tensor, hrow[j % 2][:], x_ap, small[:, 8 + j:9 + j], gains[j],
                        ALU.mult, ALU.mult, after=[tk])
                x_slot.got(a)
                if shifts is not None:
                    a = dve(V.tensor_tensor, hrow[j % 2][:], hrow[j % 2][:], shifts[j], ALU.add, after=[a])
                s.put(a)
                s_small.got(a)
                transpose_tile(hrow[j % 2], KT, dst_T, cols[j], [2 * (j % 2), 2 * (j % 2) + 1], [a], s, dst_slot)
                if to_dram is not None:
                    s.got(sp.dma(d_h[j % 2], to_dram[cols[j]:cols[j] + P, :], hrow[j % 2][:], after=[a]))
            return

        lat_tiles = [(X[:, t, :], s_X[t]) for t in range(CT, NT)]
        all_tiles = [(X[:, t, :], s_X[t]) for t in range(NT)]

        def w_cols(w, start, width):
            return w.rearrange("(t p) m -> p t m", p=P)[:, :, start] if width is None else \
                w.rearrange("(t p) m -> p t m", p=P)[:, :, bass.ds(start, width)]

        def mm_acc(out_ap, pairs, sig=True, start=True, stop=True, **kw):
            n = len(pairs)
            for j, (a, b) in enumerate(pairs):
                tk = pe(T.matmul, out_ap, a, b, start=start and j == 0, stop=stop and j == n - 1,
                        sig=sig and j == n - 1, **kw)
            return tk

        def softmax_bufs(stack, cols, n_p=2):
            bufs = {"n": 0}
            bufs["P"] = [sb(stack, f"P{j}", [P, cols]) for j in range(2)]
            bufs["PT"] = [sb(stack, f"PT{j}", [P, cols]) for j in range(2)]
            bufs["st"] = [sb(stack, f"st{j}", [P, 4]) for j in range(3)]
            bufs["sP"] = [Slot(p, f"{cols}P{j}") for j in range(2)]
            bufs["sPT"] = [Slot(p, f"{cols}PT{j}") for j in range(2)]
            bufs["sst"] = [Slot(p, f"{cols}st{j}") for j in range(3)]
            return bufs

        def attend(units, bufs, s_banks, pt_banks, o_bank, dv):
            def score(u, x):
                banks = [B[b] for b in s_banks[x % len(s_banks)]]
                b0 = s_banks[x % len(s_banks)][0]
                src = PF[:, b0 * 512:b0 * 512 + u["n"]]
                pe.take(*banks)
                renew(*banks)
                tk = u["scores"](src)
                for b in banks:
                    b.put(tk)
                w, sP, sst, st = bufs["P"][x % 2], bufs["sP"][x % 2], bufs["sst"][x % 3], bufs["st"][x % 3]
                dve.take(sP, sst)
                act.take(sP)
                renew(sP, sst)
                if u.get("bias"):
                    toks = u["bias"](src, w, [tk])
                    for b in banks:
                        b.got(*toks)
                    src = w[:, 0:u["n"]]
                else:
                    toks = [tk]
                tk = dve(V.reduce_max, st[:, 0:1], src, AX, after=toks)
                tk = dve(V.tensor_scalar, st[:, 1:2], st[:, 0:1], -u["scale"], None, ALU.mult, after=[tk])
                tk = act(S.activation, w[:, 0:u["n"]], src, ACT.Exp, bias=st[:, 1:2], scale=u["scale"],
                         accum_out=st[:, 2:3], after=[tk] + toks)
                for b in banks:
                    b.got(tk)
                sP.put(tk)
                tk = dve(V.reciprocal, st[:, 3:4], st[:, 2:3], after=[tk])
                sst.put(tk)

            def turn(u, x):
                w, sP, wT, sPT = bufs["P"][x % 2], bufs["sP"][x % 2], bufs["PT"][x % 2], bufs["sPT"][x % 2]
                nb = u["n"] // P
                pe.need(sP)
                act.take(sPT)
                dve.take(sPT)
                renew(sPT)
                for g0 in range(0, nb, 4):
                    b = pt_banks[g0 // 4]
                    m = min(4, nb - g0)
                    pe.take(B[b])
                    renew(B[b])
                    for j in range(m):
                        tk = pe(T.transpose, PS[:, b, j * P:(j + 1) * P],
                                w[:, (g0 + j) * P:(g0 + j + 1) * P], ident[:], sig=(j == m - 1))
                    B[b].put(tk)
                    sP.got(tk)
                    ev, cp = (dve, V.tensor_copy) if g0 // 4 == 1 else (act, S.copy)
                    tk = ev(cp, wT[:, g0 * P:(g0 + m) * P], PS[:, b, 0:m * P], after=[tk])
                    B[b].got(tk)
                    sPT.put(tk)

            def values(u, x):
                wT, sPT, sst, st = bufs["PT"][x % 2], bufs["sPT"][x % 2], bufs["sst"][x % 3], bufs["st"][x % 3]
                nb = u["n"] // P
                pe.need(sPT)
                pe.take(B[o_bank])
                renew(B[o_bank])
                tk = mm_acc(PS[:, o_bank, 0:dv], [(wT[:, j * P:(j + 1) * P], u["v"](j)) for j in range(nb)])
                B[o_bank].put(tk)
                sPT.got(tk)
                act.need(sst)
                act.take(s_OT)
                tk = act(S.activation, u["out"], PS[:, o_bank, 0:dv], ACT.Copy, scale=st[:, 3:4], after=[tk])
                B[o_bank].got(tk)
                sst.got(tk)
                outs.append(tk)

            outs = []
            n = len(units)
            for x in range(n + 2):
                if x < n:
                    score(units[x], x)
                if 1 <= x <= n:
                    turn(units[x - 1], x - 1)
                if x >= 2:
                    values(units[x - 2], x - 2)
            return outs

        def gate_and_project(stack, layer_w_out, gate, tiles, row_gate=None):
            wo = sb(stack, "wo", [P, KT, D])
            s_wo = Slot(p, "wo")
            sp.take(s_wo)
            t = sp.dma(d_wo, wo[:], layer_w_out.rearrange("(t p) m -> p t m", p=P))
            s_wo.put(t)
            if gate is not None:
                w, off = gate
                wg = [sb(stack, f"wg{n}", [P, KT, 512]) for n in range(2)]
                s_wg = [Slot(p, f"wg{n}") for n in range(2)]
                sg = [sb(stack, f"sg{n}", [P, 512]) for n in range(2)]
                s_sg = [Slot(p, f"sg{n}") for n in range(2)]
                for c in range(2):
                    s_wg[c].put(sp.dma(d_w[c], wg[c][:], w_cols(w, off + 512 * c, 512)))
                x = 0
                for c in range(2):
                    for n, tl in enumerate(tiles):
                        b = 4 + x % 4
                        s = s_sg[x % 2]
                        v = sg[x % 2]
                        pe.take(B[b])
                        pe.need(s_wg[c])
                        renew(B[b])
                        tk = mm_acc(PS[:, b, :], [(hT[:, k, n * P:(n + 1) * P], wg[c][:, k, :]) for k in range(KT)])
                        B[b].put(tk)
                        s_hT.got(tk)
                        act.take(s)
                        renew(s)
                        tk = act(S.activation, v[:], PS[:, b, :], ACT.Exp, scale=-1.0, after=[tk])
                        tk = dve(V.tensor_scalar, v[:], v[:], 1.0, None, ALU.add, after=[tk])
                        tk = dve(V.reciprocal, v[:], v[:], after=[tk])
                        tk = dve(V.tensor_tensor, v[:], v[:], PS[:, b, :], ALU.mult, after=[tk])
                        B[b].got(tk)
                        tk = dve(V.tensor_tensor, OT[:, tl, 512 * c:512 * c + 512],
                                 OT[:, tl, 512 * c:512 * c + 512], v[:], ALU.mult, after=[tk])
                        s.got(tk)
                        s_OT.put(tk)
                        x += 1
            for e in (act, dve, pe):
                e.take(s_hT)
            renew(s_hT)
            for n, tl in enumerate(tiles):
                transpose_tile(OT[:, tl, :], KT, hT, n * P, [2 * (n % 2), 2 * (n % 2) + 1], s_OT.fill, s_OT, s_hT)
            tmp = sb(stack, "res_tmp", [P, 2, 512])
            s_tmp = [Slot(p, f"res_tmp{n}") for n in range(2)]
            pe.need(s_hT, s_wo)
            x = 0
            for n, tl in enumerate(tiles):
                for c in range(2):
                    b = 4 + x % 4
                    pe.take(B[b])
                    renew(B[b])
                    tk = mm_acc(PS[:, b, :], [(hT[:, k, n * P:(n + 1) * P], wo[:, k, 512 * c:512 * c + 512])
                                              for k in range(KT)])
                    B[b].put(tk)
                    s_hT.got(tk)
                    dve.take(s_X[tl])
                    xs = X[:, tl, 512 * c:512 * c + 512]
                    if row_gate is None:
                        tk = dve(V.tensor_tensor, xs, xs, PS[:, b, :], ALU.add, after=[tk])
                    else:
                        g = row_gate(tl)
                        dve.take(s_tmp[x % 2])
                        renew(s_tmp[x % 2])
                        tk = dve(V.tensor_tensor, tmp[:, x % 2, :], PS[:, b, :], g[:, 512 * c:512 * c + 512],
                                 ALU.mult, after=[tk])
                        B[b].got(tk)
                        tk = dve(V.tensor_tensor, xs, xs, tmp[:, x % 2, :], ALU.add, after=[tk])
                        s_tmp[x % 2].got(tk)
                    B[b].got(tk)
                    s_X[tl].put(tk)
                    x += 1
            s_OT.free, s_OT.fill = [], []
            p.barrier()

        with ExitStack() as st:
            cv = sb(st, "cv", [P, KT, 2])
            ce = sb(st, "ce", [P, KT, 2])
            with nc.allow_non_contiguous_dma("two vectors as columns"):
                sp.dma(d_bc, cv[:, :, 0], A["c_2"][0].rearrange("(t p) -> p t", p=P))
                t = sp.dma(d_bc, cv[:, :, 1], A["c_ctx_2"].rearrange("(t p) -> p t", p=P))
            t = act(S.activation, ce[:], cv[:], ACT.Exp, scale=-1.0, after=[t])
            t = dve(V.tensor_scalar, ce[:], ce[:], 1.0, None, ALU.add, after=[t])
            t = dve(V.reciprocal, ce[:], ce[:], after=[t])
            t_c = dve(V.tensor_tensor, cv[:], cv[:], ce[:], ALU.mult, after=[t])
            wa = [sb(st, f"wa{n}", [P, KT, 1024]) for n in range(2)]
            ba = [sb(st, f"ba{n}", [2, 1024]) for n in range(2)]
            mo = [sb(st, f"mo{n}", [2, 1024]) for n in range(2)]
            s_wa = [Slot(p, f"wa{n}") for n in range(2)]
            s_mo = [Slot(p, f"mo{n}") for n in range(2)]
            pe.wait(t_c)
            with p.repeat("ada", 6) as i:
                for l in range(2):
                    sp.take(s_wa[l])
                    renew(s_wa[l])
                    sp.dma(d_ada[l], wa[l][:], w_cols(A["w_ada_2"][l], i * 1024, 1024))
                    t = sp.dma(d_ada[l], ba[l][:], A["b_ada_2"][l:l + 1, bass.ds(i * 1024, 1024)].to_broadcast([2, 1024]))
                    s_wa[l].put(t)
                    pe.need(s_wa[l])
                    for c in range(2):
                        b = 2 * l + c
                        pe.take(B[b])
                        renew(B[b])
                        t = mm_acc(PS[0:2, b, :], [(cv[:, k, :], wa[l][:, k, c * 512:c * 512 + 512]) for k in range(KT)])
                        B[b].put(t)
                        s_wa[l].got(t)
                        if c == 0:
                            dve.take(s_mo[l])
                            renew(s_mo[l])
                            dve.need(s_wa[l])
                        t = dve(V.tensor_tensor, mo[l][:, c * 512:c * 512 + 512], PS[0:2, b, :],
                                ba[l][:, c * 512:c * 512 + 512], ALU.add, after=[t])
                        B[b].got(t)
                        s_mo[l].put(t)
                        s_wa[l].got(t)
                    s_mo[l].got(sp.dma(d_mo[l], mods[l, :, bass.ds(i * 1024, 1024)], mo[l][:], after=[t]))

        memx = ExitStack()
        memT = sb(memx, "memT", [P, KT, NMEM])
        s_memT = Slot(p, "memT")
        with ExitStack() as st:
            mem = sb(st, "mem", [P, NMEM // P, D])
            s_mem = Slot(p, "mem")
            gm = sb(st, "gm", [P, D])
            sp.dma(d_bc, mem[:], A["mem"][0].rearrange("(t p) d -> p t d", p=P))
            t = sp.dma(d_bc, gm[:], bcast(A["mem_norm_w"], D))
            s_mem.put(t)
            dve.wait(t)
            norm_to_T([(mem[:, n, :], s_mem) for n in range(2)], [gm[:]] * 2, None, memT, s_memT, [0, P])
            p.barrier()

        def first_norm(st, w):
            g = sb(st, "gn", [P, D])
            t = sp.dma(d_bc, g[:], bcast(w, D))
            dve.wait(t)
            norm_to_T(lat_tiles, [g[:]] * LT, None, hT, s_hT, [P * n for n in range(LT)])
            p.barrier()

        def memory_attention(layer, w_in, q_off):
            with ExitStack() as st:
                wm = [sb(st, f"wm{j}", [P, KT, P]) for j in range(3)]
                s_wm = Slot(p, "wm")
                qT = sb(st, "mqT", [P, SEQ])
                kz = sb(st, "mkz", [P, 2, NMEM])
                vv = sb(st, "mvv", [P, NMEM // P, P])
                s_q, s_k, s_v = Slot(p, "mq"), Slot(p, "mk"), Slot(p, "mv")
                bufs = softmax_bufs(st, NMEM)
                dve(V.memset, kz[:], 0.0)
                wkv = A["w_memkv"][layer]
                with p.repeat(f"memory{layer}", 2) as i:
                    sp.take(s_wm)
                    renew(s_wm)
                    sp.dma(d_w[0], wm[0][:], w_cols(w_in, i * P + q_off, P))
                    sp.dma(d_w[0], wm[1][:], w_cols(wkv, i * P, P))
                    s_wm.put(sp.dma(d_w[0], wm[2][:], w_cols(wkv, i * P + 256, P)))
                    pe.need(s_wm)
                    pe.take(B[7], B[6], B[5])
                    renew(B[7], B[6], B[5])
                    tq = mm_acc(PS[:, 7, :], [(wm[0][:, k, :], hT[:, k, 0:SEQ]) for k in range(KT)])
                    tk = mm_acc(PS[:, 6, 0:NMEM], [(wm[1][:, k, :], memT[:, k, :]) for k in range(KT)])
                    for n in range(2):
                        tv = mm_acc(PS[:, 5, n * P:(n + 1) * P],
                                    [(memT[:, k, n * P:(n + 1) * P], wm[2][:, k, :]) for k in range(KT)])
                    s_wm.got(tv)
                    act.take(s_q)
                    dve.take(s_k, s_v)
                    renew(s_q, s_k, s_v)
                    t = act(S.copy, qT[:], PS[:, 7, :], after=[tq])
                    s_q.put(t)
                    B[7].got(t)
                    dve(V.tensor_copy, kz[0:64, 0, :], PS[0:64, 6, 0:NMEM], after=[tk])
                    t = dve(V.tensor_copy, kz[64:P, 1, :], PS[64:P, 6, 0:NMEM])
                    s_k.put(t)
                    B[6].got(t)
                    t = dve(V.tensor_copy, vv[:].rearrange("p a b -> p (a b)"), PS[:, 5, 0:256], after=[tv])
                    s_v.put(t)
                    B[5].got(t)
                    pe.need(s_q, s_k, s_v)
                    units = []
                    for hh in range(2):
                        for n in range(LT):
                            units.append(dict(
                                n=NMEM, scale=64 ** -0.5,
                                scores=lambda o, hh=hh, n=n: mm_acc(o, [(qT[:, n * P:(n + 1) * P], kz[:, hh, :])]),
                                v=lambda j, hh=hh: vv[:, j, hh * 64:hh * 64 + 64],
                                out=OT[:, CT + n, bass.ds(i * P + (768 + 64 * hh), 64)]))
                    outs = attend(units, bufs, [[0], [1]], [2], 3, 64)
                    for s in (s_q, s_k, s_v):
                        s.got(*B[3].fill)
                s_OT.put()

        w_a = A["w_in_a"][0]
        with ExitStack() as st:
            first_norm(st, A["norm_w"][0])
        with ExitStack() as st:
            DK, DV, NC_ = 96, 192, SEQ // 64
            wl = sb(st, "wl", [P, KT, 16])
            glT = sb(st, "glT", [16, SEQ])
            gmask = sb(st, "gmask", [P, P])
            reset = sb(st, "reset", [DK, SEQ])
            gw = sb(st, "gw", [P, DV])
            wh = [sb(st, f"wh{n}", [P, KT, 2 * DK + DV]) for n in range(2)]
            wu = [sb(st, f"wu{n}", [16, DK]) for n in range(2)]
            bg = [sb(st, f"bg{n}", [DK, 1]) for n in range(2)]
            s_wh = [Slot(p, f"wh{n}") for n in range(2)]
            with nc.allow_non_contiguous_dma("16 columns"):
                sp.dma(d_bc, wl[:], w_cols(w_a, 1536, 16))
            sp.dma(d_bc, gmask[:], A["c_gla_mask"])
            sp.dma(d_bc, reset[:], A["c_chunk_reset"])
            t = sp.dma(d_bc, gw[:], bcast(A["gla_norm_w"][0], DV))
            pe.wait(t)
            t = mm_acc(PS[0:16, 0, :], [(wl[:, k, :], hT[:, k, 0:SEQ]) for k in range(KT)])
            t = act(S.copy, glT[:], PS[0:16, 0, :], after=[t])
            names = ["u", "l", "bc", "eb", "q", "k", "ko"]
            W = {n: sb(st, "g_" + n, [DK, SEQ]) for n in names}
            sW = {n: Slot(p, "g_" + n) for n in names}
            qz = sb(st, "g_qz", [DK, 2, SEQ])
            koz = sb(st, "g_koz", [P, 2, LT, DK])
            vv = sb(st, "g_v", [P, LT, DV])
            AT = sb(st, "g_AT", [P, SEQ])
            Sx = sb(st, "g_S", [DK, NC_, DV])
            sm = sb(st, "g_sm", [P, 8])
            junk = sb(st, "g_junk", [P, DV])
            s_qz, s_koz, s_vv, s_AT, s_S, s_sm = (Slot(p, n) for n in ("g_qz", "g_koz", "g_v", "g_AT", "g_S", "g_sm"))
            dve(V.memset, qz[:], 0.0)
            dve(V.memset, koz[:], 0.0)
            dve(V.memset, Sx[:], 0.0)

            def chunks(ap):
                return ap.rearrange("d (c t) -> d c t", t=64)

            def gla_head(h, w, wu_, bg_, s_w):
                q, k, kx = (w[:, :, 0:DK], w[:, :, DK:2 * DK], w[:, :, 2 * DK:])
                pe.need(s_w)
                pe.take(B[2], B[0], B[1])
                renew(B[2], B[0], B[1])
                tz = mm_acc(PS[0:DK, 2, :], [(wu_[:], glT[:])])
                tq = mm_acc(PS[0:DK, 0, :], [(q[:, j, :], hT[:, j, 0:SEQ]) for j in range(KT)])
                tk = mm_acc(PS[0:DK, 1, :], [(k[:, j, :], hT[:, j, 0:SEQ]) for j in range(KT)])
                pe.take(B[3], B[4])
                renew(B[3], B[4])
                for n in range(LT):
                    tv = mm_acc(PS[:, 3 + n // 2, (n % 2) * DV:(n % 2) * DV + DV],
                                [(hT[:, j, n * P:(n + 1) * P], kx[:, j, :]) for j in range(KT)])
                s_w.got(tv)
                act.take(s_vv)
                renew(s_vv)
                for j in range(2):
                    t = act(S.copy, vv[:, 2 * j:2 * j + 2, :],
                            PS[:, 3 + j, 0:2 * DV].rearrange("p (a b) -> p a b", a=2), after=[tv])
                    B[3 + j].got(t)
                s_vv.put(t)
                act.take(sW["u"])
                renew(sW["u"])
                act.need(s_w)
                t = act(S.activation, W["u"][:], PS[0:DK, 2, :], ACT.Identity, bias=bg_[:], after=[tz])
                B[2].got(t)
                s_w.got(t)
                dve.take(sW["l"])
                renew(sW["l"])
                a = dve(V.tensor_scalar, W["l"][:], W["u"][:], -1.0, None, ALU.mult, after=[t])
                a = dve(V.tensor_tensor, W["l"][:], W["l"][:], W["u"][:], ALU.min, after=[a])
                a = act(S.activation, W["l"][:], W["l"][:], ACT.Exp, after=[a])
                a = act(S.activation, W["l"][:], W["l"][:], ACT.Ln, bias=1.0, after=[a])
                a = dve(V.scalar_tensor_tensor, W["u"][:], W["u"][:], 0.0, W["l"][:], ALU.min, ALU.subtract, after=[a])
                sW["l"].got(a)
                dve.take(sW["bc"])
                renew(sW["bc"])
                tb = dve(V.tensor_tensor_scan, W["bc"][:], reset[:], W["u"][:], 0.0, ALU.mult, ALU.add, after=[a])
                sW["u"].got(tb)
                tau = 1.0 / 16.0
                act.take(sW["eb"])
                renew(sW["eb"])
                te = act(S.activation, W["eb"][:], W["bc"][:], ACT.Exp, scale=tau, after=[tb])
                act.take(sW["l"])
                renew(sW["l"])
                tn = act(S.activation, W["l"][:], W["bc"][:], ACT.Exp, scale=-tau, after=[tb])
                dve.take(sW["ko"])
                renew(sW["ko"])
                last = chunks(W["bc"][:])[:, :, 63:64].to_broadcast([DK, NC_, 64])
                t = dve(V.tensor_tensor, chunks(W["ko"][:]), last, chunks(W["bc"][:]), ALU.subtract, after=[tb])
                sW["bc"].got(te, tn, t)
                t = act(S.activation, W["ko"][:], W["ko"][:], ACT.Exp, scale=tau, after=[t])
                dve.take(sW["q"], sW["k"], s_qz)
                renew(sW["q"], sW["k"], s_qz)
                a = dve(V.scalar_tensor_tensor, W["q"][:], PS[0:DK, 0, :], DK ** -0.5, W["eb"][:], ALU.mult,
                        ALU.mult, after=[tq, te])
                B[0].got(a)
                sW["q"].put(a)
                b = dve(V.tensor_tensor, W["k"][:], PS[0:DK, 1, :], W["l"][:], ALU.mult, after=[tk, tn])
                sW["l"].got(b)
                sW["k"].put(b)
                c = dve(V.tensor_tensor, W["ko"][:], PS[0:DK, 1, :], W["ko"][:], ALU.mult, after=[t])
                B[1].got(b, c)
                for par in range(2):
                    src = W["q"][:].rearrange("d (n c t) -> d n c t", c=2, t=64)[:, :, par, :]
                    dst = qz[:, par, :].rearrange("d (n c t) -> d n c t", c=2, t=64)[:, :, par, :]
                    t = dve(V.tensor_copy, dst, src, after=[a])
                s_qz.put(t)
                sW["q"].got(t)
                pe.take(B[6], B[5])
                renew(B[6], B[5])
                pe.wait(c)
                for n in range(LT):
                    t = pe(T.transpose, PS[:, 6, n * DK:(n + 1) * DK], W["ko"][:, n * P:(n + 1) * P],
                           ident[0:DK, 0:DK], sig=(n == LT - 1))
                sW["ko"].got(t)
                B[6].put(t)
                dve.take(s_koz)
                renew(s_koz)
                for par in range(2):
                    r = slice(64 * par, 64 * par + 64)
                    t2 = dve(V.tensor_copy, koz[r, par, :, :].rearrange("p a b -> p (a b)"),
                             PS[r, 6, 0:LT * DK], after=[t])
                B[6].got(t2)
                s_koz.put(t2)
                pe.wait(b)
                for n in range(LT):
                    t = pe(T.matmul, PS[:, 5, n * P:(n + 1) * P], W["k"][:, n * P:(n + 1) * P],
                           W["q"][:, n * P:(n + 1) * P], start=True, stop=True, sig=(n == LT - 1))
                B[5].put(t)
                sW["k"].got(t)
                sW["q"].got(t)
                dve.take(s_AT)
                renew(s_AT)
                t = dve(V.tensor_tensor, AT[:].rearrange("p (n c) -> p n c", n=LT),
                        PS[:, 5, :].rearrange("p (n c) -> p n c", n=LT),
                        gmask[:].unsqueeze(1).to_broadcast([P, LT, P]), ALU.mult, after=[t])
                B[5].got(t)
                s_AT.put(t)
                pe.need(s_koz, s_vv)
                dve.take(s_S)
                renew(s_S)
                t = None
                for n0 in range(0, NC_ - 1, 2):
                    b = (0, 1, 2, 7)[n0 // 2]
                    pair_ = range(n0, min(n0 + 2, NC_ - 1))
                    pe.take(B[b])
                    renew(B[b])
                    for n in pair_:
                        a = pe(T.matmul, PS[0:DK, b, (n % 2) * DV:(n % 2) * DV + DV], koz[:, n % 2, n // 2, :],
                               vv[:, n // 2, :], start=True, stop=True)
                    B[b].put(a)
                    for n in pair_:
                        t = dve(V.scalar_tensor_tensor, Sx[:, n + 1, :], Sx[:, n, :],
                                W["eb"][:, 64 * n + 63:64 * n + 64], PS[0:DK, b, (n % 2) * DV:(n % 2) * DV + DV],
                                ALU.mult, ALU.add, after=[a, t])
                        s_S.put(t)
                    B[b].got(t)
                s_koz.got(a)
                sW["eb"].got(t)
                pe.need(s_AT, s_qz)
                pe.take(B[3], B[4])
                renew(B[3], B[4])
                act.take(s_sm)
                renew(s_sm)
                for n in range(LT):
                    pe.wait(s_S.fill[min(2 * n, NC_ - 2)])
                    o = PS[:, 3 + n // 2, (n % 2) * DV:(n % 2) * DV + DV]
                    t = mm_acc(o, [(AT[:, n * P:(n + 1) * P], vv[:, n, :]),
                                   (qz[:, 0, n * P:(n + 1) * P], Sx[:, 2 * n, :]),
                                   (qz[:, 1, n * P:(n + 1) * P], Sx[:, 2 * n + 1, :])])
                    B[3 + n // 2].put(t)
                for n in range(LT):
                    o = PS[:, 3 + n // 2, (n % 2) * DV:(n % 2) * DV + DV]
                    tn = act(S.activation, junk[:], o, ACT.Square, accum_out=sm[:, n:n + 1], after=[t, tn])
                for s in (s_AT, s_vv, s_qz, s_S):
                    s.got(t)
                tn = rstd_of(sm[:, 0:LT], DV, P, [tn], sm[:, 4:8])
                for n in range(LT):
                    o = PS[:, 3 + n // 2, (n % 2) * DV:(n % 2) * DV + DV]
                    t = dve(V.scalar_tensor_tensor, OT[:, CT + n, bass.ds(h, DV)], o, sm[:, 4 + n:5 + n], gw[:],
                            ALU.mult, ALU.mult, after=[tn])
                    B[3 + n // 2].got(t)
                s_sm.got(t)
                s_OT.put(t)

            with p.repeat("gla", 2) as i:
                for n in range(2):
                    s, w = s_wh[n], wh[n]
                    sp.take(s)
                    renew(s)
                    col = i * (2 * DK) + n * DK
                    sp.dma(d_w[n], w[:, :, 0:DK], w_cols(w_a, col, DK))
                    sp.dma(d_w[n], w[:, :, DK:2 * DK], w_cols(w_a, col + 384, DK))
                    sp.dma(d_w[n], w[:, :, 2 * DK:], w_cols(w_a, i * (2 * DV) + (n * DV + 768), DV))
                    sp.dma(d_w[n], wu[n][:], A["w_gate_up"][0][:, bass.ds(col, DK)])
                    s.put(sp.dma(d_w[n], bg[n][:],
                                 A["b_gate"][0].rearrange("(n a) -> n a", a=1)[bass.ds(col, DK), :]))
                for n in range(2):
                    gla_head(i * (2 * DV) + n * DV, wh[n], wu[n], bg[n], s_wh[n])
        memory_attention(0, w_a, 1552)
        with ExitStack() as st:
            gate_and_project(st, A["w_out"][0], (w_a, 1808), list(range(CT, NT)))

        w_b = A["w_in_b"][0]
        with ExitStack() as st:
            first_norm(st, A["norm_w"][1])
        with ExitStack() as st:
            mask = sb(st, "mask", [P, 10 * P])
            cosT, sinT = sb(st, "cosT", [32, SEQ]), sb(st, "sinT", [32, SEQ])
            rot = sb(st, "rot", [P, P])
            wq = [sb(st, f"wq{g}", [P, KT, 3, P]) for g in range(3)]
            s_wq = [Slot(p, f"wq{g}") for g in range(3)]
            d_q = [d_w[0], d_w[1], d_g]
            qk = [[sb(st, f"qk{g}{j}", [P, SEQ]) for j in range(2)] for g in range(3)]
            vg = [sb(st, f"vg{g}", [P, LT, P]) for g in range(3)]
            rt = [sb(st, f"rt{j}", [32, SEQ]) for j in range(2)]
            s_qk = [[Slot(p, f"qk{g}{j}") for j in range(2)] for g in range(3)]
            s_vg = [Slot(p, f"vg{g}") for g in range(3)]
            s_rt = [Slot(p, f"rt{j}") for j in range(2)]
            bufs = softmax_bufs(st, 10 * P)
            sp.dma(d_bc, mask[:], A["c_dil_mask"])
            sp.dma(d_bc, cosT[:], A["c_dil_cos"])
            sp.dma(d_bc, sinT[:], A["c_dil_sin"])
            sp.dma(d_bc, rot[:], A["c_dil_rot"])
            with p.repeat("dilated", 6) as h:
                for g in range(3):
                    sp.take(s_wq[g])
                    renew(s_wq[g])
                    for j in range(3):
                        t = sp.dma(d_q[g], wq[g][:, :, j, :], w_cols(w_b, h * P + (3 * g + j) * 768, P))
                    s_wq[g].put(t)
                for g in range(3):
                    pe.need(s_wq[g])
                    for j in range(2):
                        pe.take(B[j])
                        renew(B[j])
                        t = mm_acc(PS[:, j, :], [(wq[g][:, k, j, :], hT[:, k, 0:SEQ]) for k in range(KT)])
                        act.take(s_qk[g][j])
                        renew(s_qk[g][j])
                        t = act(S.copy, qk[g][j][:], PS[:, j, :], after=[t])
                        B[j].got(t)
                        s_qk[g][j].put(t)
                    pe.take(B[2])
                    renew(B[2])
                    for n in range(LT):
                        t = mm_acc(PS[:, 2, n * P:(n + 1) * P],
                                   [(hT[:, k, n * P:(n + 1) * P], wq[g][:, k, 2, :]) for k in range(KT)])
                    s_wq[g].got(t)
                    act.take(s_vg[g])
                    renew(s_vg[g])
                    t = act(S.copy, vg[g][:].rearrange("p a b -> p (a b)"), PS[:, 2, :], after=[t])
                    B[2].got(t)
                    s_vg[g].put(t)
                    for j in range(2):
                        b, x = 3 + j, qk[g][j][0:32, :]
                        pe.take(B[b])
                        renew(B[b])
                        pe.need(s_qk[g][j])
                        t = mm_acc(PS[:, b, :], [(rot[:], qk[g][j][:])])
                        dve.take(s_rt[j])
                        renew(s_rt[j])
                        t = dve(V.tensor_tensor, rt[j][:], PS[0:32, b, :], sinT[:], ALU.mult, after=[t])
                        B[b].got(t)
                        a = dve(V.tensor_tensor, x, x, cosT[:], ALU.mult, after=[t])
                        t = dve(V.tensor_tensor, x, x, rt[j][:], ALU.add, after=[a])
                        s_rt[j].got(t)
                        s_qk[g][j].put(t)
                for g in range(3):
                    pe.need(*s_qk[g], s_vg[g])
                units = []
                for n in range(LT):
                    lo = max(n - 1, 0)
                    spans = [(0, lo, n + 1)] + [(1, 0, n + 1), (2, 0, n + 1)]
                    mcol = [(2 - (n + 1 - lo)) * P, (2 + LT - n - 1) * P, (2 + 2 * LT - n - 1) * P]
                    blocks = [(g, b) for g, a, z in spans for b in range(a, z)]

                    def scores(o, n=n, blocks=blocks):
                        tk = None
                        for x, (g, b) in enumerate(blocks):
                            tk = pe(T.matmul, o[:, x * P:(x + 1) * P], qk[g][0][:, n * P:(n + 1) * P],
                                    qk[g][1][:, b * P:(b + 1) * P], start=True, stop=True,
                                    sig=(x == len(blocks) - 1))
                        return tk

                    def bias(src, dst, toks, spans=spans, mcol=mcol):
                        at, out_ = 0, []
                        for (g, a, z), mc in zip(spans, mcol):
                            w = (z - a) * P
                            out_.append(dve(V.tensor_tensor, dst[:, at:at + w], src[:, at:at + w],
                                            mask[:, mc:mc + w], ALU.add, after=toks))
                            at += w
                        return out_

                    units.append(dict(n=len(blocks) * P, scale=P ** -0.5, scores=scores, bias=bias,
                                      v=lambda j, blocks=blocks: vg[blocks[j][0]][:, blocks[j][1], :],
                                      out=OT[:, CT + n, bass.ds(h * P, P)]))
                attend(units, bufs, [[0, 1, 2]], [3, 4, 5], 6, P)
                for g in range(3):
                    for s in (*s_qk[g], s_vg[g]):
                        s.got(*B[6].fill)
        memory_attention(1, w_b, 6912)
        with ExitStack() as st:
            gate_and_project(st, A["w_out"][1], (w_b, 7168), list(range(CT, NT)))
        memx.close()

        def norm_rows(st, w, tiles, dst):
            g = sb(st, "gf", [P, D])
            junk = sb(st, "fjunk", [P, D])
            t = sp.dma(d_bc, g[:], bcast(w, D))
            act.wait(t)
            dve.wait(t)
            t = None
            for j, tl in enumerate(tiles):
                t = act(S.activation, junk[:], X[:, tl, :], ACT.Square, accum_out=small[:, j:j + 1], after=[t])
            t = rstd_of(small[:, 0:LT], D, P, [t], small[:, 8:8 + LT])
            for j, tl in enumerate(tiles):
                a = dve(V.scalar_tensor_tensor, dst(tl), X[:, tl, :], small[:, 8 + j:9 + j], g[:],
                        ALU.mult, ALU.mult, after=[t])
            p.barrier()

        with ExitStack() as st:
            norm_rows(st, A["final_norm_w"], range(CT, NT), lambda tl: X[:, tl, :])

        def modulation(st, layer, part, norm_w, who):
            g, s = sb(st, f"mg{who}", [P, D]), sb(st, f"ms{who}", [P, D])
            w = sb(st, f"mw{who}", [P, D])
            stream = (d_bc, d_wo)[who]
            row = mods[layer, who]
            sp.dma(stream, s[:], bcast(row[(3 * part) * D:(3 * part + 1) * D], D))
            sp.dma(stream, g[:], bcast(row[(3 * part + 1) * D:(3 * part + 2) * D], D))
            t = sp.dma(stream, w[:], bcast(norm_w, D))
            dve(V.scalar_tensor_tensor, g[:], g[:], 1.0, w[:], ALU.add, ALU.mult, after=[t])
            return g, s

        def modulated_T(layer, part, norm_w, tiles, to_dram=None):
            with ExitStack() as st:
                gl, sl = modulation(st, layer, part, norm_w, 0)
                gc, sc = modulation(st, layer, part, norm_w, 1) if 0 in tiles else (None, None)
                dve.wait(*p.everything())
                norm_to_T([(X[:, t, :], s_X[t]) for t in tiles], [gc[:] if t < CT else gl[:] for t in tiles],
                          [sc[:] if t < CT else sl[:] for t in tiles], hT, s_hT,
                          [P * j for j in range(len(tiles))], to_dram)
                p.barrier()

        def row_gates(st, layer, part, with_ctx):
            gs = []
            for who in range(2 if with_ctx else 1):
                g = sb(st, f"rg{who}", [P, D])
                t = sp.dma(d_bc, g[:], bcast(mods[layer, who, (3 * part + 2) * D:(3 * part + 3) * D], D))
                gs.append(g)
            dve.wait(t)
            return lambda tl: gs[1][:] if tl < CT else gs[0][:]

        def spans():
            return [(0, NSPAN), (NSPAN, ALLT)]

        def project_T(dst, w, kt, rhs, banks, m, evac=None):
            toks = []
            for (a, z), b in zip(spans(), banks):
                pe.take(B[b])
                renew(B[b])
                t = mm_acc(PS[0:m, b, 0:z - a], [(w(k), rhs[:, k, a:z]) for k in range(kt)])
                t = act(S.copy, dst[:, a:z], PS[0:m, b, 0:z - a], after=[t])
                B[b].got(t)
                toks.append(t)
            return toks

        def feature_norm(xs, sq, s_sq, summer, width, gains, banks, n=P):
            toks = []
            for (a, z), b in zip(spans(), banks):
                pe.take(B[b])
                renew(B[b])
                for j, x in enumerate(xs):
                    act.take(s_sq)
                    renew(s_sq)
                    t = act(S.activation, sq[0:n, 0:z - a], x[:, a:z], ACT.Square)
                    t = pe(T.matmul, PS[0:n, b, 0:z - a], summer[0:n, 0:n], sq[0:n, 0:z - a], start=(j == 0),
                           stop=(j == len(xs) - 1), after=[t])
                    s_sq.got(t)
                act.take(s_sq)
                renew(s_sq)
                t = rstd_of(PS[0:n, b, 0:z - a], width, n, [t], sq[0:n, 0:z - a])
                B[b].got(t)
                for j, x in enumerate(xs):
                    t2 = dve(V.scalar_tensor_tensor, x[:, a:z], x[:, a:z], gains[j], sq[0:n, 0:z - a],
                             ALU.mult, ALU.mult, after=[t])
                    toks.append(t2)
                s_sq.got(t2)
            return toks

        def rope(x, r0, r1, cos, sin, rot_m, tmp, s_tmp, banks, after, k0=0):
            toks = []
            for n, ((a, z), b) in enumerate(zip(spans(), banks)):
                pe.take(B[b])
                renew(B[b])
                t = pe(T.matmul, PS[k0:r1, b, 0:z - a], rot_m[k0:r1, k0:r1], x[k0:r1, a:z], start=True, stop=True,
                       after=after)
                dve.take(s_tmp)
                renew(s_tmp)
                t1 = dve(V.tensor_tensor, tmp[r0:r1, 0:z - a], PS[r0:r1, b, 0:z - a], sin[r0:r1, a:z], ALU.mult, after=[t])
                B[b].got(t1)
                t2 = dve(V.tensor_tensor, x[r0:r1, a:z], x[r0:r1, a:z], cos[r0:r1, a:z], ALU.mult, after=[t])
                t = dve(V.tensor_tensor, x[r0:r1, a:z], x[r0:r1, a:z], tmp[r0:r1, 0:z - a], ALU.add, after=[t1, t2])
                s_tmp.got(t)
                toks.append(t)
            return toks

        def lat_and_ctx_units(qT, kk, v, scale, out, with_ctx=True, dq=P):
            units = []
            for n in range(0 if with_ctx else CT, NT):
                nk = CTX if n < CT else ALLT

                def scores(o, n=n, nk=nk):
                    a = pe(T.matmul, o[:, 0:min(nk, 512)], qT[:, n * P:(n + 1) * P], kk[:, 0:min(nk, 512)],
                           start=True, stop=True, sig=nk <= 512)
                    if nk > 512:
                        a = pe(T.matmul, o[:, 512:nk], qT[:, n * P:(n + 1) * P], kk[:, 512:nk], start=True, stop=True)
                    return a
                units.append(dict(n=nk, scale=scale, scores=scores, v=v, out=out(n)))
            return units

        modulated_T(0, 0, A["norm_mix_2"][0], range(NT))
        w_ab = A["ab_w_in_2"][0]
        with ExitStack() as st:
            cq = [sb(st, f"cq{j}", [P, ALLT]) for j in range(3)]
            ckv = [sb(st, f"ckv{j}", [P, ALLT]) for j in range(2)]
            kr = sb(st, "kr", [96, ALLT])
            va = sb(st, "va", [P, NT, 512])
            vb = sb(st, "vb", [P, NT, P])
            kz = sb(st, "kz", [P, 2, 2, ALLT])
            mcos, msin = sb(st, "mcos", [96, ALLT]), sb(st, "msin", [96, ALLT])
            gcos, gsin = sb(st, "gcos", [P, ALLT]), sb(st, "gsin", [P, ALLT])
            pair, hsum = sb(st, "pair", [P, P]), sb(st, "hsum", [P, P])
            gains = sb(st, "gains", [P, 8])
            sq = sb(st, "sq", [P, NSPAN])
            s_sq = Slot(p, "sq")
            tmp_ = sb(st, "rtmp", [P, NSPAN])
            s_tmp_ = Slot(p, "rtmp")
            dve(V.memset, kz[:], 0.0)
            with ExitStack() as sw:
                wx = sb(sw, "wx", [P, KT, 928])
                wv = sb(sw, "wv", [P, 2, 512])
                kb = sb(sw, "kb", [P, ALLT])
                sp.dma(d_w[0], wx[:, :, 0:672], w_cols(w_ab, 0, 672))
                sp.dma(d_w[0], wx[:, :, 672:928], w_cols(w_ab, 1184, 256))
                for j in range(2):
                    sp.dma(d_w[0], wv[:, j, :].rearrange("p (h c) -> p h c", h=8),
                           A["mla_w_kv_up_2"][0][j * P:(j + 1) * P, :].rearrange("p (h c) -> p h c", h=8)[:, :, 64:128])
                for dst, name in ((mcos, "mla_cos"), (msin, "mla_sin"), (gcos, "gqa_cos"), (gsin, "gqa_sin"),
                                  (pair, "pair_rot"), (hsum, "head_sum")):
                    sp.dma(d_w[0], dst[:], A["c_" + name])
                with nc.allow_non_contiguous_dma("norm weights as columns"):
                    sp.dma(d_w[0], gains[:, 0:3], A["mla_q_norm_2"][0].rearrange("(t p) -> p t", p=P))
                    sp.dma(d_w[0], gains[:, 3:5], A["mla_kv_norm_2"][0].rearrange("(t p) -> p t", p=P))
                    for half in range(2):
                        r = slice(64 * half, 64 * half + 64)
                        sp.dma(d_w[0], gains[r, 5:6], A["gqa_q_norm_2"][0].rearrange("(p a) -> p a", a=1))
                        t = sp.dma(d_w[0], gains[r, 6:7], A["gqa_k_norm_2"][0].rearrange("(p a) -> p a", a=1))
                for e in (pe, act, dve):
                    e.wait(t)
                tq, tkv = [], []
                for j in range(3):
                    tq += project_T(cq[j][:], lambda k, j=j: wx[:, k, j * P:(j + 1) * P], KT, hT, (0, 1), P)
                for j in range(2):
                    tkv += project_T(ckv[j][:], lambda k, j=j: wx[:, k, 384 + j * P:384 + (j + 1) * P], KT, hT, (2, 3), P)
                act.wait(*tq, *tkv)
                feature_norm([c[:] for c in cq], sq, s_sq, ones, 384, [gains[:, j:j + 1] for j in range(3)], (4, 5))
                tkv = feature_norm([c[:] for c in ckv], sq, s_sq, ones, 256, [gains[:, 3 + j:4 + j] for j in range(2)], (6, 7))
                tr = []
                for (a, z), b in zip(spans(), (0, 1)):
                    pe.take(B[b])
                    renew(B[b])
                    t = mm_acc(PS[64:96, b, 0:z - a], [(wx[:, k, 640:672], hT[:, k, a:z]) for k in range(KT)])
                    t = act(S.copy, kr[64:96, a:z], PS[64:96, b, 0:z - a], after=[t])
                    B[b].got(t)
                    tr.append(t)
                rope(kr, 64, 96, mcos, msin, pair, tmp_, s_tmp_, (2, 3), tr, k0=64)
                tk = project_T(kb[:], lambda k: wx[:, k, 672:800], KT, hT, (0, 1), P)
                act.wait(*tk)
                tk = feature_norm([kb[:]], sq, s_sq, hsum, 64, [gains[:, 6:7]], (4, 5))
                tk = rope(kb, 0, P, gcos, gsin, pair, tmp_, s_tmp_, (2, 3), tk)
                for kv in range(2):
                    r = slice(64 * kv, 64 * kv + 64)
                    dve(V.tensor_copy, kz[r, kv, kv, :], kb[r, :], after=tk)
                for kv in range(2):
                    o = 64 * (1 - kv)
                    sp.dma(d_g, kz[o:o + 64, kv, 1 - kv, :], kb[64 * kv:64 * kv + 64, :], after=tk)
                pe.wait(*tkv)
                for n in range(NT):
                    b = 4 + n % 4
                    pe.take(B[b])
                    renew(B[b])
                    t = mm_acc(PS[:, b, :], [(ckv[k][:, n * P:(n + 1) * P], wv[:, k, :]) for k in range(2)])
                    t = act(S.copy, va[:, n, :], PS[:, b, :], after=[t])
                    B[b].got(t)
                for n in range(NT):
                    b = n % 4
                    pe.take(B[b])
                    renew(B[b])
                    t = mm_acc(PS[:, b, 0:P], [(hT[:, k, n * P:(n + 1) * P], wx[:, k, 800:928]) for k in range(KT)])
                    t = act(S.copy, vb[:, n, :], PS[:, b, 0:P], after=[t])
                    B[b].got(t)
                p.barrier()
            bufs = softmax_bufs(st, ALLT)
            with ExitStack() as sh:
                wqu = [sb(sh, f"wqu{n}", [P, 3, 96]) for n in range(2)]
                wku = [sb(sh, f"wku{n}", [P, 2, 64]) for n in range(2)]
                s_wu = [Slot(p, f"wqku{n}") for n in range(2)]
                qT = [sb(sh, f"aqT{n}", [96, ALLT]) for n in range(2)]
                kT = [sb(sh, f"akT{n}", [96, ALLT]) for n in range(2)]
                s_qT, s_kT = [Slot(p, f"aqT{n}") for n in range(2)], [Slot(p, f"akT{n}") for n in range(2)]
                with p.repeat("mla", 4) as i:
                    for n in range(2):
                        sp.take(s_wu[n])
                        renew(s_wu[n])
                        sp.dma(d_w[n], wqu[n][:], A["mla_w_q_up_2"][0].rearrange("(t p) m -> p t m", p=P)
                               [:, :, bass.ds(i * 192 + 96 * n, 96)])
                        s_wu[n].put(sp.dma(d_w[n], wku[n][:], A["mla_w_kv_up_2"][0].rearrange("(t p) m -> p t m", p=P)
                                           [:, :, bass.ds(i * 256 + P * n, 64)]))
                    units = []
                    for n in range(2):
                        pe.need(s_wu[n])
                        act.take(s_qT[n], s_kT[n])
                        dve.take(s_kT[n])
                        renew(s_qT[n], s_kT[n])
                        for j, (a, z) in enumerate(spans()):
                            b = 2 * j
                            pe.take(B[b], B[b + 1])
                            renew(B[b], B[b + 1])
                            t = mm_acc(PS[0:96, b, 0:NSPAN], [(wqu[n][:, k, :], cq[k][:, a:z]) for k in range(3)])
                            t = act(S.copy, qT[n][:, a:z], PS[0:96, b, 0:NSPAN], after=[t])
                            B[b].got(t)
                            s_qT[n].put(t)
                            t = mm_acc(PS[0:64, b + 1, 0:NSPAN], [(wku[n][:, k, :], ckv[k][:, a:z]) for k in range(2)])
                            s_wu[n].got(t)
                            t = act(S.copy, kT[n][0:64, a:z], PS[0:64, b + 1, 0:NSPAN], after=[t])
                            B[b + 1].got(t)
                            s_kT[n].put(t)
                        s_kT[n].put(dve(V.tensor_copy, kT[n][64:96, :], kr[64:96, :]))
                        s_qT[n].put(*rope(qT[n], 64, 96, mcos, msin, pair, tmp_, s_tmp_, (0, 2), s_qT[n].fill))
                    for n in range(2):
                        units += lat_and_ctx_units(
                            qT[n], kT[n], lambda j, n=n: va[:, j, bass.ds(i * P + 64 * n, 64)], 96 ** -0.5,
                            lambda tl, n=n: OT[:, tl, bass.ds(i * P + 64 * n, 64)])
                    pe.need(*s_qT, *s_kT)
                    attend(units, bufs, [[0, 1], [2, 3]], [4, 5], 6, 64)
                    for s in (*s_qT, *s_kT):
                        s.got(*B[6].fill)
            with ExitStack() as sh:
                wg = sb(sh, "wgq", [P, KT, P])
                s_wg = Slot(p, "wgq")
                qT = sb(sh, "gqT", [P, ALLT])
                kc = sb(sh, "kcur", [P, 2, ALLT])
                s_qT, s_kc = Slot(p, "gqT"), Slot(p, "kcur")
                with p.repeat("gqa", 4) as i:
                    sp.take(s_wg)
                    renew(s_wg)
                    s_wg.put(sp.dma(d_w[0], wg[:], w_cols(w_ab, i * P + 672, P)))
                    pe.need(s_wg)
                    act.take(s_qT)
                    dve.take(s_qT, s_kc)
                    renew(s_qT, s_kc)
                    s_kc.put(dve(V.tensor_copy, kc[:], kz[:].rearrange("p a b c -> p a (b c)")
                                 [:, bass.ds(i // 2, 1), :].rearrange("p a (b c) -> p (a b) c", b=2)))
                    t = project_T(qT[:], lambda k: wg[:, k, :], KT, hT, (0, 2), P)
                    s_wg.got(*t)
                    act.wait(*t)
                    t = feature_norm([qT[:]], sq, s_sq, hsum, 64, [gains[:, 5:6]], (0, 2))
                    t = rope(qT, 0, P, gcos, gsin, pair, tmp_, s_tmp_, (0, 2), t)
                    s_qT.put(*t)
                    pe.need(s_qT, s_kc)
                    units = []
                    for hh in range(2):
                        units += lat_and_ctx_units(
                            qT, kc[:, hh, :], lambda j: vb[:, j, bass.ds((i // 2) * 64, 64)], 64 ** -0.5,
                            lambda tl, hh=hh: OT[:, tl, bass.ds(i * P + (512 + 64 * hh), 64)])
                    attend(units, bufs, [[0, 1], [2, 3]], [4, 5], 6, 64)
                    for s in (s_qT, s_kc):
                        s.got(*B[6].fill)
        with ExitStack() as st:
            rg = row_gates(st, 0, 0, True)
            gate_and_project(st, A["ab_w_out_2"][0], None, list(range(NT)), rg)

        def moe(layer, tiles):
            n_t = len(tiles)
            modulated_T(layer, 1, A["norm_ffn_2"][layer], tiles, to_dram=h_dram)
            with ExitStack() as st:
                idx = sb(st, "idx", [P, NBLK], U32)
                rows = sb(st, "rows", [P, 2, NT], U32)
                wts = sb(st, "wts", [P, 2, NT])
                n_ov = sb(st, "n_ov", [P, 1], U32)
                ov_e = sb(st, "ov_e", [P, 16], U32)
                route(st, layer, n_t, idx, rows, wts, n_ov, ov_e)
                with ExitStack() as se:
                    experts(se, layer, idx, n_ov, ov_e)
                g2 = row_gates(st, layer, 1, CT > 0 and 0 in tiles)
                yr = [[sb(st, f"yr{a}{b}", [P, D]) for b in range(2)] for a in range(2)]
                s_yr = [Slot(p, f"yr{a}") for a in range(2)]
                for j, tl in enumerate(tiles):
                    y, s = yr[j % 2], s_yr[j % 2]
                    pool.take(s)
                    renew(s)
                    for b in range(2):
                        t = d_yg[j % 2].counted(G.indirect_dma_start(
                            y[b][:], None, y_dram, bass.IndirectOffsetOnAxis(ap=rows[:, b, j:j + 1], axis=0)))
                    s.put(t)
                    t = dve(V.tensor_scalar, y[0][:], y[0][:], wts[:, 0, j:j + 1], None, ALU.mult, after=[t])
                    t = dve(V.scalar_tensor_tensor, y[0][:], y[1][:], wts[:, 1, j:j + 1], y[0][:], ALU.mult,
                            ALU.add, after=[t])
                    t = dve(V.tensor_tensor, y[0][:], y[0][:], g2(tl), ALU.mult, after=[t])
                    t = dve(V.tensor_tensor, X[:, tl, :], X[:, tl, :], y[0][:], ALU.add, after=[t])
                    s.got(t)
                p.barrier()

        def route(st, layer, n_t, idx, rows, wts, n_ov, ov_e):
            with ExitStack() as s:
                wr = sb(s, "wr", [P, KT, 36])
                br = sb(s, "br", [P, 36])
                L = sb(s, "L", [P, NT, 36])
                io = sb(s, "io", [P, 32])
                tri = sb(s, "tri", [P, P])
                ids = sb(s, "ids", [P, NT], U32)
                with nc.allow_non_contiguous_dma("router weights"):
                    sp.dma(d_bc, wr[:, :, 0:4], A["moe_w_rg_2"][layer].rearrange("(t p) m -> p t m", p=P))
                    sp.dma(d_bc, wr[:, :, 4:36], A["moe_w_re_2"][layer].rearrange("(t p) m -> p t m", p=P))
                sp.dma(d_bc, br[:, 0:4], bcast(A["moe_b_rg_2"][layer], 4))
                sp.dma(d_bc, br[:, 4:36], bcast(A["moe_b_re_2"][layer], 32))
                sp.dma(d_bc, io[:], A["c_iota32"])
                sp.dma(d_bc, tri[:], A["c_before"])
                sp.dma(d_bc, ids[:], A["c_token_ids"])
                t = sp.dma(d_bc, table[layer].rearrange("(p b) a -> p (b a)", p=P), A["c_zero_table"])
                for e in (pe, dve, pool):
                    e.wait(t)
                for n in range(n_t):
                    t = mm_acc(PS[:, 0, n * 36:(n + 1) * 36], [(hT[:, k, n * P:(n + 1) * P], wr[:, k, :]) for k in range(KT)])
                d = lambda *a, **k: dve(*a, after=[last_dve()], **k)

                def last_dve():
                    return Token(dve.ctr, None, 0, dve.ctr.count)

                def bc(ap, shape):
                    return ap[:].to_broadcast(shape)

                def tile(name, w, dt=F32):
                    return sb(s, "r_" + name, [P, n_t, w], dt)

                dve.wait(t)
                d(V.tensor_tensor, L[:, 0:n_t, :], PS[:, 0, 0:36 * n_t].rearrange("p (n m) -> p n m", m=36),
                  bc(br[:].unsqueeze(1), [P, n_t, 36]), ALU.add)
                lg, le = L[:, 0:n_t, 0:4], L[:, 0:n_t, 4:36]

                def first_max(src, w, mx, oh, cand):
                    d(V.tensor_reduce, mx[:, :, 0], src, AX, ALU.max)
                    d(V.tensor_tensor, cand, src, bc(mx, [P, n_t, w]), ALU.is_equal)
                    d(V.tensor_scalar, cand, cand, -1000.0, None, ALU.mult)
                    d(V.tensor_tensor, cand, cand, bc(io[:, 0:w].unsqueeze(1), [P, n_t, w]), ALU.add)
                    d(V.tensor_reduce, red[:, :, 0], cand, AX, ALU.min)
                    d(V.tensor_tensor, oh, cand, bc(red, [P, n_t, w]), ALU.is_equal)

                red, m0, m1, m2 = tile("red", 1), tile("m0", 1), tile("m1", 1), tile("m2", 1)
                oh4, c4, c32 = tile("oh4", 4), tile("c4", 4), tile("c32", 32)
                O = [tile("o1", 32), tile("o2", 32)]
                first_max(lg, 4, m0, oh4[:], c4[:])
                d(V.tensor_tensor, c4[:], lg, bc(m0, [P, n_t, 4]), ALU.subtract)
                t = act(S.activation, c4[:], c4[:], ACT.Exp, after=[last_dve()])
                dve.wait(t)
                pg = tile("pg", 1)
                d(V.tensor_reduce, pg[:, :, 0], c4[:], AX, ALU.add)
                d(V.reciprocal, pg[:], pg[:])
                d(V.tensor_scalar, oh4[:], oh4[:], -NEG, NEG, ALU.mult, ALU.add)
                for n in range(n_t):
                    d(V.tensor_tensor, L[:, n, 4:36].rearrange("p (g e) -> p g e", g=4),
                      L[:, n, 4:36].rearrange("p (g e) -> p g e", g=4),
                      bc(oh4[:, n, :].unsqueeze(2), [P, 4, 8]), ALU.add)
                first_max(le, 32, m1, O[0][:], c32[:])
                d(V.scalar_tensor_tensor, le, O[0][:], 3 * NEG, le, ALU.mult, ALU.add)
                first_max(le, 32, m2, O[1][:], c32[:])
                e2 = tile("e2", 1)
                d(V.tensor_tensor, e2[:], m2[:], m1[:], ALU.subtract)
                t = act(S.activation, e2[:], e2[:], ACT.Exp, after=[last_dve()])
                dve.wait(t)
                d(V.tensor_scalar, m0[:], e2[:], 1.0, None, ALU.add)
                d(V.reciprocal, m0[:], m0[:])
                d(V.tensor_tensor, wts[:, 0, 0:n_t], m0[:, :, 0], pg[:, :, 0], ALU.mult)
                d(V.tensor_tensor, wts[:, 1, 0:n_t], wts[:, 0, 0:n_t], e2[:, :, 0], ALU.mult)
                C = tile("C", 32)
                t = d(V.tensor_tensor, C[:], O[0][:], O[1][:], ALU.add)
                pe.wait(t)
                for n in range(n_t):
                    mm_acc(PS[:, 1, n * 32:(n + 1) * 32],
                           [(tri[:], C[:, n, :])] + [(ones[:], C[:, m, :]) for m in range(n)], sig=False)
                t = mm_acc(PS[:, 2, 0:32], [(ones[:], C[:, m, :]) for m in range(n_t)])
                dve.wait(t)
                R = tile("R", 32)
                d(V.tensor_copy, R[:], PS[:, 1, 0:32 * n_t].rearrange("p (n m) -> p n m", m=32))
                cnt, nov, oend, ost = (sb(s, f"r_{n}", [P, 32]) for n in ("cnt", "nov", "oend", "ost"))
                d(V.tensor_copy, cnt[:], PS[:, 2, 0:32])
                d(V.tensor_scalar, nov[:], cnt[:], float(P), None, ALU.is_gt)
                for j in range(2, MAXJ + 1):
                    d(V.scalar_tensor_tensor, nov[:], cnt[:], float(P * j), nov[:], ALU.is_gt, ALU.add)
                d(V.tensor_tensor_scan, oend[:], ones[:, 0:32], nov[:], 0.0, ALU.mult, ALU.add)
                d(V.tensor_tensor, ost[:], oend[:], nov[:], ALU.subtract)
                d(V.tensor_copy, n_ov[:], oend[:, 31:32])
                oe = sb(s, "r_oe", [P, 16])
                for b in range(NBLK - NEXP):
                    d(V.tensor_scalar, cnt[:], oend[:], float(b), None, ALU.is_le)
                    d(V.tensor_reduce, oe[:, b:b + 1], cnt[:], AX, ALU.add)
                d(V.tensor_scalar, oe[:, 0:NBLK - NEXP], oe[:, 0:NBLK - NEXP], float(NEXP - 1), None, ALU.min)
                d(V.tensor_copy, ov_e[:, 0:NBLK - NEXP], oe[:, 0:NBLK - NEXP])
                rk, ee, oo, jj, bb, pos = (tile(x, 1) for x in ("rk", "ee", "oo", "jj", "bb", "pos"))
                posu = [tile("pu0", 1, U32), tile("pu1", 1, U32)]
                for c in range(2):
                    for dst, src in ((rk, R[:]), (ee, bc(io[:].unsqueeze(1), [P, n_t, 32])),
                                     (oo, bc(ost[:].unsqueeze(1), [P, n_t, 32]))):
                        d(V.tensor_tensor, c32[:], O[c][:], src, ALU.mult)
                        d(V.tensor_reduce, dst[:, :, 0], c32[:], AX, ALU.add)
                    d(V.tensor_scalar, jj[:], rk[:], float(P), None, ALU.is_ge)
                    for j in range(2, MAXJ + 1):
                        d(V.scalar_tensor_tensor, jj[:], rk[:], float(P * j), jj[:], ALU.is_ge, ALU.add)
                    d(V.tensor_tensor, bb[:], oo[:], jj[:], ALU.add)
                    d(V.tensor_tensor, bb[:], bb[:], ee[:], ALU.subtract)
                    d(V.tensor_scalar, bb[:], bb[:], float(NEXP - 1), None, ALU.add)
                    d(V.tensor_scalar, pos[:], jj[:], 0.0, None, ALU.is_gt)
                    d(V.tensor_tensor, bb[:], bb[:], pos[:], ALU.mult)
                    d(V.tensor_tensor, bb[:], bb[:], ee[:], ALU.add)
                    d(V.scalar_tensor_tensor, rk[:], jj[:], -float(P), rk[:], ALU.mult, ALU.add)
                    d(V.scalar_tensor_tensor, pos[:], bb[:], float(P), rk[:], ALU.mult, ALU.add)
                    d(V.tensor_copy, rows[:, c, 0:n_t], pos[:, :, 0])
                    d(V.scalar_tensor_tensor, pos[:], rk[:], float(NBLK), bb[:], ALU.mult, ALU.add)
                    t = d(V.tensor_copy, posu[c][:], pos[:])
                pool.wait(t)
                for c in range(2):
                    for n in range(n_t):
                        t = d_idx.counted(G.indirect_dma_start(
                            table[layer], bass.IndirectOffsetOnAxis(ap=posu[c][:, n, :], axis=0),
                            ids[:, n:n + 1], None))
                sp.dma(d_bc, idx[:], table[layer].rearrange("(p b) a -> p (b a)", p=P), after=[t])
                p.barrier()

        def experts(st, layer, idx, n_ov, ov_e):
            wg, wu_, wd = (A[f"moe_w_{n}_2"][layer] for n in ("gate", "up", "down"))
            Wg = [sb(st, f"Wg{n}", [P, KT, DEXP]) for n in range(2)]
            Wu = [sb(st, f"Wu{n}", [P, KT, DEXP]) for n in range(2)]
            Wd = [sb(st, f"Wd{n}", [P, DEXP // P, D]) for n in range(2)]
            s_W = [Slot(p, f"W{n}") for n in range(2)]
            ic = [sb(st, f"ic{n}", [P, 1], U32) for n in range(2)]
            xe = [sb(st, f"xe{n}", [P, D]) for n in range(2)]
            s_ic, s_xe = [Slot(p, f"ic{n}") for n in range(2)], [Slot(p, f"xe{n}") for n in range(2)]
            xT = sb(st, "xT", [P, KT, P])
            s_xT = Slot(p, "xT")
            sg, aT = sb(st, "esg", [P, DEXP]), sb(st, "eaT", [P, DEXP])
            s_sg, s_aT = Slot(p, "esg"), Slot(p, "eaT")

            def load(n, e):
                sp.take(s_W[n])
                renew(s_W[n])
                sp.dma(d_w[n], Wg[n][:], wg[bass.ds(e, 1)].rearrange("a (p t) m -> p (a t) m", p=P))
                sp.dma(d_w[n], Wu[n][:], wu_[bass.ds(e, 1)].rearrange("a (p t) m -> p (a t) m", p=P))
                s_W[n].put(sp.dma(d_w[n], Wd[n][:], wd[bass.ds(e, 1)].rearrange("a (t p) m -> p (a t) m", p=P)))

            def fetch(n, block, stream):
                dve.take(s_ic[n])
                renew(s_ic[n])
                t = dve(V.tensor_copy, ic[n][:], idx[:, bass.ds(block, 1)])
                s_ic[n].put(t)
                pool.take(s_xe[n])
                renew(s_xe[n])
                pool.wait(t)
                t = stream.counted(G.indirect_dma_start(
                    xe[n][:], None, h_dram, bass.IndirectOffsetOnAxis(ap=ic[n][:, 0:1], axis=0)))
                s_xe[n].put(t)

            def ffn(n, block):
                pe.need(s_xe[n])
                act.take(s_xT)
                dve.take(s_xT)
                renew(s_xT)
                x3 = xe[n][:].rearrange("s (p t) -> s p t", t=KT)
                for g0 in range(0, KT, 4):
                    b = g0 // 4
                    pe.take(B[b])
                    renew(B[b])
                    for j in range(4):
                        t = pe(T.transpose, PS[:, b, j * P:(j + 1) * P], x3[:, :, g0 + j], ident[:], sig=(j == 3))
                    s_xe[n].got(t)
                    s_ic[n].got(t)
                    ev, cp = (act, S.copy) if b else (dve, V.tensor_copy)
                    t = ev(cp, xT[:, g0:g0 + 4, :], PS[:, b, :].rearrange("p (j c) -> p j c", j=4), after=[t])
                    B[b].got(t)
                    s_xT.put(t)
                pe.need(s_xT, s_W[n])
                pe.take(B[2], B[3])
                renew(B[2], B[3])
                tg = mm_acc(PS[:, 2, :], [(xT[:, k, :], Wg[n][:, k, :]) for k in range(KT)])
                tu = mm_acc(PS[:, 3, :], [(xT[:, k, :], Wu[n][:, k, :]) for k in range(KT)])
                s_xT.got(tu)
                act.take(s_sg)
                renew(s_sg)
                t = act(S.activation, sg[:], PS[:, 2, :], ACT.Exp, scale=-1.0, after=[tg])
                t = dve(V.tensor_scalar, sg[:], sg[:], 1.0, None, ALU.add, after=[t])
                t = dve(V.reciprocal, sg[:], sg[:], after=[t])
                t = dve(V.tensor_tensor, sg[:], sg[:], PS[:, 2, :], ALU.mult, after=[t])
                B[2].got(t)
                t = dve(V.tensor_tensor, sg[:], sg[:], PS[:, 3, :], ALU.mult, after=[t, tu])
                B[3].got(t)
                pe.take(B[4])
                renew(B[4])
                pe.wait(t)
                for j in range(4):
                    t = pe(T.transpose, PS[:, 4, j * P:(j + 1) * P], sg[:, j * P:(j + 1) * P], ident[:], sig=(j == 3))
                s_sg.got(t)
                act.take(s_aT)
                renew(s_aT)
                t = act(S.copy, aT[:], PS[:, 4, :], after=[t])
                B[4].got(t)
                s_aT.put(t)
                pe.wait(t)
                pe.take(B[5], B[6])
                renew(B[5], B[6])
                for c in range(2):
                    t = mm_acc(PS[:, 5 + c, :], [(aT[:, j * P:(j + 1) * P], Wd[n][:, j, c * 512:c * 512 + 512]) for j in range(4)])
                    B[5 + c].put(t)
                    ev, cp = (act, S.copy) if c else (dve, V.tensor_copy)
                    ev.wait(*s_xe[n].free)
                    a = ev(cp, xe[n][:, c * 512:c * 512 + 512], PS[:, 5 + c, :], after=[t])
                    B[5 + c].got(a)
                    sp.wait(a)
                s_aT.got(t)
                s_W[n].got(t)
                s_xe[n].got(sp.dma(d_y[n], y_dram[bass.ds(block * P, P), :], xe[n][:]))

            with p.repeat(f"experts{layer}", NEXP // 2) as i:
                for n in range(2):
                    load(n, i * 2 + n)
                    fetch(n, i * 2 + n, d_x[n])
                for n in range(2):
                    ffn(n, i * 2 + n)
            for e in p.engines:
                e.wait(*p.everything())
            count = nc.values_load(n_ov[0:1, 0:1], min_val=0, max_val=NBLK - NEXP)
            with p.repeat(f"overflow{layer}", NBLK - NEXP) as i:
                with p.only_if(count > i):
                    e = nc.values_load(ov_e[0:1, bass.ds(i, 1)], engines=(mybir.EngineType.SP,),
                                       min_val=0, max_val=NEXP - 1)
                    load(0, e)
                    fetch(0, i + NEXP, d_xo[layer])
                    ffn(0, i + NEXP)

        moe(0, list(range(NT)))

        modulated_T(1, 0, A["norm_mix_2"][1], range(NT))
        w_na = A["na_w_in_2"][0]
        with ExitStack() as st:
            NH, NR = 16, 15
            bias_t = sb(st, "bias", [P, NH, NR, 64])
            with ExitStack() as s:
                pick = sb(s, "pick", [64, 64 * P])
                rp = sb(s, "rp", [P, 2, 32])
                rT = sb(s, "rT", [64, NH * NR])
                sp.dma(d_bc, pick[:], A["c_na_pick"])
                half = NH * NR // 2
                t = dve(V.memset, rp[:], NEG)
                sp.wait(t)
                flat = A["na_rpb_2"][0].rearrange("h r c -> (h r) c")
                for j in range(2):
                    t = sp.dma(d_bc, rp[0:half, j, 0:31], flat[j * half:(j + 1) * half, :])
                pe.wait(t)
                for j in range(2):
                    t = pe(T.transpose, PS[0:32, 0, j * half:(j + 1) * half], rp[0:half, j, :], ident[0:half, 0:half])
                t = act(S.copy, rT[0:32, :], PS[0:32, 0, 0:2 * half], after=[t])
                t0 = dve(V.memset, rT[32:64, :], 0.0)
                r3 = rT[:].rearrange("x (h r) -> x h r", h=NH)
                t = sp.dma(d_bc, r3[32:64, :, 1:NR], r3[0:32, :, 0:NR - 1], after=[t, t0])
                pe.wait(t)
                s_b = Slot(p, "bias_fill")
                for kc in range(64):
                    b = kc % 8
                    if kc:
                        pe.take(B[b])
                    renew(B[b])
                    t = mm_acc(PS[:, b, 0:NH * NR], [(pick[:, kc * P:(kc + 1) * P], rT[:])])
                    ev, cp = (dve, V.tensor_copy) if kc % 2 else (act, S.copy)
                    t = ev(cp, bias_t[:, :, :, kc], PS[:, b, 0:NH * NR].rearrange("p (h r) -> p h r", h=NH), after=[t])
                    B[b].got(t)
                p.barrier()
            ws = [sb(st, f"ws{n}", [P, KT, 3, P]) for n in range(2)]
            s_ws = [Slot(p, f"ws{n}") for n in range(2)]
            qT = sb(st, "nqT", [P, ALLT])
            kz = sb(st, "nkz", [P, 2, ALLT])
            vv = sb(st, "nv", [P, NT, P])
            s_q, s_k, s_v = Slot(p, "nq"), Slot(p, "nk"), Slot(p, "nv")
            bufs = softmax_bufs(st, ALLT)
            dve(V.memset, kz[:], 0.0)
            with p.repeat("neighbours", NH // 4) as i:
                for w in range(2):
                    sp.take(s_ws[w])
                    renew(s_ws[w])
                    for j in range(3):
                        t = sp.dma(d_w[w], ws[w][:, :, j, :], w_cols(w_na, i * (2 * P) + (w * P + j * D), P))
                    s_ws[w].put(t)
                for w in range(2):
                    pe.need(s_ws[w])
                    pe.take(B[0])
                    renew(B[0])
                    t = mm_acc(PS[:, 0, :], [(ws[w][:, k, 0, :], hT[:, k, CTX:ALLT]) for k in range(KT)])
                    act.take(s_q)
                    renew(s_q)
                    t = act(S.copy, qT[:, CTX:ALLT], PS[:, 0, :], after=[t])
                    B[0].got(t)
                    s_q.put(t)
                    act.take(s_k)
                    dve.take(s_k)
                    renew(s_k)
                    for (a, z), b in zip(spans(), (1, 2)):
                        pe.take(B[b])
                        renew(B[b])
                        t = mm_acc(PS[:, b, 0:z - a], [(ws[w][:, k, 1, :], hT[:, k, a:z]) for k in range(KT)])
                        t1 = dve(V.tensor_copy, kz[0:64, 0, a:z], PS[0:64, b, 0:z - a], after=[t])
                        t2 = act(S.copy, kz[64:P, 1, a:z], PS[64:P, b, 0:z - a], after=[t])
                        B[b].got(t1, t2)
                        s_k.put(t1, t2)
                    act.take(s_v)
                    renew(s_v)
                    for g0 in range(0, NT, 3):
                        b = 3 if g0 else 7
                        pe.take(B[b])
                        renew(B[b])
                        for n in range(3):
                            tn = g0 + n
                            t = mm_acc(PS[:, b, n * P:(n + 1) * P],
                                       [(hT[:, k, tn * P:(tn + 1) * P], ws[w][:, k, 2, :]) for k in range(KT)])
                        s_ws[w].got(t)
                        t = act(S.copy, vv[:, g0:g0 + 3, :].rearrange("p a b -> p (a b)"), PS[:, b, 0:3 * P], after=[t])
                        B[b].got(t)
                        s_v.put(t)
                    pe.need(s_q, s_k, s_v)
                    units = []
                    for hh in range(2):
                        for n in range(LT):
                            def scores(o, n=n, hh=hh):
                                q = qT[:, CTX + n * P:CTX + (n + 1) * P]
                                pe(T.matmul, o[:, 0:SEQ], q, kz[:, hh, CTX:ALLT], start=True, stop=True, sig=False)
                                return pe(T.matmul, o[:, SEQ:ALLT], q, kz[:, hh, 0:CTX], start=True, stop=True)

                            def bias(src, dst, toks, n=n, hh=hh):
                                b4 = bias_t[:].rearrange("p h r c -> p h (r c)")[
                                    :, bass.ds(i * 4 + (2 * w + hh), 1), (7 - 2 * n) * 64:(15 - 2 * n) * 64]
                                a = dve(V.scalar_tensor_tensor, dst[:, 0:SEQ].unsqueeze(1), src[:, 0:SEQ].unsqueeze(1),
                                        64 ** -0.5, b4, ALU.mult, ALU.add, after=toks)
                                b = act(S.activation, dst[:, SEQ:ALLT], src[:, SEQ:ALLT], ACT.Copy, scale=64 ** -0.5,
                                        after=toks)
                                return [a, b]

                            units.append(dict(
                                n=ALLT, scale=1.0, scores=scores, bias=bias,
                                v=lambda j, hh=hh: vv[:, (j + CT) % NT, hh * 64:hh * 64 + 64],
                                out=OT[:, CT + n, bass.ds(i * (2 * P) + (w * P + hh * 64), 64)]))
                    attend(units, bufs, [[0, 1], [2, 3]], [4, 5], 6, 64)
                    for s in (s_q, s_k, s_v):
                        s.got(*B[6].fill)
        with ExitStack() as st:
            rg = row_gates(st, 1, 0, False)
            gate_and_project(st, A["na_w_out_2"][0], None, list(range(CT, NT)), rg)
        moe(1, list(range(CT, NT)))

        with ExitStack() as st:
            norm_rows(st, A["norm_final_2"], range(CT, NT), lambda tl: OT[:, tl, :])
            t = sp.dma(d_st, out[0].rearrange("(t p) d -> p t d", p=P), OT[:, CT:, :])
            sp.wait(t)
            sp.wait(*p.everything())
        return p.found


_NAMES = ["x", "mem", "mem_norm_w", "norm_w", "w_memkv", "w_out", "w_in_a", "w_gate_up", "b_gate", "gla_norm_w",
          "w_in_b", "final_norm_w", "c_2", "ctx_2", "c_ctx_2", "w_ada_2", "b_ada_2", "norm_mix_2", "norm_ffn_2",
          "norm_final_2", "ab_w_in_2", "ab_w_out_2", "mla_q_norm_2", "mla_w_q_up_2", "mla_kv_norm_2",
          "mla_w_kv_up_2", "gqa_q_norm_2", "gqa_k_norm_2", "na_w_in_2", "na_w_out_2", "na_rpb_2", "moe_w_rg_2",
          "moe_b_rg_2", "moe_w_re_2", "moe_b_re_2", "moe_w_gate_2", "moe_w_up_2", "moe_w_down_2"]


def kernel(**inputs):
    import concourse.bacc as _bacc
    from concourse.bass_utils import run_bass_kernel_spmd as _run

    arrays = {f"in_{n}": np.ascontiguousarray(inputs[n]) for n in _NAMES}
    arrays.update({f"in_c_{n}": a for n, a in shape_constants().items()})

    def assemble(plan):
        nc = _bacc.Bacc("TRN2", target_bir_lowering=False, num_devices=1)
        aps = {n[3:]: nc.dram_tensor(n, a.shape, mybir.dt.from_np(a.dtype), kind="ExternalInput").ap()
               for n, a in arrays.items()}
        out = nc.dram_tensor("out", (1, SEQ, D), F32, kind="ExternalOutput").ap()
        return nc, build(nc, aps, out, plan)

    _, plan = assemble(None)
    nc, _ = assemble(plan)
    r = _run(nc, [arrays], core_ids=[0])
    return r.results[0]["out"]
```

```python
from contextlib import ExitStack, contextmanager

import numpy as np
import concourse.bass as bass
from concourse import mybir

F32 = mybir.dt.float32
U32 = mybir.dt.uint32
ALU = mybir.AluOpType
ACT = mybir.ActivationFunctionType
AX = mybir.AxisListType.X

P = 128
D = 1024
KT = D // P
SEQ, CTX, NMEM = 512, 256, 256
LT, CT = SEQ // P, CTX // P
ALLT = SEQ + CTX
NT = LT + CT
EPS = 1e-6
NEG = -1.0e30
NEXP, DEXP = 32, 512
MAXJ = ALLT // P - 1
NBLK = NEXP + 2 * ALLT // P - 1
NSPAN = 384




class Token:
    def __init__(self, ctr, loop, shift, off):
        self.ctr, self.loop, self.shift, self.off = ctr, loop, shift, off

    def total(self):
        if self.loop is None:
            return self.off
        lp = self.loop
        return lp.base[self.ctr] + (lp.n - 1 + self.shift) * lp.rate.get(self.ctr.name, 0) + self.off


class Counter:
    def __init__(self, prog, name, unit, by_pool=False, prefix=False, ahead=False):
        self.prog, self.name, self.unit, self.by_pool, self.prefix = prog, name, unit, by_pool, prefix
        self.ahead = ahead
        self.sem = prog.ctx.enter_context(prog.nc.semaphore("s_" + name))
        self.count = 0
        self.local = 0
        prog.counters.append(self)

    def counted(self, ins):
        ins.then_inc(self.sem, self.unit)
        if self.prog.loop is None:
            self.count += 1
            return Token(self, None, 0, self.count)
        self.local += 1
        return Token(self, self.prog.loop, 0, self.local)


class Slot:

    def __init__(self, prog, name, ap=None):
        self.name, self.ap, self.fill, self.free = f"{name}.{len(prog.slots)}", ap, [], []
        prog.slots.append(self)

    def put(self, *toks):
        self.fill += toks

    def got(self, *toks):
        self.free += toks


class Loop:
    def __init__(self, name, n, i, base, rate):
        self.name, self.n, self.i, self.base, self.rate = name, n, i, base, rate


class Engine:
    def __init__(self, prog, name, eng, anchor=False):
        self.prog, self.name, self.eng = prog, name, eng
        self.ctr = Counter(prog, name, 1)
        self.seen = {}
        self.anchor = prog.ctx.enter_context(prog.nc.semaphore(f"s_{name}_anchor")) if anchor else None

    def wait(self, *toks):
        for t in toks:
            if t is None:
                continue
            lp = self.prog.loop
            if t.loop is not lp or lp is None:
                if lp is not None:
                    continue
                v = t.total()
                if self.seen.get(t.ctr, (0, 0))[1] >= v:
                    continue
                self.seen[t.ctr] = (0, v)
                self.eng.wait_ge(t.ctr.sem, v * t.ctr.unit)
                continue
            key = (t.shift, t.off)
            if self.seen.get(t.ctr, (-9, 0)) >= key:
                continue
            self.seen[t.ctr] = key
            r = lp.rate.get(t.ctr.name, 0)
            const = (lp.base[t.ctr] + t.shift * r + t.off) * t.ctr.unit
            assert self.prog.plan is None or const > 0, (t.ctr.name, const)
            self.eng.wait_ge(t.ctr.sem, lp.i * (r * t.ctr.unit) + const if r else max(const, 1))
            if self.anchor is not None:
                self.eng.sem_inc(self.anchor, 1)

    def take(self, *slots):
        for s in slots:
            self.wait(*(s.free or s.fill))

    def need(self, *slots):
        for s in slots:
            self.wait(*s.fill)

    def __call__(self, method, *args, after=(), sig=True, **kw):
        self.wait(*after)
        ins = method(*args, **kw)
        return self.ctr.counted(ins) if sig else None

    def dma(self, stream, out, in_, after=()):
        self.wait(*after)
        return stream.counted(self.eng.dma_start(out, in_))


def renew(*slots):
    for s in slots:
        s.fill, s.free = [], []


class Prog:
    def __init__(self, nc, ctx, plan):
        self.nc, self.ctx, self.plan, self.found = nc, ctx, plan, {}
        self.counters, self.slots, self.loop = [], [], None
        self.round_end = ctx.enter_context(nc.semaphore("s_round_end"))
        self.pe = Engine(self, "pe", nc.tensor)
        self.act = Engine(self, "act", nc.scalar)
        self.dve = Engine(self, "dve", nc.vector)
        self.pool = Engine(self, "pool", nc.gpsimd, anchor=True)
        self.sp = Engine(self, "sp", nc.sync, anchor=True)
        self.engines = [self.pe, self.act, self.dve, self.pool, self.sp]

    def everything(self, ahead=True):
        return [Token(c, None, 0, c.count) for c in self.counters
                if c.count and not c.prefix and (ahead or not c.ahead)]

    def barrier(self, ahead=False):
        for e in self.engines:
            e.wait(*self.everything(ahead))


    @contextmanager
    def repeat(self, name, n):
        plan = (self.plan or {}).get(name, {"rate": {}, "slots": {}})
        rate = plan["rate"]
        for c in self.counters:
            lack = rate.get(c.name, 0) - c.count
            if lack > 0 and not c.by_pool:
                self.nc.sync.sem_inc(c.sem, lack * c.unit)
                c.count += lack
        self.barrier()
        byname = {c.name: c for c in self.counters}
        with self.nc.Fori(0, n) as i:
            lp = self.loop = Loop(name, n, i, {c: c.count for c in self.counters}, rate)
            for c in self.counters:
                c.local = 0
            for e in self.engines:
                e.seen = {}
            for s in self.slots:
                fill, free = plan["slots"].get(s.name, ([], []))
                s.fill = [Token(byname[c], lp, -1, o) for c, o in fill]
                s.free = [Token(byname[c], lp, -1, o) for c, o in free]
            yield i

            def left(toks):
                return [(t.ctr.name, t.off) for t in toks if t.loop is lp and t.shift == 0]
            self.found[name] = {"rate": {c.name: c.local for c in self.counters if c.local},
                                "slots": {s.name: (left(s.fill), left(s.free)) for s in self.slots}}
            if self.plan is not None:
                assert self.found[name]["rate"] == rate, (name, rate, self.found[name]["rate"])
        self.loop = None
        for e in self.engines:
            e.seen = {}
        for c in self.counters:
            c.count += n * rate.get(c.name, c.local)
            c.local = 0
        for s in self.slots:
            s.fill = [Token(t.ctr, None, 0, t.ctr.count) for t in s.fill if t.ctr.ahead]
            s.free = []
        self.barrier()

    @contextmanager
    def while_rounds_left(self, cond):
        with self.nc.If(cond):
            yield
            for e in self.engines:
                e.wait(*[Token(c, self.loop, 0, c.local) for c in self.counters if c.local])
                e.eng.sem_inc(self.round_end, 1)

    @contextmanager
    def own_counters(self, name):
        usual = [e.ctr for e in self.engines]
        for e in self.engines[:4]:
            e.ctr = Counter(self, f"{e.name}_{name}", 1, prefix=True)
        yield
        for e, c in zip(self.engines, usual):
            e.ctr = c
            c.count += 1
            e.eng.sem_inc(c.sem, 1)
        self.barrier()


def shape_constants():
    c = {}
    r = np.arange(P)
    q, k = r[:, None], r[None, :]
    c["ident"] = np.eye(P, dtype=np.float32)
    c["gla_mask"] = ((q // 64 == k // 64) & (q <= k)).astype(np.float32)
    c["chunk_reset"] = np.broadcast_to((np.arange(SEQ) % 64 != 0).astype(np.float32), (96, SEQ)).copy()
    neg = np.float32(NEG)

    def block(ok):
        return np.where(ok, np.float32(0), neg).astype(np.float32)
    blocks = [block(k >= q), block(k <= q)]
    for dil in (4, 16):
        same = (q - k) % dil == 0
        blocks += [block(same)] * (LT - 1) + [block(same & (k <= q))]
    c["dil_mask"] = np.concatenate(blocks, axis=1)
    half = 16
    inv = np.float32(500000.0) ** (-np.arange(half, dtype=np.float32) / np.float32(half))
    ang = inv[:, None].astype(np.float32) * np.arange(SEQ, dtype=np.float32)[None, :]
    c["dil_cos"] = np.concatenate([np.cos(ang)] * 2).astype(np.float32)
    c["dil_sin"] = np.concatenate([np.sin(ang)] * 2).astype(np.float32)
    rot = np.zeros((P, P), np.float32)
    for m in range(16):
        rot[m + 16, m], rot[m, m + 16] = -1, 1
    c["dil_rot"] = rot
    t = np.arange(SEQ)
    rows, cols = (t // 64).astype(np.float32), (t % 64).astype(np.float32)

    def axial(dim):
        n = dim // 4
        inv = np.float32(10000.0) ** (-np.arange(n, dtype=np.float32) / np.float32(n))
        ang = np.concatenate([inv[:, None] * rows, inv[:, None] * cols]).astype(np.float32)
        cos = np.ones((dim, ALLT), np.float32)
        sin = np.zeros((dim, ALLT), np.float32)
        cos[:, CTX:] = np.repeat(np.cos(ang), 2, axis=0)
        sin[:, CTX:] = np.repeat(np.sin(ang), 2, axis=0)
        return cos, sin
    cb, sb = axial(64)
    c["gqa_cos"], c["gqa_sin"] = np.concatenate([cb, cb]), np.concatenate([sb, sb])
    ca, sa = axial(32)
    c["mla_cos"], c["mla_sin"] = np.zeros((96, ALLT), np.float32), np.zeros((96, ALLT), np.float32)
    c["mla_cos"][64:], c["mla_sin"][64:] = ca, sa
    pair = np.zeros((P, P), np.float32)
    for m in range(0, P, 2):
        pair[m + 1, m], pair[m, m + 1] = -1, 1
    c["pair_rot"] = pair
    c["head_sum"] = (q // 64 == k // 64).astype(np.float32)
    pick = np.zeros((64, 64, P), np.float32)
    for kc in range(64):
        for cc in range(64):
            cs = min(max(cc - 8, 0), 48)
            for half_ in range(2):
                if cs <= kc < cs + 16:
                    pick[32 * half_ + kc - cc + 15, kc, 64 * half_ + cc] = 1
                else:
                    pick[32 * half_ + 31, kc, 64 * half_ + cc] = 1
    c["na_pick"] = pick.reshape(64, 64 * P)
    c["before"] = (q < k).astype(np.float32)
    c["iota32"] = np.broadcast_to(np.arange(32, dtype=np.float32), (P, 32)).copy()
    c["token_ids"] = (r[:, None] + P * np.arange(NT)[None, :]).astype(np.uint32)
    c["zero_table"] = np.zeros((P, NBLK), np.uint32)
    return c


def build(nc, A, out, plan):
    ctx = ExitStack()
    with ctx:
        p = Prog(nc, ctx, plan)
        pe, act, dve, pool, sp = p.pe, p.act, p.dve, p.pool, p.sp
        T, S, V, G = nc.tensor, nc.scalar, nc.vector, nc.gpsimd

        def ctr(name):
            return Counter(p, name, 16)

        uses = {}

        def ctr_ahead(name):
            return Counter(p, name, 16, ahead=True)

        def sb(stack, name, shape, dt=F32):
            uses[name] = uses.get(name, -1) + 1
            name = f"{name}_{uses[name]}" if uses[name] else name
            return stack.enter_context(nc.sbuf_tensor(name, shape, dt))

        PS = ctx.enter_context(nc.psum_tensor("PS", [P, 8, 512], F32))
        PF = PS[:, :, :].rearrange("p b c -> p (b c)")
        B = [Slot(p, f"bank{b}", PS[:, b, :]) for b in range(8)]

        d_const, d_w = ctr("d_const"), [ctr("d_w0"), ctr("d_w1")]
        d_bc, d_wo, d_st, d_g, d_ada = (ctr("d_bc"), ctr("d_wo"), ctr("d_st"), ctr("d_g"),
                                        [ctr("d_ada0"), ctr("d_ada1")])
        d_y, d_h, d_mo = ([ctr(f"{n}{j}") for j in range(2)] for n in ("d_y", "d_h", "d_mo"))
        d_e = [[ctr_ahead(f"d_e{w}{j}") for j in range(2)] for w in ("g", "u", "d")]
        d_x, d_yg = ([Counter(p, f"{n}{j}", 16, by_pool=True, ahead=(n == "d_x")) for j in range(2)]
                     for n in ("d_x", "d_yg"))
        d_idx = Counter(p, "d_idx", 16, by_pool=True)
        d_over = [(Counter(p, f"d_xo{j}", 16, by_pool=True, prefix=True), Counter(p, f"d_wo{j}", 16, prefix=True),
                   Counter(p, f"d_yo{j}", 16, prefix=True)) for j in range(2)]

        X = sb(ctx, "X", [P, NT, D])
        hT = sb(ctx, "hT", [P, KT, ALLT])
        OT = sb(ctx, "OT", [P, NT, D])
        s_hT = Slot(p, "hT")
        s_OT = Slot(p, "OT")
        s_X = [Slot(p, f"X{t}") for t in range(NT)]
        ident = sb(ctx, "ident", [P, P])
        ones = sb(ctx, "ones", [P, P])
        small = sb(ctx, "small", [P, 64])
        s_small = Slot(p, "small")
        hrow = [sb(ctx, f"hrow{n}", [P, D]) for n in range(2)]
        s_hrow = [Slot(p, f"hrow{n}") for n in range(2)]
        eps_c = sb(ctx, "eps_c", [P, 1])

        mods = nc.dram_tensor("mods", [2, 2, 6 * D], F32, kind="Internal").ap()
        h_dram = nc.dram_tensor("h_dram", [ALLT, D], F32, kind="Internal").ap()
        y_dram = nc.dram_tensor("y_dram", [NBLK * P, D], F32, kind="Internal").ap()
        table = [nc.dram_tensor(f"table{n}", [P * NBLK, 1], U32, kind="Internal").ap() for n in range(2)]

        def bcast(row_ap, n):
            return row_ap.rearrange("(a n) -> a n", a=1).to_broadcast([P, n])

        sp.dma(d_const, ident[:], A["c_ident"])
        sp.dma(d_const, X[:, CT:, :], A["x"][0].rearrange("(t p) d -> p t d", p=P))
        t = sp.dma(d_const, X[:, :CT, :], A["ctx_2"][0].rearrange("(t p) d -> p t d", p=P))
        t1 = dve(V.memset, ones[:], 1.0)
        t2 = dve(V.memset, eps_c[:], EPS)
        for s in s_X:
            s.put(t)
        consts_ready = [t, t1, t2]
        for e in (pe, act, dve, pool):
            e.wait(*consts_ready)

        t = dve(V.memset, hrow[0][:], 0.0)
        for b in range(NEXP, NBLK):
            tz = sp.dma(d_st, y_dram[b * P:(b + 1) * P, :], hrow[0][:], after=[t])
        s_hrow[0].got(tz)

        def rstd_of(sums, width, n, after, scratch):
            t = act(S.activation, scratch, sums, ACT.Ln, bias=eps_c[0:n, :], scale=1.0 / width, after=after)
            return act(S.activation, scratch, scratch, ACT.Exp, scale=-0.5, after=[t])

        def transpose_tile(src, k_tiles, dst_T, col, banks, src_fill, src_slot, dst_slot):
            for g0 in range(0, k_tiles, 4):
                b = banks[(g0 // 4) % len(banks)]
                pe.take(B[b])
                pe.wait(*src_fill)
                renew(B[b])
                for j in range(4):
                    tk = pe(T.transpose, PS[:, b, j * P:(j + 1) * P], src[:, (g0 + j) * P:(g0 + j + 1) * P],
                            ident[:], sig=(j == 3))
                B[b].put(tk)
                src_slot.got(tk)
                ev, cp = (act, S.copy) if (g0 // 4) % 2 else (dve, V.tensor_copy)
                tk = ev(cp, dst_T[:, g0:g0 + 4, col:col + P],
                        PS[:, b, :].rearrange("p (j c) -> p j c", j=4), after=[tk])
                B[b].got(tk)
                dst_slot.put(tk)

        def norm_to_T(tiles, gains, shifts, dst_T, dst_slot, cols, to_dram=None):
            n = len(tiles)
            act.take(s_small)
            for t in s_hrow:
                act.take(t)
            renew(s_small)
            for j, (x_ap, x_slot) in enumerate(tiles):
                act.need(x_slot)
                tk = act(S.activation, hrow[j % 2][:], x_ap, ACT.Square, accum_out=small[:, j:j + 1],
                         after=[tk] if j else [])
                x_slot.got(tk)
            tk = rstd_of(small[:, 0:n], D, P, [tk], small[:, 8:8 + n])
            for s in s_hrow:
                s.free = [tk]
                s.fill = []
            for e in (pe, act, dve):
                e.take(dst_slot)
            renew(dst_slot)
            for j, (x_ap, x_slot) in enumerate(tiles):
                s = s_hrow[j % 2]
                dve.take(s)
                renew(s)
                a = dve(V.scalar_tensor_tensor, hrow[j % 2][:], x_ap, small[:, 8 + j:9 + j], gains[j],
                        ALU.mult, ALU.mult, after=[tk])
                x_slot.got(a)
                if shifts is not None:
                    a = dve(V.tensor_tensor, hrow[j % 2][:], hrow[j % 2][:], shifts[j], ALU.add, after=[a])
                s.put(a)
                s_small.got(a)
                transpose_tile(hrow[j % 2], KT, dst_T, cols[j], [2 * (j % 2), 2 * (j % 2) + 1], [a], s, dst_slot)
                if to_dram is not None:
                    s.got(sp.dma(d_h[j % 2], to_dram[cols[j]:cols[j] + P, :], hrow[j % 2][:], after=[a]))
            return

        lat_tiles = [(X[:, t, :], s_X[t]) for t in range(CT, NT)]
        all_tiles = [(X[:, t, :], s_X[t]) for t in range(NT)]

        def w_cols(w, start, width):
            return w.rearrange("(t p) m -> p t m", p=P)[:, :, start] if width is None else \
                w.rearrange("(t p) m -> p t m", p=P)[:, :, bass.ds(start, width)]

        def mm_acc(out_ap, pairs, sig=True, start=True, stop=True, **kw):
            n = len(pairs)
            for j, (a, b) in enumerate(pairs):
                tk = pe(T.matmul, out_ap, a, b, start=start and j == 0, stop=stop and j == n - 1,
                        sig=sig and j == n - 1, **kw)
            return tk

        def softmax_bufs(stack, cols, n_p=2):
            bufs = {"n": 0}
            bufs["P"] = [sb(stack, f"P{j}", [P, cols]) for j in range(3)]
            bufs["PT"] = [sb(stack, f"PT{j}", [P, cols]) for j in range(2)]
            bufs["st"] = [sb(stack, f"st{j}", [P, 4]) for j in range(4)]
            bufs["sP"] = [Slot(p, f"{cols}P{j}") for j in range(3)]
            bufs["sPT"] = [Slot(p, f"{cols}PT{j}") for j in range(2)]
            bufs["sst"] = [Slot(p, f"{cols}st{j}") for j in range(4)]
            return bufs

        def attend(units, bufs, s_banks, pt_banks, o_bank, dv):
            def score(u, x):
                banks = [B[b] for b in s_banks[x % len(s_banks)]]
                b0 = s_banks[x % len(s_banks)][0]
                src = PF[:, b0 * 512:b0 * 512 + u["n"]]
                pe.take(*banks)
                renew(*banks)
                tk = u["scores"](src)
                for b in banks:
                    b.put(tk)
                w, sP, sst, st = bufs["P"][x % 3], bufs["sP"][x % 3], bufs["sst"][x % 4], bufs["st"][x % 4]
                dve.take(sP, sst)
                act.take(sP)
                renew(sP, sst)
                if u.get("bias"):
                    toks = u["bias"](src, w, [tk])
                    for b in banks:
                        b.got(*toks)
                    src = src if u.get("in_place") else w[:, 0:u["n"]]
                else:
                    toks = [tk]
                tk = dve(V.reduce_max, st[:, 0:1], src, AX, after=toks)
                tk = dve(V.tensor_scalar, st[:, 1:2], st[:, 0:1], -u["scale"], None, ALU.mult, after=[tk])
                tk = act(S.activation, w[:, 0:u["n"]], src, ACT.Exp, bias=st[:, 1:2], scale=u["scale"],
                         accum_out=st[:, 2:3], after=[tk] + toks)
                for b in banks:
                    b.got(tk)
                sP.put(tk)
                tk = dve(V.reciprocal, st[:, 3:4], st[:, 2:3], after=[tk])
                sst.put(tk)

            def turn(u, x):
                w, sP, wT, sPT = bufs["P"][x % 3], bufs["sP"][x % 3], bufs["PT"][x % 2], bufs["sPT"][x % 2]
                nb = u["n"] // P
                pe.need(sP)
                act.take(sPT)
                dve.take(sPT)
                renew(sPT)
                for g0 in range(0, nb, 4):
                    b = pt_banks[g0 // 4]
                    m = min(4, nb - g0)
                    pe.take(B[b])
                    renew(B[b])
                    for j in range(m):
                        tk = pe(T.transpose, PS[:, b, j * P:(j + 1) * P],
                                w[:, (g0 + j) * P:(g0 + j + 1) * P], ident[:], sig=(j == m - 1))
                    B[b].put(tk)
                    sP.got(tk)
                    ev, cp = (dve, V.tensor_copy) if g0 // 4 == 1 else (act, S.copy)
                    tk = ev(cp, wT[:, g0 * P:(g0 + m) * P], PS[:, b, 0:m * P], after=[tk])
                    B[b].got(tk)
                    sPT.put(tk)

            def values(u, x):
                wT, sPT, sst, st = bufs["PT"][x % 2], bufs["sPT"][x % 2], bufs["sst"][x % 4], bufs["st"][x % 4]
                nb = u["n"] // P
                pe.need(sPT)
                pe.take(B[o_bank])
                renew(B[o_bank])
                tk = mm_acc(PS[:, o_bank, 0:dv], [(wT[:, j * P:(j + 1) * P], u["v"](j)) for j in range(nb)])
                B[o_bank].put(tk)
                sPT.got(tk)
                act.need(sst)
                act.take(s_OT)
                tk = act(S.activation, u["out"], PS[:, o_bank, 0:dv], ACT.Copy, scale=st[:, 3:4], after=[tk])
                B[o_bank].got(tk)
                sst.got(tk)
                outs.append(tk)

            outs = []
            n = len(units)
            for x in range(n + 3):
                if x < n:
                    score(units[x], x)
                if 2 <= x < n + 2:
                    turn(units[x - 2], x - 2)
                if x >= 3:
                    values(units[x - 3], x - 3)
            return outs

        def gate_and_project(stack, layer_w_out, gate, tiles, row_gate=None):
            wo = sb(stack, "wo", [P, KT, D])
            s_wo = Slot(p, "wo")
            sp.take(s_wo)
            t = sp.dma(d_wo, wo[:], layer_w_out.rearrange("(t p) m -> p t m", p=P))
            s_wo.put(t)
            if gate is not None:
                w, off = gate
                wg = [sb(stack, f"wg{n}", [P, KT, 512]) for n in range(2)]
                s_wg = [Slot(p, f"wg{n}") for n in range(2)]
                sg = [sb(stack, f"sg{n}", [P, 512]) for n in range(2)]
                s_sg = [Slot(p, f"sg{n}") for n in range(2)]
                for c in range(2):
                    s_wg[c].put(sp.dma(d_w[c], wg[c][:], w_cols(w, off + 512 * c, 512)))
                x = 0
                for c in range(2):
                    for n, tl in enumerate(tiles):
                        b = 4 + x % 4
                        s = s_sg[x % 2]
                        v = sg[x % 2]
                        pe.take(B[b])
                        pe.need(s_wg[c])
                        renew(B[b])
                        tk = mm_acc(PS[:, b, :], [(hT[:, k, n * P:(n + 1) * P], wg[c][:, k, :]) for k in range(KT)])
                        B[b].put(tk)
                        s_hT.got(tk)
                        act.take(s)
                        renew(s)
                        tk = act(S.activation, v[:], PS[:, b, :], ACT.Exp, scale=-1.0, after=[tk])
                        tk = dve(V.tensor_scalar, v[:], v[:], 1.0, None, ALU.add, after=[tk])
                        tk = dve(V.reciprocal, v[:], v[:], after=[tk])
                        tk = dve(V.tensor_tensor, v[:], v[:], PS[:, b, :], ALU.mult, after=[tk])
                        B[b].got(tk)
                        tk = dve(V.tensor_tensor, OT[:, tl, 512 * c:512 * c + 512],
                                 OT[:, tl, 512 * c:512 * c + 512], v[:], ALU.mult, after=[tk])
                        s.got(tk)
                        s_OT.put(tk)
                        x += 1
            for e in (act, dve, pe):
                e.take(s_hT)
            renew(s_hT)
            for n, tl in enumerate(tiles):
                transpose_tile(OT[:, tl, :], KT, hT, n * P, [2 * (n % 2), 2 * (n % 2) + 1], s_OT.fill, s_OT, s_hT)
            tmp = sb(stack, "res_tmp", [P, 2, 512])
            s_tmp = [Slot(p, f"res_tmp{n}") for n in range(2)]
            pe.need(s_hT, s_wo)
            x = 0
            for n, tl in enumerate(tiles):
                for c in range(2):
                    b = 4 + x % 4
                    pe.take(B[b])
                    renew(B[b])
                    tk = mm_acc(PS[:, b, :], [(hT[:, k, n * P:(n + 1) * P], wo[:, k, 512 * c:512 * c + 512])
                                              for k in range(KT)])
                    B[b].put(tk)
                    s_hT.got(tk)
                    dve.take(s_X[tl])
                    xs = X[:, tl, 512 * c:512 * c + 512]
                    if row_gate is None:
                        tk = dve(V.tensor_tensor, xs, xs, PS[:, b, :], ALU.add, after=[tk])
                    else:
                        g = row_gate(tl)
                        dve.take(s_tmp[x % 2])
                        renew(s_tmp[x % 2])
                        tk = dve(V.tensor_tensor, tmp[:, x % 2, :], PS[:, b, :], g[:, 512 * c:512 * c + 512],
                                 ALU.mult, after=[tk])
                        B[b].got(tk)
                        tk = dve(V.tensor_tensor, xs, xs, tmp[:, x % 2, :], ALU.add, after=[tk])
                        s_tmp[x % 2].got(tk)
                    B[b].got(tk)
                    s_X[tl].put(tk)
                    x += 1
            s_OT.free, s_OT.fill = [], []
            p.barrier()

        with ExitStack() as st:
            cv = sb(st, "cv", [P, KT, 2])
            ce = sb(st, "ce", [P, KT, 2])
            with nc.allow_non_contiguous_dma("two vectors as columns"):
                sp.dma(d_bc, cv[:, :, 0], A["c_2"][0].rearrange("(t p) -> p t", p=P))
                t = sp.dma(d_bc, cv[:, :, 1], A["c_ctx_2"].rearrange("(t p) -> p t", p=P))
            t = act(S.activation, ce[:], cv[:], ACT.Exp, scale=-1.0, after=[t])
            t = dve(V.tensor_scalar, ce[:], ce[:], 1.0, None, ALU.add, after=[t])
            t = dve(V.reciprocal, ce[:], ce[:], after=[t])
            t_c = dve(V.tensor_tensor, cv[:], cv[:], ce[:], ALU.mult, after=[t])
            wa = [sb(st, f"wa{n}", [P, KT, 1024]) for n in range(2)]
            ba = [sb(st, f"ba{n}", [2, 1024]) for n in range(2)]
            mo = [sb(st, f"mo{n}", [2, 1024]) for n in range(2)]
            s_wa = [Slot(p, f"wa{n}") for n in range(2)]
            s_mo = [Slot(p, f"mo{n}") for n in range(2)]
            pe.wait(t_c)
            with p.repeat("ada", 6) as i:
                for l in range(2):
                    sp.take(s_wa[l])
                    renew(s_wa[l])
                    sp.dma(d_ada[l], wa[l][:], w_cols(A["w_ada_2"][l], i * 1024, 1024))
                    t = sp.dma(d_ada[l], ba[l][:], A["b_ada_2"][l:l + 1, bass.ds(i * 1024, 1024)].to_broadcast([2, 1024]))
                    s_wa[l].put(t)
                    pe.need(s_wa[l])
                    for c in range(2):
                        b = 2 * l + c
                        pe.take(B[b])
                        renew(B[b])
                        t = mm_acc(PS[0:2, b, :], [(cv[:, k, :], wa[l][:, k, c * 512:c * 512 + 512]) for k in range(KT)])
                        B[b].put(t)
                        s_wa[l].got(t)
                        if c == 0:
                            dve.take(s_mo[l])
                            renew(s_mo[l])
                            dve.need(s_wa[l])
                        t = dve(V.tensor_tensor, mo[l][:, c * 512:c * 512 + 512], PS[0:2, b, :],
                                ba[l][:, c * 512:c * 512 + 512], ALU.add, after=[t])
                        B[b].got(t)
                        s_mo[l].put(t)
                        s_wa[l].got(t)
                    s_mo[l].got(act.dma(d_mo[l], mods[l, :, bass.ds(i * 1024, 1024)], mo[l][:], after=[t]))

        memx = ExitStack()
        memT = sb(memx, "memT", [P, KT, NMEM])
        s_memT = Slot(p, "memT")
        with ExitStack() as st:
            mem = sb(st, "mem", [P, NMEM // P, D])
            s_mem = Slot(p, "mem")
            gm = sb(st, "gm", [P, D])
            sp.dma(d_bc, mem[:], A["mem"][0].rearrange("(t p) d -> p t d", p=P))
            t = sp.dma(d_bc, gm[:], bcast(A["mem_norm_w"], D))
            s_mem.put(t)
            dve.wait(t)
            norm_to_T([(mem[:, n, :], s_mem) for n in range(2)], [gm[:]] * 2, None, memT, s_memT, [0, P])
            p.barrier()

        def first_norm(st, w):
            g = sb(st, "gn", [P, D])
            t = sp.dma(d_bc, g[:], bcast(w, D))
            dve.wait(t)
            norm_to_T(lat_tiles, [g[:]] * LT, None, hT, s_hT, [P * n for n in range(LT)])
            p.barrier()

        def memory_attention(layer, w_in, q_off):
            with ExitStack() as st:
                wm = [sb(st, f"wm{j}", [P, KT, P]) for j in range(3)]
                s_wm = Slot(p, "wm")
                qT = sb(st, "mqT", [P, SEQ])
                kz = sb(st, "mkz", [P, 2, NMEM])
                vv = sb(st, "mvv", [P, NMEM // P, P])
                s_q, s_k, s_v = Slot(p, "mq"), Slot(p, "mk"), Slot(p, "mv")
                bufs = softmax_bufs(st, NMEM)
                dve(V.memset, kz[:], 0.0)
                wkv = A["w_memkv"][layer]
                with p.repeat(f"memory{layer}", 2) as i:
                    sp.take(s_wm)
                    renew(s_wm)
                    sp.dma(d_w[0], wm[0][:], w_cols(w_in, i * P + q_off, P))
                    sp.dma(d_w[0], wm[1][:], w_cols(wkv, i * P, P))
                    s_wm.put(sp.dma(d_w[0], wm[2][:], w_cols(wkv, i * P + 256, P)))
                    pe.need(s_wm)
                    pe.take(B[7], B[6], B[5])
                    renew(B[7], B[6], B[5])
                    tq = mm_acc(PS[:, 7, :], [(wm[0][:, k, :], hT[:, k, 0:SEQ]) for k in range(KT)])
                    tk = mm_acc(PS[:, 6, 0:NMEM], [(wm[1][:, k, :], memT[:, k, :]) for k in range(KT)])
                    for n in range(2):
                        tv = mm_acc(PS[:, 5, n * P:(n + 1) * P],
                                    [(memT[:, k, n * P:(n + 1) * P], wm[2][:, k, :]) for k in range(KT)])
                    s_wm.got(tv)
                    act.take(s_q)
                    dve.take(s_k, s_v)
                    renew(s_q, s_k, s_v)
                    t = act(S.copy, qT[:], PS[:, 7, :], after=[tq])
                    s_q.put(t)
                    B[7].got(t)
                    dve(V.tensor_copy, kz[0:64, 0, :], PS[0:64, 6, 0:NMEM], after=[tk])
                    t = dve(V.tensor_copy, kz[64:P, 1, :], PS[64:P, 6, 0:NMEM])
                    s_k.put(t)
                    B[6].got(t)
                    t = dve(V.tensor_copy, vv[:].rearrange("p a b -> p (a b)"), PS[:, 5, 0:256], after=[tv])
                    s_v.put(t)
                    B[5].got(t)
                    pe.need(s_q, s_k, s_v)
                    units = []
                    for hh in range(2):
                        for n in range(LT):
                            units.append(dict(
                                n=NMEM, scale=64 ** -0.5,
                                scores=lambda o, hh=hh, n=n: mm_acc(o, [(qT[:, n * P:(n + 1) * P], kz[:, hh, :])]),
                                v=lambda j, hh=hh: vv[:, j, hh * 64:hh * 64 + 64],
                                out=OT[:, CT + n, bass.ds(i * P + (768 + 64 * hh), 64)]))
                    outs = attend(units, bufs, [[0], [1]], [2], 3, 64)
                    for s in (s_q, s_k, s_v):
                        s.got(*B[3].fill)
                s_OT.put()

        w_a = A["w_in_a"][0]
        with ExitStack() as st:
            first_norm(st, A["norm_w"][0])
        with ExitStack() as st:
            DK, DV, NC_ = 96, 192, SEQ // 64
            wl = sb(st, "wl", [P, KT, 16])
            glT = sb(st, "glT", [16, SEQ])
            gmask = sb(st, "gmask", [P, P])
            reset = sb(st, "reset", [DK, SEQ])
            gw = sb(st, "gw", [P, DV])
            wh = [sb(st, f"wh{n}", [P, KT, 2 * DK + DV]) for n in range(2)]
            wu = [sb(st, f"wu{n}", [16, DK]) for n in range(2)]
            bg = [sb(st, f"bg{n}", [DK, 1]) for n in range(2)]
            s_wh = [Slot(p, f"wh{n}") for n in range(2)]
            with nc.allow_non_contiguous_dma("16 columns"):
                sp.dma(d_bc, wl[:], w_cols(w_a, 1536, 16))
            sp.dma(d_bc, gmask[:], A["c_gla_mask"])
            sp.dma(d_bc, reset[:], A["c_chunk_reset"])
            t = sp.dma(d_bc, gw[:], bcast(A["gla_norm_w"][0], DV))
            pe.wait(t)
            t = mm_acc(PS[0:16, 0, :], [(wl[:, k, :], hT[:, k, 0:SEQ]) for k in range(KT)])
            t = act(S.copy, glT[:], PS[0:16, 0, :], after=[t])
            names = ["u", "l", "bc", "eb", "q", "k", "ko"]
            W = {n: sb(st, "g_" + n, [DK, SEQ]) for n in names}
            sW = {n: Slot(p, "g_" + n) for n in names}
            qz = sb(st, "g_qz", [DK, 2, SEQ])
            koz = sb(st, "g_koz", [P, 2, LT, DK])
            vv = sb(st, "g_v", [P, LT, DV])
            AT = sb(st, "g_AT", [P, SEQ])
            Sx = sb(st, "g_S", [DK, NC_, DV])
            sm = sb(st, "g_sm", [P, 8])
            junk = sb(st, "g_junk", [P, DV])
            s_qz, s_koz, s_vv, s_AT, s_S, s_sm = (Slot(p, n) for n in ("g_qz", "g_koz", "g_v", "g_AT", "g_S", "g_sm"))
            dve(V.memset, qz[:], 0.0)
            dve(V.memset, koz[:], 0.0)
            dve(V.memset, Sx[:], 0.0)

            def chunks(ap):
                return ap.rearrange("d (c t) -> d c t", t=64)

            def gla_head(h, w, wu_, bg_, s_w):
                q, k, kx = (w[:, :, 0:DK], w[:, :, DK:2 * DK], w[:, :, 2 * DK:])
                pe.need(s_w)
                pe.take(B[2], B[0], B[1])
                renew(B[2], B[0], B[1])
                tz = mm_acc(PS[0:DK, 2, :], [(wu_[:], glT[:])])
                tq = mm_acc(PS[0:DK, 0, :], [(q[:, j, :], hT[:, j, 0:SEQ]) for j in range(KT)])
                tk = mm_acc(PS[0:DK, 1, :], [(k[:, j, :], hT[:, j, 0:SEQ]) for j in range(KT)])
                pe.take(B[3], B[4])
                renew(B[3], B[4])
                for n in range(LT):
                    tv = mm_acc(PS[:, 3 + n // 2, (n % 2) * DV:(n % 2) * DV + DV],
                                [(hT[:, j, n * P:(n + 1) * P], kx[:, j, :]) for j in range(KT)])
                s_w.got(tv)
                act.take(s_vv)
                renew(s_vv)
                for j in range(2):
                    t = act(S.copy, vv[:, 2 * j:2 * j + 2, :],
                            PS[:, 3 + j, 0:2 * DV].rearrange("p (a b) -> p a b", a=2), after=[tv])
                    B[3 + j].got(t)
                s_vv.put(t)
                act.take(sW["u"])
                renew(sW["u"])
                act.need(s_w)
                t = act(S.activation, W["u"][:], PS[0:DK, 2, :], ACT.Identity, bias=bg_[:], after=[tz])
                B[2].got(t)
                s_w.got(t)
                dve.take(sW["l"])
                renew(sW["l"])
                a = dve(V.tensor_scalar, W["l"][:], W["u"][:], -1.0, None, ALU.mult, after=[t])
                a = dve(V.tensor_tensor, W["l"][:], W["l"][:], W["u"][:], ALU.min, after=[a])
                a = act(S.activation, W["l"][:], W["l"][:], ACT.Exp, after=[a])
                a = act(S.activation, W["l"][:], W["l"][:], ACT.Ln, bias=1.0, after=[a])
                a = dve(V.scalar_tensor_tensor, W["u"][:], W["u"][:], 0.0, W["l"][:], ALU.min, ALU.subtract, after=[a])
                sW["l"].got(a)
                dve.take(sW["bc"])
                renew(sW["bc"])
                tb = dve(V.tensor_tensor_scan, W["bc"][:], reset[:], W["u"][:], 0.0, ALU.mult, ALU.add, after=[a])
                sW["u"].got(tb)
                tau = 1.0 / 16.0
                act.take(sW["eb"])
                renew(sW["eb"])
                te = act(S.activation, W["eb"][:], W["bc"][:], ACT.Exp, scale=tau, after=[tb])
                act.take(sW["l"])
                renew(sW["l"])
                tn = act(S.activation, W["l"][:], W["bc"][:], ACT.Exp, scale=-tau, after=[tb])
                dve.take(sW["ko"])
                renew(sW["ko"])
                last = chunks(W["bc"][:])[:, :, 63:64].to_broadcast([DK, NC_, 64])
                t = dve(V.tensor_tensor, chunks(W["ko"][:]), last, chunks(W["bc"][:]), ALU.subtract, after=[tb])
                sW["bc"].got(te, tn, t)
                t = act(S.activation, W["ko"][:], W["ko"][:], ACT.Exp, scale=tau, after=[t])
                dve.take(sW["q"], sW["k"], s_qz)
                renew(sW["q"], sW["k"], s_qz)
                a = dve(V.scalar_tensor_tensor, W["q"][:], PS[0:DK, 0, :], DK ** -0.5, W["eb"][:], ALU.mult,
                        ALU.mult, after=[tq, te])
                B[0].got(a)
                sW["q"].put(a)
                b = dve(V.tensor_tensor, W["k"][:], PS[0:DK, 1, :], W["l"][:], ALU.mult, after=[tk, tn])
                sW["l"].got(b)
                sW["k"].put(b)
                c = dve(V.tensor_tensor, W["ko"][:], PS[0:DK, 1, :], W["ko"][:], ALU.mult, after=[t])
                B[1].got(b, c)
                for par in range(2):
                    src = W["q"][:].rearrange("d (n c t) -> d n c t", c=2, t=64)[:, :, par, :]
                    dst = qz[:, par, :].rearrange("d (n c t) -> d n c t", c=2, t=64)[:, :, par, :]
                    t = dve(V.tensor_copy, dst, src, after=[a])
                s_qz.put(t)
                sW["q"].got(t)
                pe.take(B[6], B[5])
                renew(B[6], B[5])
                pe.wait(c)
                for n in range(LT):
                    t = pe(T.transpose, PS[:, 6, n * DK:(n + 1) * DK], W["ko"][:, n * P:(n + 1) * P],
                           ident[0:DK, 0:DK], sig=(n == LT - 1))
                sW["ko"].got(t)
                B[6].put(t)
                dve.take(s_koz)
                renew(s_koz)
                for par in range(2):
                    r = slice(64 * par, 64 * par + 64)
                    t2 = dve(V.tensor_copy, koz[r, par, :, :].rearrange("p a b -> p (a b)"),
                             PS[r, 6, 0:LT * DK], after=[t])
                B[6].got(t2)
                s_koz.put(t2)
                pe.wait(b)
                for n in range(LT):
                    t = pe(T.matmul, PS[:, 5, n * P:(n + 1) * P], W["k"][:, n * P:(n + 1) * P],
                           W["q"][:, n * P:(n + 1) * P], start=True, stop=True, sig=(n == LT - 1))
                B[5].put(t)
                sW["k"].got(t)
                sW["q"].got(t)
                dve.take(s_AT)
                renew(s_AT)
                t = dve(V.tensor_tensor, AT[:].rearrange("p (n c) -> p n c", n=LT),
                        PS[:, 5, :].rearrange("p (n c) -> p n c", n=LT),
                        gmask[:].unsqueeze(1).to_broadcast([P, LT, P]), ALU.mult, after=[t])
                B[5].got(t)
                s_AT.put(t)
                pe.need(s_koz, s_vv)
                dve.take(s_S)
                renew(s_S)
                t = None
                for n0 in range(0, NC_ - 1, 2):
                    b = (0, 1, 2, 7)[n0 // 2]
                    pair_ = range(n0, min(n0 + 2, NC_ - 1))
                    pe.take(B[b])
                    renew(B[b])
                    for n in pair_:
                        a = pe(T.matmul, PS[0:DK, b, (n % 2) * DV:(n % 2) * DV + DV], koz[:, n % 2, n // 2, :],
                               vv[:, n // 2, :], start=True, stop=True)
                    B[b].put(a)
                    for n in pair_:
                        t = dve(V.scalar_tensor_tensor, Sx[:, n + 1, :], Sx[:, n, :],
                                W["eb"][:, 64 * n + 63:64 * n + 64], PS[0:DK, b, (n % 2) * DV:(n % 2) * DV + DV],
                                ALU.mult, ALU.add, after=[a, t])
                        s_S.put(t)
                    B[b].got(t)
                s_koz.got(a)
                sW["eb"].got(t)
                pe.need(s_AT, s_qz)
                pe.take(B[3], B[4])
                renew(B[3], B[4])
                act.take(s_sm)
                renew(s_sm)
                for n in range(LT):
                    pe.wait(s_S.fill[min(2 * n, NC_ - 2)])
                    o = PS[:, 3 + n // 2, (n % 2) * DV:(n % 2) * DV + DV]
                    t = mm_acc(o, [(AT[:, n * P:(n + 1) * P], vv[:, n, :]),
                                   (qz[:, 0, n * P:(n + 1) * P], Sx[:, 2 * n, :]),
                                   (qz[:, 1, n * P:(n + 1) * P], Sx[:, 2 * n + 1, :])])
                    B[3 + n // 2].put(t)
                for n in range(LT):
                    o = PS[:, 3 + n // 2, (n % 2) * DV:(n % 2) * DV + DV]
                    tn = act(S.activation, junk[:], o, ACT.Square, accum_out=sm[:, n:n + 1], after=[t, tn])
                for s in (s_AT, s_vv, s_qz, s_S):
                    s.got(t)
                tn = rstd_of(sm[:, 0:LT], DV, P, [tn], sm[:, 4:8])
                for n in range(LT):
                    o = PS[:, 3 + n // 2, (n % 2) * DV:(n % 2) * DV + DV]
                    t = dve(V.scalar_tensor_tensor, OT[:, CT + n, bass.ds(h, DV)], o, sm[:, 4 + n:5 + n], gw[:],
                            ALU.mult, ALU.mult, after=[tn])
                    B[3 + n // 2].got(t)
                s_sm.got(t)
                s_OT.put(t)

            with p.repeat("gla", 2) as i:
                for n in range(2):
                    s, w = s_wh[n], wh[n]
                    sp.take(s)
                    renew(s)
                    col = i * (2 * DK) + n * DK
                    sp.dma(d_w[n], w[:, :, 0:DK], w_cols(w_a, col, DK))
                    sp.dma(d_w[n], w[:, :, DK:2 * DK], w_cols(w_a, col + 384, DK))
                    sp.dma(d_w[n], w[:, :, 2 * DK:], w_cols(w_a, i * (2 * DV) + (n * DV + 768), DV))
                    sp.dma(d_w[n], wu[n][:], A["w_gate_up"][0][:, bass.ds(col, DK)])
                    s.put(sp.dma(d_w[n], bg[n][:],
                                 A["b_gate"][0].rearrange("(n a) -> n a", a=1)[bass.ds(col, DK), :]))
                for n in range(2):
                    gla_head(i * (2 * DV) + n * DV, wh[n], wu[n], bg[n], s_wh[n])
        memory_attention(0, w_a, 1552)
        with ExitStack() as st:
            gate_and_project(st, A["w_out"][0], (w_a, 1808), list(range(CT, NT)))

        w_b = A["w_in_b"][0]
        with ExitStack() as st:
            first_norm(st, A["norm_w"][1])
        with ExitStack() as st:
            mask = sb(st, "mask", [P, 10 * P])
            cosT, sinT = sb(st, "cosT", [32, SEQ]), sb(st, "sinT", [32, SEQ])
            rot = sb(st, "rot", [P, P])
            wq = [sb(st, f"wq{g}", [P, KT, 3, P]) for g in range(3)]
            s_wq = [Slot(p, f"wq{g}") for g in range(3)]
            d_q = [d_w[0], d_w[1], d_g]
            qk = [[sb(st, f"qk{g}{j}", [P, SEQ]) for j in range(2)] for g in range(3)]
            vg = [sb(st, f"vg{g}", [P, LT, P]) for g in range(3)]
            rt = [sb(st, f"rt{j}", [32, SEQ]) for j in range(2)]
            s_qk = [[Slot(p, f"qk{g}{j}") for j in range(2)] for g in range(3)]
            s_vg = [Slot(p, f"vg{g}") for g in range(3)]
            s_rt = [Slot(p, f"rt{j}") for j in range(2)]
            bufs = softmax_bufs(st, 10 * P)
            sp.dma(d_bc, mask[:], A["c_dil_mask"])
            sp.dma(d_bc, cosT[:], A["c_dil_cos"])
            sp.dma(d_bc, sinT[:], A["c_dil_sin"])
            sp.dma(d_bc, rot[:], A["c_dil_rot"])
            with p.repeat("dilated", 6) as h:
                for g in range(3):
                    sp.take(s_wq[g])
                    renew(s_wq[g])
                    for j in range(3):
                        t = sp.dma(d_q[g], wq[g][:, :, j, :], w_cols(w_b, h * P + (3 * g + j) * 768, P))
                    s_wq[g].put(t)
                for g in range(3):
                    pe.need(s_wq[g])
                    for j in range(2):
                        pe.take(B[j])
                        renew(B[j])
                        t = mm_acc(PS[:, j, :], [(wq[g][:, k, j, :], hT[:, k, 0:SEQ]) for k in range(KT)])
                        act.take(s_qk[g][j])
                        renew(s_qk[g][j])
                        t = act(S.copy, qk[g][j][:], PS[:, j, :], after=[t])
                        B[j].got(t)
                        s_qk[g][j].put(t)
                    pe.take(B[2])
                    renew(B[2])
                    for n in range(LT):
                        t = mm_acc(PS[:, 2, n * P:(n + 1) * P],
                                   [(hT[:, k, n * P:(n + 1) * P], wq[g][:, k, 2, :]) for k in range(KT)])
                    s_wq[g].got(t)
                    act.take(s_vg[g])
                    renew(s_vg[g])
                    t = act(S.copy, vg[g][:].rearrange("p a b -> p (a b)"), PS[:, 2, :], after=[t])
                    B[2].got(t)
                    s_vg[g].put(t)
                    for j in range(2):
                        b, x = 3 + j, qk[g][j][0:32, :]
                        pe.take(B[b])
                        renew(B[b])
                        pe.need(s_qk[g][j])
                        t = mm_acc(PS[:, b, :], [(rot[:], qk[g][j][:])])
                        dve.take(s_rt[j])
                        renew(s_rt[j])
                        t = dve(V.tensor_tensor, rt[j][:], PS[0:32, b, :], sinT[:], ALU.mult, after=[t])
                        B[b].got(t)
                        a = dve(V.tensor_tensor, x, x, cosT[:], ALU.mult, after=[t])
                        t = dve(V.tensor_tensor, x, x, rt[j][:], ALU.add, after=[a])
                        s_rt[j].got(t)
                        s_qk[g][j].put(t)
                for g in range(3):
                    pe.need(*s_qk[g], s_vg[g])
                units = []
                for n in range(LT):
                    lo = max(n - 1, 0)
                    spans = [(0, lo, n + 1)] + [(1, 0, n + 1), (2, 0, n + 1)]
                    mcol = [(2 - (n + 1 - lo)) * P, (2 + LT - n - 1) * P, (2 + 2 * LT - n - 1) * P]
                    blocks = [(g, b) for g, a, z in spans for b in range(a, z)]

                    def scores(o, n=n, blocks=blocks):
                        tk = None
                        for x, (g, b) in enumerate(blocks):
                            tk = pe(T.matmul, o[:, x * P:(x + 1) * P], qk[g][0][:, n * P:(n + 1) * P],
                                    qk[g][1][:, b * P:(b + 1) * P], start=True, stop=True,
                                    sig=(x == len(blocks) - 1))
                        return tk

                    def bias(src, dst, toks, spans=spans, mcol=mcol):
                        at, out_ = 0, []
                        for (g, a, z), mc in zip(spans, mcol):
                            w = (z - a) * P
                            out_.append(dve(V.tensor_tensor, dst[:, at:at + w], src[:, at:at + w],
                                            mask[:, mc:mc + w], ALU.add, after=toks))
                            at += w
                        return out_

                    units.append(dict(n=len(blocks) * P, scale=P ** -0.5, scores=scores, bias=bias,
                                      v=lambda j, blocks=blocks: vg[blocks[j][0]][:, blocks[j][1], :],
                                      out=OT[:, CT + n, bass.ds(h * P, P)]))
                attend(units, bufs, [[0, 1, 2]], [3, 4, 5], 6, P)
                for g in range(3):
                    for s in (*s_qk[g], s_vg[g]):
                        s.got(*B[6].fill)
        memory_attention(1, w_b, 6912)
        with ExitStack() as st:
            gate_and_project(st, A["w_out"][1], (w_b, 7168), list(range(CT, NT)))
        memx.close()

        def norm_rows(st, w, tiles, dst):
            g = sb(st, "gf", [P, D])
            junk = sb(st, "fjunk", [P, D])
            t = sp.dma(d_bc, g[:], bcast(w, D))
            act.wait(t)
            dve.wait(t)
            t = None
            for j, tl in enumerate(tiles):
                t = act(S.activation, junk[:], X[:, tl, :], ACT.Square, accum_out=small[:, j:j + 1], after=[t])
            t = rstd_of(small[:, 0:LT], D, P, [t], small[:, 8:8 + LT])
            for j, tl in enumerate(tiles):
                a = dve(V.scalar_tensor_tensor, dst(tl), X[:, tl, :], small[:, 8 + j:9 + j], g[:],
                        ALU.mult, ALU.mult, after=[t])
            p.barrier()

        with ExitStack() as st:
            norm_rows(st, A["final_norm_w"], range(CT, NT), lambda tl: X[:, tl, :])

        def modulation(st, layer, part, norm_w, who, w):
            g, s = sb(st, f"mg{who}", [P, D]), sb(st, f"ms{who}", [P, D])
            stream = (d_bc, d_wo)[who]
            row = mods[layer, who]
            sp.dma(stream, s[:], bcast(row[(3 * part) * D:(3 * part + 1) * D], D))
            sp.dma(stream, g[:], bcast(row[(3 * part + 1) * D:(3 * part + 2) * D], D))
            t = sp.dma(stream, w[:], bcast(norm_w, D)) if who == 0 else Token(stream, None, 0, stream.count)
            dve(V.scalar_tensor_tensor, g[:], g[:], 1.0, w[:], ALU.add, ALU.mult, after=[t])
            return g, s

        def modulated_T(layer, part, norm_w, tiles, to_dram=None):
            with ExitStack() as st:
                mw = sb(st, "mw", [P, D])
                gl, sl = modulation(st, layer, part, norm_w, 0, mw)
                gc, sc = modulation(st, layer, part, norm_w, 1, mw) if 0 in tiles else (None, None)
                dve.wait(*p.everything(ahead=False))
                norm_to_T([(X[:, t, :], s_X[t]) for t in tiles], [gc[:] if t < CT else gl[:] for t in tiles],
                          [sc[:] if t < CT else sl[:] for t in tiles], hT, s_hT,
                          [P * j for j in range(len(tiles))], to_dram)
                p.barrier()

        def row_gates(st, layer, part, with_ctx):
            gs = []
            for who in range(2 if with_ctx else 1):
                g = sb(st, f"rg{who}", [P, D])
                t = sp.dma(d_bc, g[:], bcast(mods[layer, who, (3 * part + 2) * D:(3 * part + 3) * D], D))
                gs.append(g)
            dve.wait(t)
            return lambda tl: gs[1][:] if tl < CT else gs[0][:]

        def spans():
            return [(0, NSPAN), (NSPAN, ALLT)]

        def project_T(dst, w, kt, rhs, banks, m, evac=None):
            toks = []
            for (a, z), b in zip(spans(), banks):
                pe.take(B[b])
                renew(B[b])
                t = mm_acc(PS[0:m, b, 0:z - a], [(w(k), rhs[:, k, a:z]) for k in range(kt)])
                t = act(S.copy, dst[:, a:z], PS[0:m, b, 0:z - a], after=[t])
                B[b].got(t)
                toks.append(t)
            return toks

        def feature_norm(xs, sq, s_sq, summer, width, gains, banks, n=P):
            toks = []
            for (a, z), b in zip(spans(), banks):
                pe.take(B[b])
                renew(B[b])
                for j, x in enumerate(xs):
                    act.take(s_sq)
                    renew(s_sq)
                    t = act(S.activation, sq[0:n, 0:z - a], x[:, a:z], ACT.Square)
                    t = pe(T.matmul, PS[0:n, b, 0:z - a], summer[0:n, 0:n], sq[0:n, 0:z - a], start=(j == 0),
                           stop=(j == len(xs) - 1), after=[t])
                    s_sq.got(t)
                act.take(s_sq)
                renew(s_sq)
                t = rstd_of(PS[0:n, b, 0:z - a], width, n, [t], sq[0:n, 0:z - a])
                B[b].got(t)
                for j, x in enumerate(xs):
                    t2 = dve(V.scalar_tensor_tensor, x[:, a:z], x[:, a:z], gains[j], sq[0:n, 0:z - a],
                             ALU.mult, ALU.mult, after=[t])
                    toks.append(t2)
                s_sq.got(t2)
            return toks

        def rope(x, r0, r1, cos, sin, rot_m, tmp, s_tmp, banks, after, k0=0):
            toks = []
            for n, ((a, z), b) in enumerate(zip(spans(), banks)):
                pe.take(B[b])
                renew(B[b])
                t = pe(T.matmul, PS[k0:r1, b, 0:z - a], rot_m[k0:r1, k0:r1], x[k0:r1, a:z], start=True, stop=True,
                       after=after)
                dve.take(s_tmp)
                renew(s_tmp)
                t1 = dve(V.tensor_tensor, tmp[r0:r1, 0:z - a], PS[r0:r1, b, 0:z - a], sin[r0:r1, a:z], ALU.mult, after=[t])
                B[b].got(t1)
                t2 = dve(V.tensor_tensor, x[r0:r1, a:z], x[r0:r1, a:z], cos[r0:r1, a:z], ALU.mult, after=[t])
                t = dve(V.tensor_tensor, x[r0:r1, a:z], x[r0:r1, a:z], tmp[r0:r1, 0:z - a], ALU.add, after=[t1, t2])
                s_tmp.got(t)
                toks.append(t)
            return toks

        def lat_and_ctx_units(qT, kk, v, scale, out, with_ctx=True, dq=P):
            units = []
            for n in range(0 if with_ctx else CT, NT):
                nk = CTX if n < CT else ALLT

                def scores(o, n=n, nk=nk):
                    a = pe(T.matmul, o[:, 0:min(nk, 512)], qT[:, n * P:(n + 1) * P], kk[:, 0:min(nk, 512)],
                           start=True, stop=True, sig=nk <= 512)
                    if nk > 512:
                        a = pe(T.matmul, o[:, 512:nk], qT[:, n * P:(n + 1) * P], kk[:, 512:nk], start=True, stop=True)
                    return a
                units.append(dict(n=nk, scale=scale, scores=scores, v=v, out=out(n)))
            return units

        modulated_T(0, 0, A["norm_mix_2"][0], range(NT))
        w_ab = A["ab_w_in_2"][0]
        with ExitStack() as st:
            cq = [sb(st, f"cq{j}", [P, ALLT]) for j in range(3)]
            ckv = [sb(st, f"ckv{j}", [P, ALLT]) for j in range(2)]
            kr = sb(st, "kr", [96, ALLT])
            va = sb(st, "va", [P, NT, 512])
            vb = sb(st, "vb", [P, NT, P])
            kz = sb(st, "kz", [P, 2, 2, ALLT])
            mcos, msin = sb(st, "mcos", [96, ALLT]), sb(st, "msin", [96, ALLT])
            gcos, gsin = sb(st, "gcos", [P, ALLT]), sb(st, "gsin", [P, ALLT])
            pair, hsum = sb(st, "pair", [P, P]), sb(st, "hsum", [P, P])
            gains = sb(st, "gains", [P, 8])
            sq = sb(st, "sq", [P, NSPAN])
            s_sq = Slot(p, "sq")
            tmp_ = sb(st, "rtmp", [P, NSPAN])
            s_tmp_ = Slot(p, "rtmp")
            dve(V.memset, kz[:], 0.0)
            with ExitStack() as sw:
                wx = sb(sw, "wx", [P, KT, 928])
                wv = sb(sw, "wv", [P, 2, 512])
                kb = sb(sw, "kb", [P, ALLT])
                sp.dma(d_w[0], wx[:, :, 0:672], w_cols(w_ab, 0, 672))
                sp.dma(d_w[0], wx[:, :, 672:928], w_cols(w_ab, 1184, 256))
                for j in range(2):
                    sp.dma(d_w[0], wv[:, j, :].rearrange("p (h c) -> p h c", h=8),
                           A["mla_w_kv_up_2"][0][j * P:(j + 1) * P, :].rearrange("p (h c) -> p h c", h=8)[:, :, 64:128])
                for dst, name in ((mcos, "mla_cos"), (msin, "mla_sin"), (gcos, "gqa_cos"), (gsin, "gqa_sin"),
                                  (pair, "pair_rot"), (hsum, "head_sum")):
                    sp.dma(d_w[0], dst[:], A["c_" + name])
                with nc.allow_non_contiguous_dma("norm weights as columns"):
                    sp.dma(d_w[0], gains[:, 0:3], A["mla_q_norm_2"][0].rearrange("(t p) -> p t", p=P))
                    sp.dma(d_w[0], gains[:, 3:5], A["mla_kv_norm_2"][0].rearrange("(t p) -> p t", p=P))
                    for half in range(2):
                        r = slice(64 * half, 64 * half + 64)
                        sp.dma(d_w[0], gains[r, 5:6], A["gqa_q_norm_2"][0].rearrange("(p a) -> p a", a=1))
                        t = sp.dma(d_w[0], gains[r, 6:7], A["gqa_k_norm_2"][0].rearrange("(p a) -> p a", a=1))
                for e in (pe, act, dve):
                    e.wait(t)
                tq, tkv = [], []
                for j in range(3):
                    tq += project_T(cq[j][:], lambda k, j=j: wx[:, k, j * P:(j + 1) * P], KT, hT, (0, 1), P)
                for j in range(2):
                    tkv += project_T(ckv[j][:], lambda k, j=j: wx[:, k, 384 + j * P:384 + (j + 1) * P], KT, hT, (2, 3), P)
                act.wait(*tq, *tkv)
                feature_norm([c[:] for c in cq], sq, s_sq, ones, 384, [gains[:, j:j + 1] for j in range(3)], (4, 5))
                tkv = feature_norm([c[:] for c in ckv], sq, s_sq, ones, 256, [gains[:, 3 + j:4 + j] for j in range(2)], (6, 7))
                tr = []
                for (a, z), b in zip(spans(), (0, 1)):
                    pe.take(B[b])
                    renew(B[b])
                    t = mm_acc(PS[64:96, b, 0:z - a], [(wx[:, k, 640:672], hT[:, k, a:z]) for k in range(KT)])
                    t = act(S.copy, kr[64:96, a:z], PS[64:96, b, 0:z - a], after=[t])
                    B[b].got(t)
                    tr.append(t)
                rope(kr, 64, 96, mcos, msin, pair, tmp_, s_tmp_, (2, 3), tr, k0=64)
                tk = project_T(kb[:], lambda k: wx[:, k, 672:800], KT, hT, (0, 1), P)
                act.wait(*tk)
                tk = feature_norm([kb[:]], sq, s_sq, hsum, 64, [gains[:, 6:7]], (4, 5))
                tk = rope(kb, 0, P, gcos, gsin, pair, tmp_, s_tmp_, (2, 3), tk)
                for kv in range(2):
                    r = slice(64 * kv, 64 * kv + 64)
                    dve(V.tensor_copy, kz[r, kv, kv, :], kb[r, :], after=tk)
                for kv in range(2):
                    o = 64 * (1 - kv)
                    sp.dma(d_g, kz[o:o + 64, kv, 1 - kv, :], kb[64 * kv:64 * kv + 64, :], after=tk)
                pe.wait(*tkv)
                for n in range(NT):
                    b = 4 + n % 4
                    pe.take(B[b])
                    renew(B[b])
                    t = mm_acc(PS[:, b, :], [(ckv[k][:, n * P:(n + 1) * P], wv[:, k, :]) for k in range(2)])
                    t = act(S.copy, va[:, n, :], PS[:, b, :], after=[t])
                    B[b].got(t)
                for n in range(NT):
                    b = n % 4
                    pe.take(B[b])
                    renew(B[b])
                    t = mm_acc(PS[:, b, 0:P], [(hT[:, k, n * P:(n + 1) * P], wx[:, k, 800:928]) for k in range(KT)])
                    t = act(S.copy, vb[:, n, :], PS[:, b, 0:P], after=[t])
                    B[b].got(t)
                p.barrier()
            bufs = softmax_bufs(st, ALLT)
            with ExitStack() as sh:
                wqu = [sb(sh, f"wqu{n}", [P, 3, 96]) for n in range(2)]
                wku = [sb(sh, f"wku{n}", [P, 2, 64]) for n in range(2)]
                s_wu = [Slot(p, f"wqku{n}") for n in range(2)]
                qT = [sb(sh, f"aqT{n}", [96, ALLT]) for n in range(2)]
                kT = [sb(sh, f"akT{n}", [96, ALLT]) for n in range(2)]
                s_qT, s_kT = [Slot(p, f"aqT{n}") for n in range(2)], [Slot(p, f"akT{n}") for n in range(2)]
                with p.repeat("mla", 4) as i:
                    for n in range(2):
                        sp.take(s_wu[n])
                        renew(s_wu[n])
                        sp.dma(d_w[n], wqu[n][:], A["mla_w_q_up_2"][0].rearrange("(t p) m -> p t m", p=P)
                               [:, :, bass.ds(i * 192 + 96 * n, 96)])
                        s_wu[n].put(sp.dma(d_w[n], wku[n][:], A["mla_w_kv_up_2"][0].rearrange("(t p) m -> p t m", p=P)
                                           [:, :, bass.ds(i * 256 + P * n, 64)]))
                    units = []
                    for n in range(2):
                        pe.need(s_wu[n])
                        act.take(s_qT[n], s_kT[n])
                        dve.take(s_kT[n])
                        renew(s_qT[n], s_kT[n])
                        for j, (a, z) in enumerate(spans()):
                            b = 2 * j
                            pe.take(B[b], B[b + 1])
                            renew(B[b], B[b + 1])
                            t = mm_acc(PS[0:96, b, 0:NSPAN], [(wqu[n][:, k, :], cq[k][:, a:z]) for k in range(3)])
                            t = act(S.copy, qT[n][:, a:z], PS[0:96, b, 0:NSPAN], after=[t])
                            B[b].got(t)
                            s_qT[n].put(t)
                            t = mm_acc(PS[0:64, b + 1, 0:NSPAN], [(wku[n][:, k, :], ckv[k][:, a:z]) for k in range(2)])
                            s_wu[n].got(t)
                            t = act(S.copy, kT[n][0:64, a:z], PS[0:64, b + 1, 0:NSPAN], after=[t])
                            B[b + 1].got(t)
                            s_kT[n].put(t)
                        s_kT[n].put(dve(V.tensor_copy, kT[n][64:96, :], kr[64:96, :]))
                        s_qT[n].put(*rope(qT[n], 64, 96, mcos, msin, pair, tmp_, s_tmp_, (0, 2), s_qT[n].fill))
                    for n in range(2):
                        units += lat_and_ctx_units(
                            qT[n], kT[n], lambda j, n=n: va[:, j, bass.ds(i * P + 64 * n, 64)], 96 ** -0.5,
                            lambda tl, n=n: OT[:, tl, bass.ds(i * P + 64 * n, 64)])
                    pe.need(*s_qT, *s_kT)
                    attend(units, bufs, [[0, 1], [2, 3]], [4, 5], 6, 64)
                    for s in (*s_qT, *s_kT):
                        s.got(*B[6].fill)
            with ExitStack() as sh:
                wg = sb(sh, "wgq", [P, KT, P])
                s_wg = Slot(p, "wgq")
                qT = sb(sh, "gqT", [P, ALLT])
                kc = sb(sh, "kcur", [P, 2, ALLT])
                s_qT, s_kc = Slot(p, "gqT"), Slot(p, "kcur")
                with p.repeat("gqa", 4) as i:
                    sp.take(s_wg)
                    renew(s_wg)
                    s_wg.put(sp.dma(d_w[0], wg[:], w_cols(w_ab, i * P + 672, P)))
                    pe.need(s_wg)
                    act.take(s_qT)
                    dve.take(s_qT, s_kc)
                    renew(s_qT, s_kc)
                    s_kc.put(dve(V.tensor_copy, kc[:], kz[:].rearrange("p a b c -> p a (b c)")
                                 [:, bass.ds(i // 2, 1), :].rearrange("p a (b c) -> p (a b) c", b=2)))
                    t = project_T(qT[:], lambda k: wg[:, k, :], KT, hT, (0, 2), P)
                    s_wg.got(*t)
                    act.wait(*t)
                    t = feature_norm([qT[:]], sq, s_sq, hsum, 64, [gains[:, 5:6]], (0, 2))
                    t = rope(qT, 0, P, gcos, gsin, pair, tmp_, s_tmp_, (0, 2), t)
                    s_qT.put(*t)
                    pe.need(s_qT, s_kc)
                    units = []
                    for hh in range(2):
                        units += lat_and_ctx_units(
                            qT, kc[:, hh, :], lambda j: vb[:, j, bass.ds((i // 2) * 64, 64)], 64 ** -0.5,
                            lambda tl, hh=hh: OT[:, tl, bass.ds(i * P + (512 + 64 * hh), 64)])
                    attend(units, bufs, [[0, 1], [2, 3]], [4, 5], 6, 64)
                    for s in (s_qT, s_kc):
                        s.got(*B[6].fill)
        with ExitStack() as st:
            rg = row_gates(st, 0, 0, True)
            gate_and_project(st, A["ab_w_out_2"][0], None, list(range(NT)), rg)

        def moe(layer, tiles):
            n_t = len(tiles)
            with ExitStack() as st:
                E = expert_buffers(st, layer)
                for e in range(2):
                    for w in range(3):
                        load(E, w, e, e % 2)
                modulated_T(layer, 1, A["norm_ffn_2"][layer], tiles, to_dram=h_dram)
                idx = sb(st, "idx", [P, NBLK], U32)
                rows = sb(st, "rows", [P, 2, NT], U32)
                wts = sb(st, "wts", [P, 2, NT])
                n_ov = sb(st, "n_ov", [P, 1], U32)
                ov_e = sb(st, "ov_e", [P, 16], U32)
                route(st, layer, n_t, idx, rows, wts, n_ov, ov_e)
                experts(E, layer, idx, n_ov, ov_e)
                g2 = row_gates(st, layer, 1, 0 in tiles)
                yr = [[OT[:, 2 * a + b, :] for b in range(2)] for a in range(2)]
                s_yr = [Slot(p, f"yr{a}") for a in range(2)]
                for j, tl in enumerate(tiles):
                    y, s = yr[j % 2], s_yr[j % 2]
                    pool.take(s)
                    renew(s)
                    for b in range(2):
                        t = d_yg[j % 2].counted(G.indirect_dma_start(
                            y[b][:], None, y_dram, bass.IndirectOffsetOnAxis(ap=rows[:, b, j:j + 1], axis=0)))
                    s.put(t)
                    t = dve(V.tensor_scalar, y[0][:], y[0][:], wts[:, 0, j:j + 1], None, ALU.mult, after=[t])
                    t = dve(V.scalar_tensor_tensor, y[0][:], y[1][:], wts[:, 1, j:j + 1], y[0][:], ALU.mult,
                            ALU.add, after=[t])
                    t = dve(V.tensor_tensor, y[0][:], y[0][:], g2(tl), ALU.mult, after=[t])
                    t = dve(V.tensor_tensor, X[:, tl, :], X[:, tl, :], y[0][:], ALU.add, after=[t])
                    s.got(t)
                p.barrier(ahead=True)

        def route(st, layer, n_t, idx, rows, wts, n_ov, ov_e):
            with ExitStack() as s:
                wr = sb(s, "wr", [P, KT, 36])
                br = sb(s, "br", [P, 36])
                L = sb(s, "L", [P, NT, 36])
                io = sb(s, "io", [P, 32])
                tri = sb(s, "tri", [P, P])
                ids = sb(s, "ids", [P, NT], U32)
                with nc.allow_non_contiguous_dma("router weights"):
                    sp.dma(d_bc, wr[:, :, 0:4], A["moe_w_rg_2"][layer].rearrange("(t p) m -> p t m", p=P))
                    sp.dma(d_bc, wr[:, :, 4:36], A["moe_w_re_2"][layer].rearrange("(t p) m -> p t m", p=P))
                sp.dma(d_bc, br[:, 0:4], bcast(A["moe_b_rg_2"][layer], 4))
                sp.dma(d_bc, br[:, 4:36], bcast(A["moe_b_re_2"][layer], 32))
                sp.dma(d_bc, io[:], A["c_iota32"])
                sp.dma(d_bc, tri[:], A["c_before"])
                sp.dma(d_bc, ids[:], A["c_token_ids"])
                t = sp.dma(d_bc, table[layer].rearrange("(p b) a -> p (b a)", p=P), A["c_zero_table"])
                for e in (pe, dve, pool):
                    e.wait(t)
                for n in range(n_t):
                    t = mm_acc(PS[:, 0, n * 36:(n + 1) * 36], [(hT[:, k, n * P:(n + 1) * P], wr[:, k, :]) for k in range(KT)])
                d = lambda *a, **k: dve(*a, after=[last_dve()], **k)

                def last_dve():
                    return Token(dve.ctr, None, 0, dve.ctr.count)

                def bc(ap, shape):
                    return ap[:].to_broadcast(shape)

                def tile(name, w, dt=F32):
                    return sb(s, "r_" + name, [P, n_t, w], dt)

                dve.wait(t)
                d(V.tensor_tensor, L[:, 0:n_t, :], PS[:, 0, 0:36 * n_t].rearrange("p (n m) -> p n m", m=36),
                  bc(br[:].unsqueeze(1), [P, n_t, 36]), ALU.add)
                lg, le = L[:, 0:n_t, 0:4], L[:, 0:n_t, 4:36]

                def first_max(src, w, mx, oh, cand):
                    d(V.tensor_reduce, mx[:, :, 0], src, AX, ALU.max)
                    d(V.tensor_tensor, cand, src, bc(mx, [P, n_t, w]), ALU.is_equal)
                    d(V.tensor_scalar, cand, cand, -1000.0, None, ALU.mult)
                    d(V.tensor_tensor, cand, cand, bc(io[:, 0:w].unsqueeze(1), [P, n_t, w]), ALU.add)
                    d(V.tensor_reduce, red[:, :, 0], cand, AX, ALU.min)
                    d(V.tensor_tensor, oh, cand, bc(red, [P, n_t, w]), ALU.is_equal)

                red, m0, m1, m2 = tile("red", 1), tile("m0", 1), tile("m1", 1), tile("m2", 1)
                oh4, c4, c32 = tile("oh4", 4), tile("c4", 4), tile("c32", 32)
                O = [tile("o1", 32), tile("o2", 32)]
                first_max(lg, 4, m0, oh4[:], c4[:])
                d(V.tensor_tensor, c4[:], lg, bc(m0, [P, n_t, 4]), ALU.subtract)
                t = act(S.activation, c4[:], c4[:], ACT.Exp, after=[last_dve()])
                dve.wait(t)
                pg = tile("pg", 1)
                d(V.tensor_reduce, pg[:, :, 0], c4[:], AX, ALU.add)
                d(V.reciprocal, pg[:], pg[:])
                d(V.tensor_scalar, oh4[:], oh4[:], -NEG, NEG, ALU.mult, ALU.add)
                for n in range(n_t):
                    d(V.tensor_tensor, L[:, n, 4:36].rearrange("p (g e) -> p g e", g=4),
                      L[:, n, 4:36].rearrange("p (g e) -> p g e", g=4),
                      bc(oh4[:, n, :].unsqueeze(2), [P, 4, 8]), ALU.add)
                first_max(le, 32, m1, O[0][:], c32[:])
                d(V.scalar_tensor_tensor, le, O[0][:], 3 * NEG, le, ALU.mult, ALU.add)
                first_max(le, 32, m2, O[1][:], c32[:])
                e2 = tile("e2", 1)
                d(V.tensor_tensor, e2[:], m2[:], m1[:], ALU.subtract)
                t = act(S.activation, e2[:], e2[:], ACT.Exp, after=[last_dve()])
                dve.wait(t)
                d(V.tensor_scalar, m0[:], e2[:], 1.0, None, ALU.add)
                d(V.reciprocal, m0[:], m0[:])
                d(V.tensor_tensor, wts[:, 0, 0:n_t], m0[:, :, 0], pg[:, :, 0], ALU.mult)
                d(V.tensor_tensor, wts[:, 1, 0:n_t], wts[:, 0, 0:n_t], e2[:, :, 0], ALU.mult)
                C = tile("C", 32)
                t = d(V.tensor_tensor, C[:], O[0][:], O[1][:], ALU.add)
                pe.wait(t)
                for n in range(n_t):
                    mm_acc(PS[:, 1, n * 32:(n + 1) * 32],
                           [(tri[:], C[:, n, :])] + [(ones[:], C[:, m, :]) for m in range(n)], sig=False)
                t = mm_acc(PS[:, 2, 0:32], [(ones[:], C[:, m, :]) for m in range(n_t)])
                dve.wait(t)
                R = tile("R", 32)
                d(V.tensor_copy, R[:], PS[:, 1, 0:32 * n_t].rearrange("p (n m) -> p n m", m=32))
                cnt, nov, oend, ost = (sb(s, f"r_{n}", [P, 32]) for n in ("cnt", "nov", "oend", "ost"))
                d(V.tensor_copy, cnt[:], PS[:, 2, 0:32])
                d(V.tensor_scalar, nov[:], cnt[:], float(P), None, ALU.is_gt)
                for j in range(2, MAXJ + 1):
                    d(V.scalar_tensor_tensor, nov[:], cnt[:], float(P * j), nov[:], ALU.is_gt, ALU.add)
                d(V.tensor_tensor_scan, oend[:], ones[:, 0:32], nov[:], 0.0, ALU.mult, ALU.add)
                d(V.tensor_tensor, ost[:], oend[:], nov[:], ALU.subtract)
                d(V.tensor_copy, n_ov[:], oend[:, 31:32])
                oe = sb(s, "r_oe", [P, 16])
                for b in range(NBLK - NEXP):
                    d(V.tensor_scalar, cnt[:], oend[:], float(b), None, ALU.is_le)
                    d(V.tensor_reduce, oe[:, b:b + 1], cnt[:], AX, ALU.add)
                d(V.tensor_scalar, oe[:, 0:NBLK - NEXP], oe[:, 0:NBLK - NEXP], float(NEXP - 1), None, ALU.min)
                d(V.tensor_copy, ov_e[:, 0:NBLK - NEXP], oe[:, 0:NBLK - NEXP])
                rk, ee, oo, jj, bb, pos = (tile(x, 1) for x in ("rk", "ee", "oo", "jj", "bb", "pos"))
                posu = [tile("pu0", 1, U32), tile("pu1", 1, U32)]
                for c in range(2):
                    for dst, src in ((rk, R[:]), (ee, bc(io[:].unsqueeze(1), [P, n_t, 32])),
                                     (oo, bc(ost[:].unsqueeze(1), [P, n_t, 32]))):
                        d(V.tensor_tensor, c32[:], O[c][:], src, ALU.mult)
                        d(V.tensor_reduce, dst[:, :, 0], c32[:], AX, ALU.add)
                    d(V.tensor_scalar, jj[:], rk[:], float(P), None, ALU.is_ge)
                    for j in range(2, MAXJ + 1):
                        d(V.scalar_tensor_tensor, jj[:], rk[:], float(P * j), jj[:], ALU.is_ge, ALU.add)
                    d(V.tensor_tensor, bb[:], oo[:], jj[:], ALU.add)
                    d(V.tensor_tensor, bb[:], bb[:], ee[:], ALU.subtract)
                    d(V.tensor_scalar, bb[:], bb[:], float(NEXP - 1), None, ALU.add)
                    d(V.tensor_scalar, pos[:], jj[:], 0.0, None, ALU.is_gt)
                    d(V.tensor_tensor, bb[:], bb[:], pos[:], ALU.mult)
                    d(V.tensor_tensor, bb[:], bb[:], ee[:], ALU.add)
                    d(V.scalar_tensor_tensor, rk[:], jj[:], -float(P), rk[:], ALU.mult, ALU.add)
                    d(V.scalar_tensor_tensor, pos[:], bb[:], float(P), rk[:], ALU.mult, ALU.add)
                    d(V.tensor_copy, rows[:, c, 0:n_t], pos[:, :, 0])
                    d(V.scalar_tensor_tensor, pos[:], rk[:], float(NBLK), bb[:], ALU.mult, ALU.add)
                    t = d(V.tensor_copy, posu[c][:], pos[:])
                pool.wait(t)
                for c in range(2):
                    for n in range(n_t):
                        t = d_idx.counted(G.indirect_dma_start(
                            table[layer], bass.IndirectOffsetOnAxis(ap=posu[c][:, n, :], axis=0),
                            ids[:, n:n + 1], None))
                sp.dma(d_bc, idx[:], table[layer].rearrange("(p b) a -> p (b a)", p=P), after=[t])
                p.barrier()

        def expert_buffers(st, layer):
            E = {"dram": [A[f"moe_w_{n}_2"][layer] for n in ("gate", "up", "down")]}
            shapes = ([P, KT, DEXP], [P, KT, DEXP], [P, DEXP // P, D])
            E["W"] = [[sb(st, f"W{w}{n}", shapes[w]) for n in range(2)] for w in range(3)]
            E["sW"] = [[Slot(p, f"W{w}{n}") for n in range(2)] for w in range(3)]
            E["ic"] = [sb(st, f"e_ic{j}", [P, 1], U32) for j in range(2)]
            E["aT"] = [sb(st, "e_aT", [P, DEXP])]
            E["xe"], E["y"] = [OT[:, j, :] for j in range(2)], [OT[:, 2 + j, :] for j in range(2)]
            E["xT"] = [OT[:, 4, :].rearrange("p (k c) -> p k c", k=KT)]
            E["sg"] = [OT[:, 5, j * DEXP:(j + 1) * DEXP] for j in range(2)]
            for name in ("ic", "aT", "xe", "y", "xT", "sg"):
                E["s" + name] = [Slot(p, f"e_{name}{j}") for j in range(len(E[name]))]
            return E

        def load(E, w, e, n, stream=None):
            sp.take(E["sW"][w][n])
            renew(E["sW"][w][n])
            order = "a (p t) m -> p (a t) m" if w < 2 else "a (t p) m -> p (a t) m"
            E["sW"][w][n].put(sp.dma(stream or d_e[w][n], E["W"][w][n][:],
                                     E["dram"][w][bass.ds(e, 1)].rearrange(order, p=P)))

        def fetch(E, block, n, idx, stream=None):
            dve.take(E["sic"][n])
            renew(E["sic"][n])
            t = dve(V.tensor_copy, E["ic"][n][:], idx[:, bass.ds(block, 1)])
            E["sic"][n].put(t)
            pool.take(E["sxe"][n])
            renew(E["sxe"][n])
            pool.wait(t)
            E["sxe"][n].put((stream or d_x[n]).counted(G.indirect_dma_start(
                E["xe"][n], None, h_dram, bass.IndirectOffsetOnAxis(ap=E["ic"][n][:, 0:1], axis=0))))

        def up_half(E, n, then=None):
            xe, sxe, xT, sxT = E["xe"][n], E["sxe"][n], E["xT"][0], E["sxT"][0]
            sg, ssg = E["sg"][n], E["ssg"][n]
            then = then or (lambda what: None)
            pe.need(sxe)
            act.take(sxT)
            dve.take(sxT)
            renew(sxT)
            x3 = xe.rearrange("s (p t) -> s p t", t=KT)
            for b in range(2):
                pe.take(B[b])
                renew(B[b])
                for j in range(4):
                    t = pe(T.transpose, PS[:, b, j * P:(j + 1) * P], x3[:, :, 4 * b + j], ident[:], sig=(j == 3))
                sxe.got(t)
                E["sic"][n].got(t)
                ev, cp = (act, S.copy) if b else (dve, V.tensor_copy)
                t = ev(cp, xT[:, 4 * b:4 * b + 4, :], PS[:, b, :].rearrange("p (j c) -> p j c", j=4), after=[t])
                B[b].got(t)
                sxT.put(t)
            then("rows")
            bg, bu = 2 + 2 * n, 3 + 2 * n
            pe.need(sxT)
            toks = []
            for w, b in ((0, bg), (1, bu)):
                pe.need(E["sW"][w][n])
                pe.take(B[b])
                renew(B[b])
                t = mm_acc(PS[:, b, :], [(xT[:, k, :], E["W"][w][n][:, k, :]) for k in range(KT)])
                B[b].put(t)
                E["sW"][w][n].got(t)
                toks.append(t)
                then(w)
            sxT.got(t)
            act.take(ssg)
            renew(ssg)
            t = act(S.activation, sg, PS[:, bg, :], ACT.Exp, scale=-1.0, after=[toks[0]])
            t = dve(V.tensor_scalar, sg, sg, 1.0, None, ALU.add, after=[t])
            t = dve(V.reciprocal, sg, sg, after=[t])
            t = dve(V.tensor_tensor, sg, sg, PS[:, bg, :], ALU.mult, after=[t])
            B[bg].got(t)
            t = dve(V.tensor_tensor, sg, sg, PS[:, bu, :], ALU.mult, after=[t, toks[1]])
            B[bu].got(t)
            ssg.put(t)

        def down_half(E, n, block, then=None, stream=None):
            sg, ssg, aT, saT = E["sg"][n], E["ssg"][n], E["aT"][0], E["saT"][0]
            y, sy = E["y"][n], E["sy"][n]
            pe.need(ssg)
            pe.take(B[0])
            renew(B[0])
            for j in range(4):
                t = pe(T.transpose, PS[:, 0, j * P:(j + 1) * P], sg[:, j * P:(j + 1) * P], ident[:], sig=(j == 3))
            ssg.got(t)
            act.take(saT)
            renew(saT)
            t = act(S.copy, aT[:], PS[:, 0, :], after=[t])
            B[0].got(t)
            saT.put(t)
            pe.wait(t)
            pe.need(E["sW"][2][n])
            pe.take(B[6], B[7])
            renew(B[6], B[7])
            act.take(sy)
            dve.take(sy)
            renew(sy)
            for c in range(2):
                t = mm_acc(PS[:, 6 + c, :], [(aT[:, j * P:(j + 1) * P],
                                              E["W"][2][n][:, j, c * 512:c * 512 + 512]) for j in range(4)])
                B[6 + c].put(t)
                ev, cp = (act, S.copy) if c else (dve, V.tensor_copy)
                a = ev(cp, y[:, c * 512:c * 512 + 512], PS[:, 6 + c, :], after=[t])
                B[6 + c].got(a)
                sy.put(a)
            saT.got(t)
            E["sW"][2][n].got(t)
            if then:
                then(2)
            sp.need(sy)
            sy.got(sp.dma(stream or d_y[n], y_dram[bass.ds(block * P, P), :], y))

        def experts(E, layer, idx, n_ov, ov_e):
            def step(e, first=False, more=True, n=None):
                n = e % 2 if n is None else n

                def then(what):
                    if what == "rows":
                        if more:
                            fetch(E, e + 2, n, idx)
                    elif more:
                        load(E, what, e + 2, n)
                up_half(E, n, then)
                if not first:
                    down_half(E, 1 - n, e - 1, lambda w: load(E, w, e + 1, 1 - n))

            for e in range(2):
                fetch(E, e, e, idx)
            step(0, first=True)
            rounds = (NEXP - 4) // 2
            with p.repeat(f"experts{layer}", rounds) as i:
                step(i * 2 + 1, n=1)
                step(i * 2 + 2, n=0)
            step(NEXP - 3)
            up_half(E, 0)
            down_half(E, 1, NEXP - 3, lambda w: load(E, w, NEXP - 1, 1))
            up_half(E, 1)
            down_half(E, 0, NEXP - 2)
            down_half(E, 1, NEXP - 1)
            p.barrier(ahead=True)
            gathers, weights, stores = d_over[layer]
            count = nc.values_load(n_ov[0:1, 0:1], min_val=0, max_val=NBLK - NEXP)
            with p.own_counters(f"over{layer}"):
                with p.repeat(f"overflow{layer}", NBLK - NEXP) as i:
                    with p.while_rounds_left(count > i):
                        e = nc.values_load(ov_e[0:1, bass.ds(i, 1)], engines=(mybir.EngineType.SP,),
                                           min_val=0, max_val=NEXP - 1)
                        for w in range(3):
                            load(E, w, e, 0, weights)
                        fetch(E, i + NEXP, 0, idx, gathers)
                        up_half(E, 0)
                        down_half(E, 0, i + NEXP, stream=stores)

        moe(0, list(range(NT)))

        modulated_T(1, 0, A["norm_mix_2"][1], range(NT))
        w_na = A["na_w_in_2"][0]
        with ExitStack() as st:
            NH, NR = 16, 15
            bias_t = sb(st, "bias", [P, NH, NR, 64])
            with ExitStack() as s:
                pick = sb(s, "pick", [64, 64 * P])
                rp = sb(s, "rp", [P, 2, 32])
                rT = sb(s, "rT", [64, NH * NR])
                sp.dma(d_bc, pick[:], A["c_na_pick"])
                half = NH * NR // 2
                t = dve(V.memset, rp[:], NEG)
                sp.wait(t)
                flat = A["na_rpb_2"][0].rearrange("h r c -> (h r) c")
                for j in range(2):
                    t = sp.dma(d_bc, rp[0:half, j, 0:31], flat[j * half:(j + 1) * half, :])
                pe.wait(t)
                for j in range(2):
                    t = pe(T.transpose, PS[0:32, 0, j * half:(j + 1) * half], rp[0:half, j, :], ident[0:half, 0:half])
                t = act(S.copy, rT[0:32, :], PS[0:32, 0, 0:2 * half], after=[t])
                t0 = dve(V.memset, rT[32:64, :], 0.0)
                r3 = rT[:].rearrange("x (h r) -> x h r", h=NH)
                t = sp.dma(d_bc, r3[32:64, :, 1:NR], r3[0:32, :, 0:NR - 1], after=[t, t0])
                pe.wait(t)
                s_b = Slot(p, "bias_fill")
                for kc in range(64):
                    b = kc % 8
                    if kc:
                        pe.take(B[b])
                    renew(B[b])
                    t = mm_acc(PS[:, b, 0:NH * NR], [(pick[:, kc * P:(kc + 1) * P], rT[:])])
                    ev, cp = (dve, V.tensor_copy) if kc % 2 else (act, S.copy)
                    t = ev(cp, bias_t[:, :, :, kc], PS[:, b, 0:NH * NR].rearrange("p (h r) -> p h r", h=NH), after=[t])
                    B[b].got(t)
                p.barrier()
            ws = [sb(st, f"ws{n}", [P, KT, 3, P]) for n in range(2)]
            s_ws = [Slot(p, f"ws{n}") for n in range(2)]
            qT = sb(st, "nqT", [P, ALLT])
            kz = sb(st, "nkz", [P, 2, ALLT])
            vv = sb(st, "nv", [P, NT, P])
            s_q, s_k, s_v = Slot(p, "nq"), Slot(p, "nk"), Slot(p, "nv")
            bufs = softmax_bufs(st, ALLT)
            dve(V.memset, kz[:], 0.0)
            with p.repeat("neighbours", NH // 4) as i:
                for w in range(2):
                    sp.take(s_ws[w])
                    renew(s_ws[w])
                    for j in range(3):
                        t = sp.dma(d_w[w], ws[w][:, :, j, :], w_cols(w_na, i * (2 * P) + (w * P + j * D), P))
                    s_ws[w].put(t)
                for w in range(2):
                    pe.need(s_ws[w])
                    pe.take(B[0])
                    renew(B[0])
                    t = mm_acc(PS[:, 0, :], [(ws[w][:, k, 0, :], hT[:, k, CTX:ALLT]) for k in range(KT)])
                    act.take(s_q)
                    renew(s_q)
                    t = act(S.activation, qT[:, CTX:ALLT], PS[:, 0, :], ACT.Copy, scale=64 ** -0.5, after=[t])
                    B[0].got(t)
                    s_q.put(t)
                    act.take(s_k)
                    dve.take(s_k)
                    renew(s_k)
                    for (a, z), b in zip(spans(), (1, 2)):
                        pe.take(B[b])
                        renew(B[b])
                        t = mm_acc(PS[:, b, 0:z - a], [(ws[w][:, k, 1, :], hT[:, k, a:z]) for k in range(KT)])
                        t1 = dve(V.tensor_copy, kz[0:64, 0, a:z], PS[0:64, b, 0:z - a], after=[t])
                        t2 = act(S.copy, kz[64:P, 1, a:z], PS[64:P, b, 0:z - a], after=[t])
                        B[b].got(t1, t2)
                        s_k.put(t1, t2)
                    act.take(s_v)
                    renew(s_v)
                    for g0 in range(0, NT, 3):
                        b = 3 if g0 else 7
                        pe.take(B[b])
                        renew(B[b])
                        for n in range(3):
                            tn = g0 + n
                            t = mm_acc(PS[:, b, n * P:(n + 1) * P],
                                       [(hT[:, k, tn * P:(tn + 1) * P], ws[w][:, k, 2, :]) for k in range(KT)])
                        s_ws[w].got(t)
                        t = act(S.copy, vv[:, g0:g0 + 3, :].rearrange("p a b -> p (a b)"), PS[:, b, 0:3 * P], after=[t])
                        B[b].got(t)
                        s_v.put(t)
                    pe.need(s_q, s_k, s_v)
                    units = []
                    for hh in range(2):
                        for n in range(LT):
                            def scores(o, n=n, hh=hh):
                                q = qT[:, CTX + n * P:CTX + (n + 1) * P]
                                pe(T.matmul, o[:, 0:SEQ], q, kz[:, hh, CTX:ALLT], start=True, stop=True, sig=False)
                                return pe(T.matmul, o[:, SEQ:ALLT], q, kz[:, hh, 0:CTX], start=True, stop=True)

                            def bias(src, dst, toks, n=n, hh=hh):
                                b4 = bias_t[:].rearrange("p h r c -> p h (r c)")[
                                    :, bass.ds(i * 4 + (2 * w + hh), 1), (7 - 2 * n) * 64:(15 - 2 * n) * 64]
                                return [dve(V.tensor_tensor, src[:, 0:SEQ].unsqueeze(1), src[:, 0:SEQ].unsqueeze(1),
                                            b4, ALU.add, after=toks)]

                            units.append(dict(
                                n=ALLT, scale=1.0, in_place=True, scores=scores, bias=bias,
                                v=lambda j, hh=hh: vv[:, (j + CT) % NT, hh * 64:hh * 64 + 64],
                                out=OT[:, CT + n, bass.ds(i * (2 * P) + (w * P + hh * 64), 64)]))
                    attend(units, bufs, [[0, 1], [2, 3]], [4, 5], 6, 64)
                    for s in (s_q, s_k, s_v):
                        s.got(*B[6].fill)
        with ExitStack() as st:
            rg = row_gates(st, 1, 0, False)
            gate_and_project(st, A["na_w_out_2"][0], None, list(range(CT, NT)), rg)
        moe(1, list(range(CT, NT)))

        with ExitStack() as st:
            norm_rows(st, A["norm_final_2"], range(CT, NT), lambda tl: OT[:, tl, :])
            t = sp.dma(d_st, out[0].rearrange("(t p) d -> p t d", p=P), OT[:, CT:, :])
            sp.wait(t)
            sp.wait(*p.everything())
        return p.found


_NAMES = ["x", "mem", "mem_norm_w", "norm_w", "w_memkv", "w_out", "w_in_a", "w_gate_up", "b_gate", "gla_norm_w",
          "w_in_b", "final_norm_w", "c_2", "ctx_2", "c_ctx_2", "w_ada_2", "b_ada_2", "norm_mix_2", "norm_ffn_2",
          "norm_final_2", "ab_w_in_2", "ab_w_out_2", "mla_q_norm_2", "mla_w_q_up_2", "mla_kv_norm_2",
          "mla_w_kv_up_2", "gqa_q_norm_2", "gqa_k_norm_2", "na_w_in_2", "na_w_out_2", "na_rpb_2", "moe_w_rg_2",
          "moe_b_rg_2", "moe_w_re_2", "moe_b_re_2", "moe_w_gate_2", "moe_w_up_2", "moe_w_down_2"]


def kernel(**inputs):
    import concourse.bacc as _bacc
    from concourse.bass_utils import run_bass_kernel_spmd as _run

    arrays = {f"in_{n}": np.ascontiguousarray(inputs[n]) for n in _NAMES}
    arrays.update({f"in_c_{n}": a for n, a in shape_constants().items()})

    def assemble(plan):
        nc = _bacc.Bacc("TRN2", target_bir_lowering=False, num_devices=1)
        aps = {n[3:]: nc.dram_tensor(n, a.shape, mybir.dt.from_np(a.dtype), kind="ExternalInput").ap()
               for n, a in arrays.items()}
        out = nc.dram_tensor("out", (1, SEQ, D), F32, kind="ExternalOutput").ap()
        return nc, build(nc, aps, out, plan)

    _, plan = assemble(None)
    nc, _ = assemble(plan)
    r = _run(nc, [arrays], core_ids=[0])
    return r.results[0]["out"]
```

```python
from contextlib import ExitStack, contextmanager

import numpy as np
import concourse.bass as bass
from concourse import mybir

F32 = mybir.dt.float32
U32 = mybir.dt.uint32
ALU = mybir.AluOpType
ACT = mybir.ActivationFunctionType
AX = mybir.AxisListType.X

P = 128
D = 1024
KT = D // P
SEQ, CTX, NMEM = 512, 256, 256
LT, CT = SEQ // P, CTX // P
ALLT = SEQ + CTX
NT = LT + CT
EPS = 1e-6
NEG = -1.0e30
NEXP, DEXP = 32, 512
MAXJ = ALLT // P - 1
NBLK = NEXP + 2 * ALLT // P - 1
NSPAN = 384




class Token:
    def __init__(self, ctr, loop, shift, off):
        self.ctr, self.loop, self.shift, self.off = ctr, loop, shift, off

    def total(self):
        if self.loop is None:
            return self.off
        lp = self.loop
        return lp.base[self.ctr] + (lp.n - 1 + self.shift) * lp.rate.get(self.ctr.name, 0) + self.off


class Counter:
    def __init__(self, prog, name, unit, by_pool=False, prefix=False, ahead=False):
        self.prog, self.name, self.unit, self.by_pool, self.prefix = prog, name, unit, by_pool, prefix
        self.ahead = ahead
        self.sem = prog.ctx.enter_context(prog.nc.semaphore("s_" + name))
        self.count = 0
        self.local = 0
        prog.counters.append(self)

    def counted(self, ins):
        ins.then_inc(self.sem, self.unit)
        if self.prog.loop is None:
            self.count += 1
            return Token(self, None, 0, self.count)
        self.local += 1
        return Token(self, self.prog.loop, 0, self.local)


class Slot:

    def __init__(self, prog, name, ap=None):
        self.name, self.ap, self.fill, self.free = f"{name}.{len(prog.slots)}", ap, [], []
        prog.slots.append(self)

    def put(self, *toks):
        self.fill += toks

    def got(self, *toks):
        self.free += toks


class Loop:
    def __init__(self, name, n, i, base, rate):
        self.name, self.n, self.i, self.base, self.rate = name, n, i, base, rate


class Engine:
    def __init__(self, prog, name, eng, anchor=False):
        self.prog, self.name, self.eng = prog, name, eng
        self.ctr = Counter(prog, name, 1)
        self.seen = {}
        self.anchor = prog.ctx.enter_context(prog.nc.semaphore(f"s_{name}_anchor")) if anchor else None

    def wait(self, *toks):
        for t in toks:
            if t is None:
                continue
            lp = self.prog.loop
            if t.loop is not lp or lp is None:
                if lp is not None:
                    continue
                v = t.total()
                if self.seen.get(t.ctr, (0, 0))[1] >= v:
                    continue
                self.seen[t.ctr] = (0, v)
                self.eng.wait_ge(t.ctr.sem, v * t.ctr.unit)
                continue
            key = (t.shift, t.off)
            if self.seen.get(t.ctr, (-9, 0)) >= key:
                continue
            self.seen[t.ctr] = key
            r = lp.rate.get(t.ctr.name, 0)
            const = (lp.base[t.ctr] + t.shift * r + t.off) * t.ctr.unit
            assert self.prog.plan is None or const > 0, (t.ctr.name, const)
            self.eng.wait_ge(t.ctr.sem, lp.i * (r * t.ctr.unit) + const if r else max(const, 1))
            if self.anchor is not None:
                self.eng.sem_inc(self.anchor, 1)

    def take(self, *slots):
        for s in slots:
            self.wait(*(s.free or s.fill))

    def need(self, *slots):
        for s in slots:
            self.wait(*s.fill)

    def __call__(self, method, *args, after=(), sig=True, **kw):
        self.wait(*after)
        ins = method(*args, **kw)
        return self.ctr.counted(ins) if sig else None

    def dma(self, stream, out, in_, after=()):
        self.wait(*after)
        return stream.counted(self.eng.dma_start(out, in_))


def renew(*slots):
    for s in slots:
        s.fill, s.free = [], []


class Prog:
    def __init__(self, nc, ctx, plan):
        self.nc, self.ctx, self.plan, self.found = nc, ctx, plan, {}
        self.counters, self.slots, self.loop = [], [], None
        self.round_end = ctx.enter_context(nc.semaphore("s_round_end"))
        self.pe = Engine(self, "pe", nc.tensor)
        self.act = Engine(self, "act", nc.scalar)
        self.dve = Engine(self, "dve", nc.vector)
        self.pool = Engine(self, "pool", nc.gpsimd, anchor=True)
        self.sp = Engine(self, "sp", nc.sync, anchor=True)
        self.engines = [self.pe, self.act, self.dve, self.pool, self.sp]

    def everything(self, ahead=True):
        return [Token(c, None, 0, c.count) for c in self.counters
                if c.count and not c.prefix and (ahead or not c.ahead)]

    def barrier(self, ahead=False):
        for e in self.engines:
            e.wait(*self.everything(ahead))


    @contextmanager
    def repeat(self, name, n):
        plan = (self.plan or {}).get(name, {"rate": {}, "slots": {}})
        rate = plan["rate"]
        self.sp.wait(*self.everything())
        for c in self.counters:
            lack = rate.get(c.name, 0) - c.count
            if lack > 0 and not c.by_pool:
                self.nc.sync.sem_inc(c.sem, lack * c.unit)
                c.count += lack
        self.barrier()
        byname = {c.name: c for c in self.counters}
        with self.nc.Fori(0, n) as i:
            lp = self.loop = Loop(name, n, i, {c: c.count for c in self.counters}, rate)
            for c in self.counters:
                c.local = 0
            for e in self.engines:
                e.seen = {}
            for s in self.slots:
                fill, free = plan["slots"].get(s.name, ([], []))
                s.fill = [Token(byname[c], lp, -1, o) for c, o in fill]
                s.free = [Token(byname[c], lp, -1, o) for c, o in free]
            yield i

            def left(toks):
                return [(t.ctr.name, t.off) for t in toks if t.loop is lp and t.shift == 0]
            self.found[name] = {"rate": {c.name: c.local for c in self.counters if c.local},
                                "slots": {s.name: (left(s.fill), left(s.free)) for s in self.slots}}
            if self.plan is not None:
                assert self.found[name]["rate"] == rate, (name, rate, self.found[name]["rate"])
        self.loop = None
        for e in self.engines:
            e.seen = {}
        for c in self.counters:
            c.count += n * rate.get(c.name, c.local)
            c.local = 0
        for s in self.slots:
            s.fill = [Token(t.ctr, None, 0, t.ctr.count) for t in s.fill if t.ctr.ahead]
            s.free = []
        self.barrier()

    @contextmanager
    def while_rounds_left(self, cond):
        with self.nc.If(cond):
            yield
            for e in self.engines:
                e.wait(*[Token(c, self.loop, 0, c.local) for c in self.counters if c.local])
                e.eng.sem_inc(self.round_end, 1)

    @contextmanager
    def own_counters(self, name):
        usual = [e.ctr for e in self.engines]
        for e in self.engines[:4]:
            e.ctr = Counter(self, f"{e.name}_{name}", 1, prefix=True)
        yield
        for e, c in zip(self.engines, usual):
            e.ctr = c
            c.count += 1
            e.eng.sem_inc(c.sem, 1)
        self.barrier()


def shape_constants():
    c = {}
    r = np.arange(P)
    q, k = r[:, None], r[None, :]
    c["ident"] = np.eye(P, dtype=np.float32)
    c["gla_mask"] = ((q // 64 == k // 64) & (q <= k)).astype(np.float32)
    c["chunk_reset"] = np.broadcast_to((np.arange(SEQ) % 64 != 0).astype(np.float32), (96, SEQ)).copy()
    neg = np.float32(NEG)

    def block(ok):
        return np.where(ok, np.float32(0), neg).astype(np.float32)
    blocks = [block(k >= q), block(k <= q)]
    for dil in (4, 16):
        same = (q - k) % dil == 0
        blocks += [block(same)] * (LT - 1) + [block(same & (k <= q))]
    c["dil_mask"] = np.concatenate(blocks, axis=1)
    half = 16
    inv = np.float32(500000.0) ** (-np.arange(half, dtype=np.float32) / np.float32(half))
    ang = inv[:, None].astype(np.float32) * np.arange(SEQ, dtype=np.float32)[None, :]
    c["dil_cos"] = np.concatenate([np.cos(ang)] * 2).astype(np.float32)
    c["dil_sin"] = np.concatenate([np.sin(ang)] * 2).astype(np.float32)
    rot = np.zeros((P, P), np.float32)
    for m in range(16):
        rot[m + 16, m], rot[m, m + 16] = -1, 1
    c["dil_rot"] = rot
    t = np.arange(SEQ)
    rows, cols = (t // 64).astype(np.float32), (t % 64).astype(np.float32)

    def axial(dim):
        n = dim // 4
        inv = np.float32(10000.0) ** (-np.arange(n, dtype=np.float32) / np.float32(n))
        ang = np.concatenate([inv[:, None] * rows, inv[:, None] * cols]).astype(np.float32)
        cos = np.ones((dim, ALLT), np.float32)
        sin = np.zeros((dim, ALLT), np.float32)
        cos[:, CTX:] = np.repeat(np.cos(ang), 2, axis=0)
        sin[:, CTX:] = np.repeat(np.sin(ang), 2, axis=0)
        return cos, sin
    cb, sb = axial(64)
    c["gqa_cos"], c["gqa_sin"] = np.concatenate([cb, cb]), np.concatenate([sb, sb])
    ca, sa = axial(32)
    c["mla_cos"], c["mla_sin"] = np.zeros((96, ALLT), np.float32), np.zeros((96, ALLT), np.float32)
    c["mla_cos"][64:], c["mla_sin"][64:] = ca, sa
    pair = np.zeros((P, P), np.float32)
    for m in range(0, P, 2):
        pair[m + 1, m], pair[m, m + 1] = -1, 1
    c["pair_rot"] = pair
    c["head_sum"] = (q // 64 == k // 64).astype(np.float32)
    pick = np.zeros((64, 64, P), np.float32)
    for kc in range(64):
        for cc in range(64):
            cs = min(max(cc - 8, 0), 48)
            for half_ in range(2):
                if cs <= kc < cs + 16:
                    pick[32 * half_ + kc - cc + 15, kc, 64 * half_ + cc] = 1
                else:
                    pick[32 * half_ + 31, kc, 64 * half_ + cc] = 1
    c["na_pick"] = pick.reshape(64, 64 * P)
    c["before"] = (q < k).astype(np.float32)
    c["iota32"] = np.broadcast_to(np.arange(32, dtype=np.float32), (P, 32)).copy()
    c["token_ids"] = (r[:, None] + P * np.arange(NT)[None, :]).astype(np.uint32)
    c["zero_table"] = np.zeros((P, NBLK), np.uint32)
    return c


def build(nc, A, out, plan):
    ctx = ExitStack()
    with ctx:
        p = Prog(nc, ctx, plan)
        pe, act, dve, pool, sp = p.pe, p.act, p.dve, p.pool, p.sp
        T, S, V, G = nc.tensor, nc.scalar, nc.vector, nc.gpsimd

        def ctr(name):
            return Counter(p, name, 16)

        uses = {}

        def ctr_ahead(name):
            return Counter(p, name, 16, ahead=True)

        def sb(stack, name, shape, dt=F32):
            uses[name] = uses.get(name, -1) + 1
            name = f"{name}_{uses[name]}" if uses[name] else name
            return stack.enter_context(nc.sbuf_tensor(name, shape, dt))

        PS = ctx.enter_context(nc.psum_tensor("PS", [P, 8, 512], F32))
        PF = PS[:, :, :].rearrange("p b c -> p (b c)")
        B = [Slot(p, f"bank{b}", PS[:, b, :]) for b in range(8)]

        d_const, d_w = ctr("d_const"), [ctr("d_w0"), ctr("d_w1")]
        d_bc, d_wo, d_st, d_g, d_ada = (ctr("d_bc"), ctr("d_wo"), ctr("d_st"), ctr("d_g"),
                                        [ctr_ahead("d_ada0"), ctr_ahead("d_ada1")])
        d_y, d_h = ([ctr(f"{n}{j}") for j in range(2)] for n in ("d_y", "d_h"))
        d_e = [[ctr_ahead(f"d_e{w}{j}") for j in range(2)] for w in ("g", "u", "d")]
        d_qkv = [ctr_ahead(f"d_qkv{j}") for j in range(3)]
        d_x, d_yg = ([Counter(p, f"{n}{j}", 16, by_pool=True, ahead=(n == "d_x")) for j in range(2)]
                     for n in ("d_x", "d_yg"))
        d_idx = Counter(p, "d_idx", 16, by_pool=True)
        d_over = [(Counter(p, f"d_xo{j}", 16, by_pool=True, prefix=True),
                   [Counter(p, f"d_eo{w}{j}", 16, prefix=True) for w in range(3)],
                   Counter(p, f"d_yo{j}", 16, prefix=True)) for j in range(2)]

        X = sb(ctx, "X", [P, NT, D])
        hT = sb(ctx, "hT", [P, KT, ALLT])
        OT = sb(ctx, "OT", [P, NT, D])
        s_hT = Slot(p, "hT")
        s_OT = Slot(p, "OT")
        s_X = [Slot(p, f"X{t}") for t in range(NT)]
        ident = sb(ctx, "ident", [P, P])
        ones = sb(ctx, "ones", [P, P])
        small = sb(ctx, "small", [P, 64])
        s_small = Slot(p, "small")
        hrow = [sb(ctx, f"hrow{n}", [P, D]) for n in range(2)]
        s_hrow = [Slot(p, f"hrow{n}") for n in range(2)]
        eps_c = sb(ctx, "eps_c", [P, 1])

        mods = nc.dram_tensor("mods", [2, 2, 6 * D], F32, kind="Internal").ap()
        h_dram = nc.dram_tensor("h_dram", [ALLT, D], F32, kind="Internal").ap()
        y_dram = nc.dram_tensor("y_dram", [NBLK * P, D], F32, kind="Internal").ap()
        table = [nc.dram_tensor(f"table{n}", [P * NBLK, 1], U32, kind="Internal").ap() for n in range(2)]

        def bcast(row_ap, n):
            return row_ap.rearrange("(a n) -> a n", a=1).to_broadcast([P, n])

        sp.dma(d_const, ident[:], A["c_ident"])
        sp.dma(d_const, X[:, CT:, :], A["x"][0].rearrange("(t p) d -> p t d", p=P))
        t = sp.dma(d_const, X[:, :CT, :], A["ctx_2"][0].rearrange("(t p) d -> p t d", p=P))
        t1 = dve(V.memset, ones[:], 1.0)
        t2 = dve(V.memset, eps_c[:], EPS)
        for s in s_X:
            s.put(t)
        consts_ready = [t, t1, t2]
        for e in (pe, act, dve, pool):
            e.wait(*consts_ready)

        t = dve(V.memset, hrow[0][:], 0.0)
        for b in range(NEXP, NBLK):
            tz = sp.dma(d_st, y_dram[b * P:(b + 1) * P, :], hrow[0][:], after=[t])
        s_hrow[0].got(tz)

        def rstd_of(sums, width, n, after, scratch):
            t = act(S.activation, scratch, sums, ACT.Ln, bias=eps_c[0:n, :], scale=1.0 / width, after=after)
            return act(S.activation, scratch, scratch, ACT.Exp, scale=-0.5, after=[t])

        def transpose_tile(src, k_tiles, dst_T, col, banks, src_fill, src_slot, dst_slot):
            for g0 in range(0, k_tiles, 4):
                b = banks[(g0 // 4) % len(banks)]
                pe.take(B[b])
                pe.wait(*src_fill)
                renew(B[b])
                for j in range(4):
                    tk = pe(T.transpose, PS[:, b, j * P:(j + 1) * P], src[:, (g0 + j) * P:(g0 + j + 1) * P],
                            ident[:], sig=(j == 3))
                B[b].put(tk)
                src_slot.got(tk)
                ev, cp = (act, S.copy) if (g0 // 4) % 2 else (dve, V.tensor_copy)
                tk = ev(cp, dst_T[:, g0:g0 + 4, col:col + P],
                        PS[:, b, :].rearrange("p (j c) -> p j c", j=4), after=[tk])
                B[b].got(tk)
                dst_slot.put(tk)

        def norm_to_T(tiles, gains, shifts, dst_T, dst_slot, cols, to_dram=None):
            n = len(tiles)
            act.take(s_small)
            for t in s_hrow:
                act.take(t)
            renew(s_small)
            for j, (x_ap, x_slot) in enumerate(tiles):
                act.need(x_slot)
                tk = act(S.activation, hrow[j % 2][:], x_ap, ACT.Square, accum_out=small[:, j:j + 1],
                         after=[tk] if j else [])
                x_slot.got(tk)
            tk = rstd_of(small[:, 0:n], D, P, [tk], small[:, 8:8 + n])
            for s in s_hrow:
                s.free = [tk]
                s.fill = []
            for e in (pe, act, dve):
                e.take(dst_slot)
            renew(dst_slot)
            for j, (x_ap, x_slot) in enumerate(tiles):
                s = s_hrow[j % 2]
                dve.take(s)
                renew(s)
                a = dve(V.scalar_tensor_tensor, hrow[j % 2][:], x_ap, small[:, 8 + j:9 + j], gains[j],
                        ALU.mult, ALU.mult, after=[tk])
                x_slot.got(a)
                if shifts is not None:
                    a = dve(V.tensor_tensor, hrow[j % 2][:], hrow[j % 2][:], shifts[j], ALU.add, after=[a])
                s.put(a)
                s_small.got(a)
                transpose_tile(hrow[j % 2], KT, dst_T, cols[j], [2 * (j % 2), 2 * (j % 2) + 1], [a], s, dst_slot)
                if to_dram is not None:
                    s.got(sp.dma(d_h[j % 2], to_dram[cols[j]:cols[j] + P, :], hrow[j % 2][:], after=[a]))
            return

        lat_tiles = [(X[:, t, :], s_X[t]) for t in range(CT, NT)]
        all_tiles = [(X[:, t, :], s_X[t]) for t in range(NT)]

        def w_cols(w, start, width):
            return w.rearrange("(t p) m -> p t m", p=P)[:, :, start] if width is None else \
                w.rearrange("(t p) m -> p t m", p=P)[:, :, bass.ds(start, width)]

        def mm_acc(out_ap, pairs, sig=True, start=True, stop=True, **kw):
            n = len(pairs)
            for j, (a, b) in enumerate(pairs):
                tk = pe(T.matmul, out_ap, a, b, start=start and j == 0, stop=stop and j == n - 1,
                        sig=sig and j == n - 1, **kw)
            return tk

        def softmax_bufs(stack, cols, n_p=3):
            bufs = {"n_p": n_p}
            bufs["P"] = [sb(stack, f"P{j}", [P, cols]) for j in range(n_p)]
            bufs["PT"] = [sb(stack, f"PT{j}", [P, cols]) for j in range(2)]
            bufs["st"] = [sb(stack, f"st{j}", [P, 4]) for j in range(4)]
            bufs["sP"] = [Slot(p, f"{cols}P{j}") for j in range(n_p)]
            bufs["sPT"] = [Slot(p, f"{cols}PT{j}") for j in range(2)]
            bufs["sst"] = [Slot(p, f"{cols}st{j}") for j in range(4)]
            return bufs

        def stages(bufs, s_banks, pt_banks, o_bank, dv):
            def score(u, x):
                banks = [B[b] for b in s_banks[x % len(s_banks)]]
                b0 = s_banks[x % len(s_banks)][0]
                src = PF[:, b0 * 512:b0 * 512 + u["n"]]
                pe.take(*banks)
                renew(*banks)
                tk = scored = u["scores"](src)
                for b in banks:
                    b.put(tk)
                w, sP, sst, st = bufs["P"][x % bufs["n_p"]], bufs["sP"][x % bufs["n_p"]], bufs["sst"][x % 4], bufs["st"][x % 4]
                dve.take(sP, sst)
                act.take(sP)
                renew(sP, sst)
                if u.get("bias"):
                    toks = u["bias"](src, w, [tk])
                    for b in banks:
                        b.got(*toks)
                    src = src if u.get("in_place") else w[:, 0:u["n"]]
                else:
                    toks = [tk]
                tk = dve(V.reduce_max, st[:, 0:1], src, AX, after=toks)
                tk = dve(V.tensor_scalar, st[:, 1:2], st[:, 0:1], -u["scale"], None, ALU.mult, after=[tk])
                tk = act(S.activation, w[:, 0:u["n"]], src, ACT.Exp, bias=st[:, 1:2], scale=u["scale"],
                         accum_out=st[:, 2:3], after=[tk] + toks)
                for b in banks:
                    b.got(tk)
                sP.put(tk)
                return scored

            def turn(u, x):
                w, sP, wT, sPT = bufs["P"][x % bufs["n_p"]], bufs["sP"][x % bufs["n_p"]], bufs["PT"][x % 2], bufs["sPT"][x % 2]
                sst, st = bufs["sst"][x % 4], bufs["st"][x % 4]
                nb = u["n"] // P
                sst.put(dve(V.reciprocal, st[:, 3:4], st[:, 2:3], after=sP.fill))
                pe.need(sP)
                act.take(sPT)
                dve.take(sPT)
                renew(sPT)
                for g0 in range(0, nb, 4):
                    b = pt_banks[g0 // 4]
                    m = min(4, nb - g0)
                    pe.take(B[b])
                    renew(B[b])
                    for j in range(m):
                        tk = pe(T.transpose, PS[:, b, j * P:(j + 1) * P],
                                w[:, (g0 + j) * P:(g0 + j + 1) * P], ident[:], sig=(j == m - 1))
                    B[b].put(tk)
                    sP.got(tk)
                    ev, cp = (dve, V.tensor_copy) if g0 // 4 == 1 and nb < 7 else (act, S.copy)
                    tk = ev(cp, wT[:, g0 * P:(g0 + m) * P], PS[:, b, 0:m * P], after=[tk])
                    B[b].got(tk)
                    sPT.put(tk)

            def values(u, x):
                wT, sPT, sst, st = bufs["PT"][x % 2], bufs["sPT"][x % 2], bufs["sst"][x % 4], bufs["st"][x % 4]
                nb = u["n"] // P
                pe.need(sPT)
                pe.take(B[o_bank])
                renew(B[o_bank])
                tk = mm_acc(PS[:, o_bank, 0:dv], [(wT[:, j * P:(j + 1) * P], u["v"](j)) for j in range(nb)])
                B[o_bank].put(tk)
                sPT.got(tk)
                valued = tk
                act.need(sst)
                act.take(s_OT)
                tk = act(S.activation, u["out"], PS[:, o_bank, 0:dv], ACT.Copy, scale=st[:, 3:4], after=[tk])
                B[o_bank].got(tk)
                sst.got(tk)
                return valued

            return score, turn, values

        def attend(units, bufs, *banks_and_width):
            score, turn, values = stages(bufs, *banks_and_width)
            n = len(units)
            for x in range(n + 3):
                if x < n:
                    score(units[x], x)
                if 2 <= x < n + 2:
                    turn(units[x - 2], x - 2)
                if x >= 3:
                    values(units[x - 3], x - 3)

        def pipeline(name, n, depth, load, project, units, per_item, stage, beside=None,
                     turn_first=True):
            score, turn, values = stage
            for e in range(depth):
                load(e, e)
            for _, f in project(0, 0, depth):
                f()

            def positions(item, xs, ahead, last=4):
                got = {}

                def unit(x):
                    j = x // per_item
                    if j not in got:
                        got[j] = units(item(j), j % 2)
                    return got[j], got[j][0][x % per_item]
                steps = {j: project(item(j), j % 2, ahead(j)) for j in range(1, min(last, 4))}
                def score_at(x):
                    (_, reads, _), u = unit(x)
                    if x % per_item == 0:
                        pe.need(*reads)
                    t = score(u, x)
                    if (x + 1) % per_item == 0:
                        for s in reads:
                            s.got(t)

                def values_at(x):
                    (_, _, reads), u = unit(x)
                    if x % per_item == 0:
                        pe.need(*reads)
                    t = values(u, x)
                    if (x + 1) % per_item == 0:
                        for s in reads:
                            s.got(t)

                for x in xs:
                    here = []
                    if x + 3 < last * per_item:
                        here.append(lambda: score_at(x + 3))
                    if 0 <= x + 1 < last * per_item:
                        here.append(lambda: turn(unit(x + 1)[1], x + 1))
                        brief.append(here[-1])
                    if turn_first:
                        here.reverse()
                    if x >= 0:
                        here.append(lambda: values_at(x))
                    for j in sorted(steps):
                        here += [f for at, f in steps[j] if at == x - (j - 1) * per_item]
                    others = []
                    if beside is not None and x >= 0:
                        j = x // per_item
                        others = beside(item(j), x % per_item, x == last * per_item - 1)
                    long = [f not in brief for f in here]
                    for k, f in enumerate(here):
                        f()
                        if long[k]:
                            for _ in range(-(-len(others) // sum(long[k:]))):
                                others.pop(0)()

            positions(lambda j: j, range(-3, 0), lambda j: j + depth)
            with p.repeat(name, n // 2 - 1) as i:
                positions(lambda j: i * 2 + j, range(2 * per_item),
                          lambda j: (i * 2 + (j + depth)) % n if j + depth > 3 else i * 2 + (j + depth))
            positions(lambda j: n - 2 + j, range(2 * per_item), lambda j: None, last=2)
            p.barrier(ahead=True)

        brief = []

        def dealt(first, last, steps):
            return [(first + k * (last - first + 1) // len(steps), f) for k, f in enumerate(steps)]

        def gate_and_project(stack, layer_w_out, gate, tiles, row_gate=None):
            wo = sb(stack, "wo", [P, KT, D])
            s_wo = Slot(p, "wo")

            def load_w_out():
                s_wo.put(sp.dma(d_wo, wo[:], layer_w_out.rearrange("(t p) m -> p t m", p=P)))
            if gate is None:
                load_w_out()
            if gate is not None:
                w, off = gate
                wg = [sb(stack, f"wg{n}", [P, KT, 512]) for n in range(2)]
                s_wg = [Slot(p, f"wg{n}") for n in range(2)]
                sg = [sb(stack, f"sg{n}", [P, 512]) for n in range(2)]
                s_sg = [Slot(p, f"sg{n}") for n in range(2)]
                for c in range(2):
                    s_wg[c].put(sp.dma(d_w[c], wg[c][:], w_cols(w, off + 512 * c, 512)))
                load_w_out()
                x = 0
                for c in range(2):
                    for n, tl in enumerate(tiles):
                        b = 4 + x % 4
                        s = s_sg[x % 2]
                        v = sg[x % 2]
                        pe.take(B[b])
                        pe.need(s_wg[c])
                        renew(B[b])
                        tk = mm_acc(PS[:, b, :], [(hT[:, k, n * P:(n + 1) * P], wg[c][:, k, :]) for k in range(KT)])
                        B[b].put(tk)
                        s_hT.got(tk)
                        act.take(s)
                        renew(s)
                        tk = act(S.activation, v[:], PS[:, b, :], ACT.Exp, scale=-1.0, after=[tk])
                        tk = dve(V.tensor_scalar, v[:], v[:], 1.0, None, ALU.add, after=[tk])
                        tk = dve(V.reciprocal, v[:], v[:], after=[tk])
                        tk = dve(V.tensor_tensor, v[:], v[:], PS[:, b, :], ALU.mult, after=[tk])
                        B[b].got(tk)
                        tk = dve(V.tensor_tensor, OT[:, tl, 512 * c:512 * c + 512],
                                 OT[:, tl, 512 * c:512 * c + 512], v[:], ALU.mult, after=[tk])
                        s.got(tk)
                        s_OT.put(tk)
                        x += 1
            for e in (act, dve, pe):
                e.take(s_hT)
            renew(s_hT)
            for n, tl in enumerate(tiles):
                transpose_tile(OT[:, tl, :], KT, hT, n * P, [2 * (n % 2), 2 * (n % 2) + 1], s_OT.fill, s_OT, s_hT)
            tmp = sb(stack, "res_tmp", [P, 2, 512])
            s_tmp = [Slot(p, f"res_tmp{n}") for n in range(2)]
            pe.need(s_hT, s_wo)
            x = 0
            for n, tl in enumerate(tiles):
                for c in range(2):
                    b = 4 + x % 4
                    pe.take(B[b])
                    renew(B[b])
                    tk = mm_acc(PS[:, b, :], [(hT[:, k, n * P:(n + 1) * P], wo[:, k, 512 * c:512 * c + 512])
                                              for k in range(KT)])
                    B[b].put(tk)
                    s_hT.got(tk)
                    dve.take(s_X[tl])
                    xs = X[:, tl, 512 * c:512 * c + 512]
                    if row_gate is None:
                        tk = dve(V.tensor_tensor, xs, xs, PS[:, b, :], ALU.add, after=[tk])
                    else:
                        g = row_gate(tl)
                        dve.take(s_tmp[x % 2])
                        renew(s_tmp[x % 2])
                        tk = dve(V.tensor_tensor, tmp[:, x % 2, :], PS[:, b, :], g[:, 512 * c:512 * c + 512],
                                 ALU.mult, after=[tk])
                        B[b].got(tk)
                        tk = dve(V.tensor_tensor, xs, xs, tmp[:, x % 2, :], ALU.add, after=[tk])
                        s_tmp[x % 2].got(tk)
                    B[b].got(tk)
                    s_X[tl].put(tk)
                    x += 1
            s_OT.free, s_OT.fill = [], []
            p.barrier()

        cv = sb(ctx, "cv", [P, KT, 2])
        with ExitStack() as st:
            ce = sb(st, "ce", [P, KT, 2])
            with nc.allow_non_contiguous_dma("two vectors as columns"):
                sp.dma(d_bc, cv[:, :, 0], A["c_2"][0].rearrange("(t p) -> p t", p=P))
                t = sp.dma(d_bc, cv[:, :, 1], A["c_ctx_2"].rearrange("(t p) -> p t", p=P))
            t = act(S.activation, ce[:], cv[:], ACT.Exp, scale=-1.0, after=[t])
            t = dve(V.tensor_scalar, ce[:], ce[:], 1.0, None, ALU.add, after=[t])
            t = dve(V.reciprocal, ce[:], ce[:], after=[t])
            dve(V.tensor_tensor, cv[:], cv[:], ce[:], ALU.mult, after=[t])
            p.barrier()

        memx = ExitStack()
        memT = sb(memx, "memT", [P, KT, NMEM])
        s_memT = Slot(p, "memT")
        with ExitStack() as st:
            mem = sb(st, "mem", [P, NMEM // P, D])
            s_mem = Slot(p, "mem")
            gm = sb(st, "gm", [P, D])
            sp.dma(d_bc, mem[:], A["mem"][0].rearrange("(t p) d -> p t d", p=P))
            t = sp.dma(d_bc, gm[:], bcast(A["mem_norm_w"], D))
            s_mem.put(t)
            dve.wait(t)
            norm_to_T([(mem[:, n, :], s_mem) for n in range(2)], [gm[:]] * 2, None, memT, s_memT, [0, P])
            p.barrier()

        def first_norm(st, w):
            g = sb(st, "gn", [P, D])
            t = sp.dma(d_bc, g[:], bcast(w, D))
            dve.wait(t)
            norm_to_T(lat_tiles, [g[:]] * LT, None, hT, s_hT, [P * n for n in range(LT)])
            p.barrier()

        def memory_attention(layer, w_in, q_off):
            with ExitStack() as st:
                wm = [sb(st, f"wm{j}", [P, KT, P]) for j in range(3)]
                s_wm = Slot(p, "wm")
                qT = sb(st, "mqT", [P, SEQ])
                kz = sb(st, "mkz", [P, 2, NMEM])
                vv = sb(st, "mvv", [P, NMEM // P, P])
                s_q, s_k, s_v = Slot(p, "mq"), Slot(p, "mk"), Slot(p, "mv")
                bufs = softmax_bufs(st, NMEM)
                dve(V.memset, kz[:], 0.0)
                wkv = A["w_memkv"][layer]
                with p.repeat(f"memory{layer}", 2) as i:
                    sp.take(s_wm)
                    renew(s_wm)
                    sp.dma(d_w[0], wm[0][:], w_cols(w_in, i * P + q_off, P))
                    sp.dma(d_w[0], wm[1][:], w_cols(wkv, i * P, P))
                    s_wm.put(sp.dma(d_w[0], wm[2][:], w_cols(wkv, i * P + 256, P)))
                    pe.need(s_wm)
                    pe.take(B[7], B[6], B[5])
                    renew(B[7], B[6], B[5])
                    tq = mm_acc(PS[:, 7, :], [(wm[0][:, k, :], hT[:, k, 0:SEQ]) for k in range(KT)])
                    tk = mm_acc(PS[:, 6, 0:NMEM], [(wm[1][:, k, :], memT[:, k, :]) for k in range(KT)])
                    for n in range(2):
                        tv = mm_acc(PS[:, 5, n * P:(n + 1) * P],
                                    [(memT[:, k, n * P:(n + 1) * P], wm[2][:, k, :]) for k in range(KT)])
                    s_wm.got(tv)
                    act.take(s_q)
                    dve.take(s_k, s_v)
                    renew(s_q, s_k, s_v)
                    t = act(S.copy, qT[:], PS[:, 7, :], after=[tq])
                    s_q.put(t)
                    B[7].got(t)
                    dve(V.tensor_copy, kz[0:64, 0, :], PS[0:64, 6, 0:NMEM], after=[tk])
                    t = dve(V.tensor_copy, kz[64:P, 1, :], PS[64:P, 6, 0:NMEM])
                    s_k.put(t)
                    B[6].got(t)
                    t = dve(V.tensor_copy, vv[:].rearrange("p a b -> p (a b)"), PS[:, 5, 0:256], after=[tv])
                    s_v.put(t)
                    B[5].got(t)
                    pe.need(s_q, s_k, s_v)
                    units = []
                    for hh in range(2):
                        for n in range(LT):
                            units.append(dict(
                                n=NMEM, scale=64 ** -0.5,
                                scores=lambda o, hh=hh, n=n: mm_acc(o, [(qT[:, n * P:(n + 1) * P], kz[:, hh, :])]),
                                v=lambda j, hh=hh: vv[:, j, hh * 64:hh * 64 + 64],
                                out=OT[:, CT + n, bass.ds(i * P + (768 + 64 * hh), 64)]))
                    attend(units, bufs, [[0], [1]], [2], 3, 64)
                    for s in (s_q, s_k, s_v):
                        s.got(*B[3].fill)
                s_OT.put()

        w_a = A["w_in_a"][0]
        with ExitStack() as st:
            first_norm(st, A["norm_w"][0])
        with ExitStack() as st:
            DK, DV, NC_ = 96, 192, SEQ // 64
            wl = sb(st, "wl", [P, KT, 16])
            glT = sb(st, "glT", [16, SEQ])
            gmask = sb(st, "gmask", [P, P])
            reset = sb(st, "reset", [DK, SEQ])
            gw = sb(st, "gw", [P, DV])
            wh = [sb(st, f"wh{n}", [P, KT, 2 * DK + DV]) for n in range(2)]
            wu = [sb(st, f"wu{n}", [16, DK]) for n in range(2)]
            bg = [sb(st, f"bg{n}", [DK, 1]) for n in range(2)]
            s_wh = [Slot(p, f"wh{n}") for n in range(2)]
            with nc.allow_non_contiguous_dma("16 columns"):
                sp.dma(d_bc, wl[:], w_cols(w_a, 1536, 16))
            sp.dma(d_bc, gmask[:], A["c_gla_mask"])
            sp.dma(d_bc, reset[:], A["c_chunk_reset"])
            t = sp.dma(d_bc, gw[:], bcast(A["gla_norm_w"][0], DV))
            pe.wait(t)
            t = mm_acc(PS[0:16, 0, :], [(wl[:, k, :], hT[:, k, 0:SEQ]) for k in range(KT)])
            t = act(S.copy, glT[:], PS[0:16, 0, :], after=[t])
            names = ["u", "l", "bc", "eb", "q", "k", "ko"]
            W = {n: sb(st, "g_" + n, [DK, SEQ]) for n in names}
            sW = {n: Slot(p, "g_" + n) for n in names}
            qz = sb(st, "g_qz", [DK, 2, SEQ])
            koz = sb(st, "g_koz", [P, 2, LT, DK])
            vv = sb(st, "g_v", [P, LT, DV])
            AT = sb(st, "g_AT", [P, SEQ])
            Sx = sb(st, "g_S", [DK, NC_, DV])
            sm = sb(st, "g_sm", [P, 8])
            junk = sb(st, "g_junk", [P, DV])
            s_qz, s_koz, s_vv, s_AT, s_S, s_sm = (Slot(p, n) for n in ("g_qz", "g_koz", "g_v", "g_AT", "g_S", "g_sm"))
            dve(V.memset, qz[:], 0.0)
            dve(V.memset, koz[:], 0.0)
            dve(V.memset, Sx[:], 0.0)

            def chunks(ap):
                return ap.rearrange("d (c t) -> d c t", t=64)

            def gla_head(h, w, wu_, bg_, s_w):
                q, k, kx = (w[:, :, 0:DK], w[:, :, DK:2 * DK], w[:, :, 2 * DK:])
                pe.need(s_w)
                pe.take(B[2], B[0], B[1])
                renew(B[2], B[0], B[1])
                tz = mm_acc(PS[0:DK, 2, :], [(wu_[:], glT[:])])
                tq = mm_acc(PS[0:DK, 0, :], [(q[:, j, :], hT[:, j, 0:SEQ]) for j in range(KT)])
                tk = mm_acc(PS[0:DK, 1, :], [(k[:, j, :], hT[:, j, 0:SEQ]) for j in range(KT)])
                pe.take(B[3], B[4])
                renew(B[3], B[4])
                for n in range(LT):
                    tv = mm_acc(PS[:, 3 + n // 2, (n % 2) * DV:(n % 2) * DV + DV],
                                [(hT[:, j, n * P:(n + 1) * P], kx[:, j, :]) for j in range(KT)])
                s_w.got(tv)
                act.take(s_vv)
                renew(s_vv)
                for j in range(2):
                    t = act(S.copy, vv[:, 2 * j:2 * j + 2, :],
                            PS[:, 3 + j, 0:2 * DV].rearrange("p (a b) -> p a b", a=2), after=[tv])
                    B[3 + j].got(t)
                s_vv.put(t)
                act.take(sW["u"])
                renew(sW["u"])
                act.need(s_w)
                t = act(S.activation, W["u"][:], PS[0:DK, 2, :], ACT.Identity, bias=bg_[:], after=[tz])
                B[2].got(t)
                s_w.got(t)
                dve.take(sW["l"])
                renew(sW["l"])
                a = dve(V.tensor_scalar, W["l"][:], W["u"][:], -1.0, None, ALU.mult, after=[t])
                a = dve(V.tensor_tensor, W["l"][:], W["l"][:], W["u"][:], ALU.min, after=[a])
                a = act(S.activation, W["l"][:], W["l"][:], ACT.Exp, after=[a])
                a = act(S.activation, W["l"][:], W["l"][:], ACT.Ln, bias=1.0, after=[a])
                a = dve(V.scalar_tensor_tensor, W["u"][:], W["u"][:], 0.0, W["l"][:], ALU.min, ALU.subtract, after=[a])
                sW["l"].got(a)
                dve.take(sW["bc"])
                renew(sW["bc"])
                tb = dve(V.tensor_tensor_scan, W["bc"][:], reset[:], W["u"][:], 0.0, ALU.mult, ALU.add, after=[a])
                sW["u"].got(tb)
                tau = 1.0 / 16.0
                act.take(sW["eb"])
                renew(sW["eb"])
                te = act(S.activation, W["eb"][:], W["bc"][:], ACT.Exp, scale=tau, after=[tb])
                act.take(sW["l"])
                renew(sW["l"])
                tn = act(S.activation, W["l"][:], W["bc"][:], ACT.Exp, scale=-tau, after=[tb])
                dve.take(sW["ko"])
                renew(sW["ko"])
                last = chunks(W["bc"][:])[:, :, 63:64].to_broadcast([DK, NC_, 64])
                t = dve(V.tensor_tensor, chunks(W["ko"][:]), last, chunks(W["bc"][:]), ALU.subtract, after=[tb])
                sW["bc"].got(te, tn, t)
                t = act(S.activation, W["ko"][:], W["ko"][:], ACT.Exp, scale=tau, after=[t])
                dve.take(sW["q"], sW["k"], s_qz)
                renew(sW["q"], sW["k"], s_qz)
                a = dve(V.scalar_tensor_tensor, W["q"][:], PS[0:DK, 0, :], DK ** -0.5, W["eb"][:], ALU.mult,
                        ALU.mult, after=[tq, te])
                B[0].got(a)
                sW["q"].put(a)
                b = dve(V.tensor_tensor, W["k"][:], PS[0:DK, 1, :], W["l"][:], ALU.mult, after=[tk, tn])
                sW["l"].got(b)
                sW["k"].put(b)
                c = dve(V.tensor_tensor, W["ko"][:], PS[0:DK, 1, :], W["ko"][:], ALU.mult, after=[t])
                B[1].got(b, c)
                for par in range(2):
                    src = W["q"][:].rearrange("d (n c t) -> d n c t", c=2, t=64)[:, :, par, :]
                    dst = qz[:, par, :].rearrange("d (n c t) -> d n c t", c=2, t=64)[:, :, par, :]
                    t = dve(V.tensor_copy, dst, src, after=[a])
                s_qz.put(t)
                sW["q"].got(t)
                pe.take(B[6], B[5])
                renew(B[6], B[5])
                pe.wait(c)
                for n in range(LT):
                    t = pe(T.transpose, PS[:, 6, n * DK:(n + 1) * DK], W["ko"][:, n * P:(n + 1) * P],
                           ident[0:DK, 0:DK], sig=(n == LT - 1))
                sW["ko"].got(t)
                B[6].put(t)
                dve.take(s_koz)
                renew(s_koz)
                for par in range(2):
                    r = slice(64 * par, 64 * par + 64)
                    t2 = dve(V.tensor_copy, koz[r, par, :, :].rearrange("p a b -> p (a b)"),
                             PS[r, 6, 0:LT * DK], after=[t])
                B[6].got(t2)
                s_koz.put(t2)
                pe.wait(b)
                for n in range(LT):
                    t = pe(T.matmul, PS[:, 5, n * P:(n + 1) * P], W["k"][:, n * P:(n + 1) * P],
                           W["q"][:, n * P:(n + 1) * P], start=True, stop=True, sig=(n == LT - 1))
                B[5].put(t)
                sW["k"].got(t)
                sW["q"].got(t)
                dve.take(s_AT)
                renew(s_AT)
                t = dve(V.tensor_tensor, AT[:].rearrange("p (n c) -> p n c", n=LT),
                        PS[:, 5, :].rearrange("p (n c) -> p n c", n=LT),
                        gmask[:].unsqueeze(1).to_broadcast([P, LT, P]), ALU.mult, after=[t])
                B[5].got(t)
                s_AT.put(t)
                pe.need(s_koz, s_vv)
                dve.take(s_S)
                renew(s_S)
                t = None
                for n0 in range(0, NC_ - 1, 2):
                    b = (0, 1, 2, 7)[n0 // 2]
                    pair_ = range(n0, min(n0 + 2, NC_ - 1))
                    pe.take(B[b])
                    renew(B[b])
                    for n in pair_:
                        a = pe(T.matmul, PS[0:DK, b, (n % 2) * DV:(n % 2) * DV + DV], koz[:, n % 2, n // 2, :],
                               vv[:, n // 2, :], start=True, stop=True)
                    B[b].put(a)
                    for n in pair_:
                        t = dve(V.scalar_tensor_tensor, Sx[:, n + 1, :], Sx[:, n, :],
                                W["eb"][:, 64 * n + 63:64 * n + 64], PS[0:DK, b, (n % 2) * DV:(n % 2) * DV + DV],
                                ALU.mult, ALU.add, after=[a, t])
                        s_S.put(t)
                    B[b].got(t)
                s_koz.got(a)
                sW["eb"].got(t)
                pe.need(s_AT, s_qz)
                pe.take(B[3], B[4])
                renew(B[3], B[4])
                act.take(s_sm)
                renew(s_sm)
                for n in range(LT):
                    pe.wait(s_S.fill[min(2 * n, NC_ - 2)])
                    o = PS[:, 3 + n // 2, (n % 2) * DV:(n % 2) * DV + DV]
                    t = mm_acc(o, [(AT[:, n * P:(n + 1) * P], vv[:, n, :]),
                                   (qz[:, 0, n * P:(n + 1) * P], Sx[:, 2 * n, :]),
                                   (qz[:, 1, n * P:(n + 1) * P], Sx[:, 2 * n + 1, :])])
                    B[3 + n // 2].put(t)
                for n in range(LT):
                    o = PS[:, 3 + n // 2, (n % 2) * DV:(n % 2) * DV + DV]
                    tn = act(S.activation, junk[:], o, ACT.Square, accum_out=sm[:, n:n + 1], after=[t, tn])
                for s in (s_AT, s_vv, s_qz, s_S):
                    s.got(t)
                tn = rstd_of(sm[:, 0:LT], DV, P, [tn], sm[:, 4:8])
                for n in range(LT):
                    o = PS[:, 3 + n // 2, (n % 2) * DV:(n % 2) * DV + DV]
                    t = dve(V.scalar_tensor_tensor, OT[:, CT + n, bass.ds(h, DV)], o, sm[:, 4 + n:5 + n], gw[:],
                            ALU.mult, ALU.mult, after=[tn])
                    B[3 + n // 2].got(t)
                s_sm.got(t)
                s_OT.put(t)

            with p.repeat("gla", 2) as i:
                for n in range(2):
                    s, w = s_wh[n], wh[n]
                    sp.take(s)
                    renew(s)
                    col = i * (2 * DK) + n * DK
                    sp.dma(d_w[n], w[:, :, 0:DK], w_cols(w_a, col, DK))
                    sp.dma(d_w[n], w[:, :, DK:2 * DK], w_cols(w_a, col + 384, DK))
                    sp.dma(d_w[n], w[:, :, 2 * DK:], w_cols(w_a, i * (2 * DV) + (n * DV + 768), DV))
                    sp.dma(d_w[n], wu[n][:], A["w_gate_up"][0][:, bass.ds(col, DK)])
                    s.put(sp.dma(d_w[n], bg[n][:],
                                 A["b_gate"][0].rearrange("(n a) -> n a", a=1)[bass.ds(col, DK), :]))
                for n in range(2):
                    gla_head(i * (2 * DV) + n * DV, wh[n], wu[n], bg[n], s_wh[n])
        memory_attention(0, w_a, 1552)
        with ExitStack() as st:
            gate_and_project(st, A["w_out"][0], (w_a, 1808), list(range(CT, NT)))

        w_b = A["w_in_b"][0]
        with ExitStack() as st:
            first_norm(st, A["norm_w"][1])
        with ExitStack() as st:
            mask = sb(st, "mask", [P, 10 * P])
            cosT, sinT = sb(st, "cosT", [32, SEQ]), sb(st, "sinT", [32, SEQ])
            rot = sb(st, "rot", [P, P])
            wq = [sb(st, f"wq{g}", [P, KT, 3, P]) for g in range(3)]
            s_wq = [Slot(p, f"wq{g}") for g in range(3)]
            qk = [[[sb(st, f"qk{m}{g}{j}", [P, SEQ]) for j in range(2)] for g in range(3)] for m in range(2)]
            vg = [[sb(st, f"vg{m}{g}", [P, LT, P]) for g in range(3)] for m in range(2)]
            rt = [hrow[j][0:32, SEQ:2 * SEQ] for j in range(2)]
            s_qk = [[[Slot(p, f"qk{m}{g}{j}") for j in range(2)] for g in range(3)] for m in range(2)]
            s_vg = [[Slot(p, f"vg{m}{g}") for g in range(3)] for m in range(2)]
            s_rt = [Slot(p, f"rt{j}") for j in range(2)]
            bufs = softmax_bufs(st, 10 * P, 4)
            sp.dma(d_bc, mask[:], A["c_dil_mask"])
            sp.dma(d_bc, cosT[:], A["c_dil_cos"])
            sp.dma(d_bc, sinT[:], A["c_dil_sin"])
            t = sp.dma(d_bc, rot[:], A["c_dil_rot"])
            for e in (pe, dve):
                e.wait(t)

            def load_group(h, g):
                sp.take(s_wq[g])
                renew(s_wq[g])
                for j in range(3):
                    t = sp.dma(d_qkv[g], wq[g][:, :, j, :], w_cols(w_b, h * P + (3 * g + j) * 768, P))
                s_wq[g].put(t)

            def load(h, par):
                for g in range(3):
                    load_group(h, g)

            def project(h, par, ahead):
                steps = []

                def qk_step(g, j):
                    pe.need(s_wq[g])
                    pe.take(B[7])
                    renew(B[7])
                    t = mm_acc(PS[:, 7, :], [(wq[g][:, k, j, :], hT[:, k, 0:SEQ]) for k in range(KT)])
                    s_wq[g].got(t)
                    act.take(s_qk[par][g][j])
                    renew(s_qk[par][g][j])
                    t = act(S.copy, qk[par][g][j][:], PS[:, 7, :], after=[t])
                    B[7].got(t)
                    s_qk[par][g][j].put(t)

                def v_step(g):
                    pe.take(B[7])
                    renew(B[7])
                    for n in range(LT):
                        t = mm_acc(PS[:, 7, n * P:(n + 1) * P],
                                   [(hT[:, k, n * P:(n + 1) * P], wq[g][:, k, 2, :]) for k in range(KT)])
                    s_wq[g].got(t)
                    act.take(s_vg[par][g])
                    renew(s_vg[par][g])
                    t = act(S.copy, vg[par][g][:].rearrange("p a b -> p (a b)"), PS[:, 7, :], after=[t])
                    B[7].got(t)
                    s_vg[par][g].put(t)
                    if ahead is not None:
                        load_group(ahead, g)

                def rope_step(g, j):
                    x, s = qk[par][g][j][0:32, :], s_qk[par][g][j]
                    pe.take(B[7])
                    renew(B[7])
                    pe.need(s)
                    t = mm_acc(PS[:, 7, :], [(rot[:], qk[par][g][j][:])])
                    act.take(s_rt[j])
                    renew(s_rt[j])
                    t = act(S.copy, rt[j], PS[0:32, 7, :], after=[t])
                    B[7].got(t)
                    t = dve(V.tensor_tensor, rt[j], rt[j], sinT[:], ALU.mult, after=[t])
                    a = dve(V.tensor_tensor, x, x, cosT[:], ALU.mult, after=[t])
                    t = dve(V.tensor_tensor, x, x, rt[j], ALU.add, after=[a])
                    s_rt[j].got(t)
                    s.put(t)

                for g in range(3):
                    steps += [lambda g=g: qk_step(g, 0), lambda g=g: qk_step(g, 1),
                              lambda g=g: rope_step(g, 0), lambda g=g: rope_step(g, 1)]
                    brief.extend(steps[-2:])
                return dealt(-3, 0, steps) + dealt(0, 1, [lambda g=g: v_step(g) for g in range(3)])

            def units(h, par):
                q_k, v_g = qk[par], vg[par]
                out_ = []
                for n in range(LT):
                    lo = max(n - 1, 0)
                    spans = [(0, lo, n + 1)] + [(1, 0, n + 1), (2, 0, n + 1)]
                    mcol = [(2 - (n + 1 - lo)) * P, (2 + LT - n - 1) * P, (2 + 2 * LT - n - 1) * P]
                    blocks = [(g, b) for g, a, z in spans for b in range(a, z)]

                    def scores(o, n=n, blocks=blocks):
                        tk = None
                        for x, (g, b) in enumerate(blocks):
                            tk = pe(T.matmul, o[:, x * P:(x + 1) * P], q_k[g][0][:, n * P:(n + 1) * P],
                                    q_k[g][1][:, b * P:(b + 1) * P], start=True, stop=True,
                                    sig=(x == len(blocks) - 1))
                        return tk

                    def bias(src, dst, toks, spans=spans, mcol=mcol):
                        at, toks_ = 0, []
                        for (g, a, z), mc in zip(spans, mcol):
                            w = (z - a) * P
                            toks_.append(dve(V.tensor_tensor, dst[:, at:at + w], src[:, at:at + w],
                                             mask[:, mc:mc + w], ALU.add, after=toks))
                            at += w
                        return toks_

                    out_.append(dict(n=len(blocks) * P, scale=P ** -0.5, scores=scores, bias=bias,
                                     v=lambda j, blocks=blocks: v_g[blocks[j][0]][:, blocks[j][1], :],
                                     out=OT[:, CT + n, bass.ds(h * P, P)]))
                return out_, [s for g in range(3) for s in s_qk[par][g]], s_vg[par]

            AW = 6 * D // (6 * LT)
            wa = [OT[:, 0:CT, :].rearrange("p a (b c) -> p (a b) c", c=AW), hT[:, :, SEQ:ALLT]]
            acc = [hrow[l][:, 0:2 * AW].rearrange("p (a b) -> p a b", a=2) for l in range(2)]
            BLK = AW // P
            mod_cols = sb(st, "mod_cols", [P, 2, 2, BLK + 6 * KT])
            s_wa, s_acc = ([Slot(p, f"{n}{l}") for l in range(2)] for n in ("wa", "ada_acc"))

            def load_ada(l, col):
                sp.take(s_wa[l])
                renew(s_wa[l])
                s_wa[l].put(sp.dma(d_ada[l], wa[l], w_cols(A["w_ada_2"][l], col, AW)))

            def ada_steps(h, x, last):
                def rows(l, k):
                    if k == 0:
                        dve.need(s_wa[l])
                        dve.take(s_acc[l])
                        renew(s_acc[l])
                    toks = []
                    for c in range(2):
                        a, w_ = acc[l][:, c, :], wa[l][:, k, :]
                        toks.append(dve(V.tensor_scalar, a, w_, cv[:, k, c:c + 1], None, ALU.mult) if k == 0 else
                                    dve(V.scalar_tensor_tensor, a, w_, cv[:, k, c:c + 1], a, ALU.mult, ALU.add,
                                        after=[s_acc[l].fill[c]]))
                    s_acc[l].fill = toks
                    if k == KT - 1:
                        s_wa[l].got(*toks)
                        if not last:
                            load_ada(l, h * D + (x + 1) * AW)

                first, second = ([lambda l=l, k=k: rows(l, k) for k in range(KT)] for l in range(2))
                before = h * KT + x * BLK
                return ([lambda: sum_up(0, before)] + first[:KT // 2] + [lambda: sum_up(1, before)]
                        + first[KT // 2:] + second)

            def sum_up(l, at):
                pe.need(s_acc[l])
                pe.take(B[7])
                renew(B[7])
                for c in range(2):
                    for m in range(BLK):
                        t = pe(T.matmul, PS[:, 7, c * BLK + m:c * BLK + m + 1], acc[l][:, c, m * P:(m + 1) * P],
                               ones[:, 0:1], start=True, stop=True, sig=c * BLK + m == 2 * BLK - 1)
                B[7].put(t)
                s_acc[l].got(t)
                t = act(S.copy, mod_cols[:, l, :, bass.ds(at, BLK)],
                        PS[:, 7, 0:2 * BLK].rearrange("p (c m) -> p c m", c=2), after=[t])
                B[7].got(t)

            for l in range(2):
                s_acc[l].put(*[dve(V.memset, acc[l][:, c, :], 0.0) for c in range(2)])
                load_ada(l, 0)
            pipeline("dilated", 6, 1, load, project, units, LT, stages(bufs, [[0, 1, 2]], [3, 4, 5], 6, P), ada_steps,
                     turn_first=False)

            for l in range(2):
                sum_up(l, 6 * KT)
            p.barrier()
            rows_ = hrow[0][0:6 * KT, 512:512 + 4 * P].rearrange("t (l c p) -> t l c p", l=2, c=2)
            b_rows = hrow[1][0:6 * KT, 512:512 + 2 * P].rearrange("t (l p) -> t l p", l=2)
            t_b = sp.dma(d_bc, b_rows, A["b_ada_2"].rearrange("l (t p) -> t l p", p=P))
            dve.wait(t_b)
            for l in range(2):
                for c in range(2):
                    t = pe(T.transpose, PS[0:6 * KT, 2 * l + c, 0:P], mod_cols[:, l, c, BLK:], ident[:])
                    t = dve(V.tensor_tensor, rows_[:, l, c, :], PS[0:6 * KT, 2 * l + c, 0:P], b_rows[:, l, :],
                            ALU.add, after=[t])
                    sp.dma(d_st, mods[l, c].rearrange("(t p) -> t p", p=P), rows_[:, l, c, :], after=[t])
            p.barrier()
        memory_attention(1, w_b, 6912)
        with ExitStack() as st:
            gate_and_project(st, A["w_out"][1], (w_b, 7168), list(range(CT, NT)))
        memx.close()

        def norm_rows(st, w, tiles, dst):
            g = sb(st, "gf", [P, D])
            junk = sb(st, "fjunk", [P, D])
            t = sp.dma(d_bc, g[:], bcast(w, D))
            act.wait(t)
            dve.wait(t)
            t = None
            for j, tl in enumerate(tiles):
                t = act(S.activation, junk[:], X[:, tl, :], ACT.Square, accum_out=small[:, j:j + 1], after=[t])
            t = rstd_of(small[:, 0:LT], D, P, [t], small[:, 8:8 + LT])
            for j, tl in enumerate(tiles):
                a = dve(V.scalar_tensor_tensor, dst(tl), X[:, tl, :], small[:, 8 + j:9 + j], g[:],
                        ALU.mult, ALU.mult, after=[t])
            p.barrier()

        with ExitStack() as st:
            norm_rows(st, A["final_norm_w"], range(CT, NT), lambda tl: X[:, tl, :])

        def modulation(st, layer, part, norm_w, who, w):
            g, s = sb(st, f"mg{who}", [P, D]), sb(st, f"ms{who}", [P, D])
            stream = (d_bc, d_wo)[who]
            row = mods[layer, who]
            sp.dma(stream, s[:], bcast(row[(3 * part) * D:(3 * part + 1) * D], D))
            sp.dma(stream, g[:], bcast(row[(3 * part + 1) * D:(3 * part + 2) * D], D))
            t = sp.dma(stream, w[:], bcast(norm_w, D)) if who == 0 else Token(stream, None, 0, stream.count)
            dve(V.scalar_tensor_tensor, g[:], g[:], 1.0, w[:], ALU.add, ALU.mult, after=[t])
            return g, s

        def modulated_T(layer, part, norm_w, tiles, to_dram=None):
            with ExitStack() as st:
                mw = sb(st, "mw", [P, D])
                gl, sl = modulation(st, layer, part, norm_w, 0, mw)
                gc, sc = modulation(st, layer, part, norm_w, 1, mw) if 0 in tiles else (None, None)
                dve.wait(*p.everything(ahead=False))
                norm_to_T([(X[:, t, :], s_X[t]) for t in tiles], [gc[:] if t < CT else gl[:] for t in tiles],
                          [sc[:] if t < CT else sl[:] for t in tiles], hT, s_hT,
                          [P * j for j in range(len(tiles))], to_dram)
                p.barrier()

        def row_gates(st, layer, part, with_ctx):
            gs = []
            for who in range(2 if with_ctx else 1):
                g = sb(st, f"rg{who}", [P, D])
                t = sp.dma(d_bc, g[:], bcast(mods[layer, who, (3 * part + 2) * D:(3 * part + 3) * D], D))
                gs.append(g)
            dve.wait(t)
            return lambda tl: gs[1][:] if tl < CT else gs[0][:]

        def spans():
            return [(0, NSPAN), (NSPAN, ALLT)]

        def project_T(dst, w, kt, rhs, banks, m, evac=None):
            toks = []
            for (a, z), b in zip(spans(), banks):
                pe.take(B[b])
                renew(B[b])
                t = mm_acc(PS[0:m, b, 0:z - a], [(w(k), rhs[:, k, a:z]) for k in range(kt)])
                t = act(S.copy, dst[:, a:z], PS[0:m, b, 0:z - a], after=[t])
                B[b].got(t)
                toks.append(t)
            return toks

        def feature_norm(xs, sq, s_sq, summer, width, gains, banks, n=P):
            toks = []
            for (a, z), b in zip(spans(), banks):
                pe.take(B[b])
                renew(B[b])
                for j, x in enumerate(xs):
                    act.take(s_sq)
                    renew(s_sq)
                    t = act(S.activation, sq[0:n, 0:z - a], x[:, a:z], ACT.Square)
                    t = pe(T.matmul, PS[0:n, b, 0:z - a], summer[0:n, 0:n], sq[0:n, 0:z - a], start=(j == 0),
                           stop=(j == len(xs) - 1), after=[t])
                    s_sq.got(t)
                act.take(s_sq)
                renew(s_sq)
                t = rstd_of(PS[0:n, b, 0:z - a], width, n, [t], sq[0:n, 0:z - a])
                B[b].got(t)
                for j, x in enumerate(xs):
                    t2 = dve(V.scalar_tensor_tensor, x[:, a:z], x[:, a:z], gains[j], sq[0:n, 0:z - a],
                             ALU.mult, ALU.mult, after=[t])
                    toks.append(t2)
                s_sq.got(t2)
            return toks

        def rope(x, r0, r1, cos, sin, rot_m, tmp, s_tmp, banks, after, k0=0):
            toks = []
            for n, ((a, z), b) in enumerate(zip(spans(), banks)):
                pe.take(B[b])
                renew(B[b])
                t = pe(T.matmul, PS[k0:r1, b, 0:z - a], rot_m[k0:r1, k0:r1], x[k0:r1, a:z], start=True, stop=True,
                       after=after)
                dve.take(s_tmp)
                renew(s_tmp)
                t1 = dve(V.tensor_tensor, tmp[r0:r1, 0:z - a], PS[r0:r1, b, 0:z - a], sin[r0:r1, a:z], ALU.mult, after=[t])
                B[b].got(t1)
                t2 = dve(V.tensor_tensor, x[r0:r1, a:z], x[r0:r1, a:z], cos[r0:r1, a:z], ALU.mult, after=[t])
                t = dve(V.tensor_tensor, x[r0:r1, a:z], x[r0:r1, a:z], tmp[r0:r1, 0:z - a], ALU.add, after=[t1, t2])
                s_tmp.got(t)
                toks.append(t)
            return toks

        def lat_and_ctx_units(qT, kk, v, scale, out, with_ctx=True, dq=P):
            units = []
            for n in range(0 if with_ctx else CT, NT):
                nk = CTX if n < CT else ALLT

                def scores(o, n=n, nk=nk):
                    a = pe(T.matmul, o[:, 0:min(nk, 512)], qT[:, n * P:(n + 1) * P], kk[..., 0:min(nk, 512)],
                           start=True, stop=True, sig=nk <= 512)
                    if nk > 512:
                        a = pe(T.matmul, o[:, 512:nk], qT[:, n * P:(n + 1) * P], kk[..., 512:nk], start=True, stop=True)
                    return a
                units.append(dict(n=nk, scale=scale, scores=scores, v=v, out=out(n)))
            return units

        modulated_T(0, 0, A["norm_mix_2"][0], range(NT))
        w_ab = A["ab_w_in_2"][0]
        with ExitStack() as st:
            cq = [sb(st, f"cq{j}", [P, ALLT]) for j in range(3)]
            ckv = [sb(st, f"ckv{j}", [P, ALLT]) for j in range(2)]
            kr = sb(st, "kr", [96, ALLT])
            va = sb(st, "va", [P, NT, 512])
            vb = sb(st, "vb", [P, NT, P])
            kz = sb(st, "kz", [P, 2, 2, ALLT])
            mcos, msin = sb(st, "mcos", [96, ALLT]), sb(st, "msin", [96, ALLT])
            gcos, gsin = sb(st, "gcos", [P, ALLT]), sb(st, "gsin", [P, ALLT])
            pair, hsum = sb(st, "pair", [P, P]), sb(st, "hsum", [P, P])
            gains = sb(st, "gains", [P, 8])
            sq = sb(st, "sq", [P, NSPAN])
            s_sq = Slot(p, "sq")
            tmp_ = sb(st, "rtmp", [P, NSPAN])
            s_tmp_ = Slot(p, "rtmp")
            dve(V.memset, kz[:], 0.0)
            with ExitStack() as sw:
                wx = sb(sw, "wx", [P, KT, 928])
                wv = sb(sw, "wv", [P, 2, 512])
                kb = sb(sw, "kb", [P, ALLT])
                sp.dma(d_w[0], wx[:, :, 0:672], w_cols(w_ab, 0, 672))
                sp.dma(d_w[0], wx[:, :, 672:928], w_cols(w_ab, 1184, 256))
                for j in range(2):
                    sp.dma(d_w[0], wv[:, j, :].rearrange("p (h c) -> p h c", h=8),
                           A["mla_w_kv_up_2"][0][j * P:(j + 1) * P, :].rearrange("p (h c) -> p h c", h=8)[:, :, 64:128])
                for dst, name in ((mcos, "mla_cos"), (msin, "mla_sin"), (gcos, "gqa_cos"), (gsin, "gqa_sin"),
                                  (pair, "pair_rot"), (hsum, "head_sum")):
                    sp.dma(d_w[0], dst[:], A["c_" + name])
                with nc.allow_non_contiguous_dma("norm weights as columns"):
                    sp.dma(d_w[0], gains[:, 0:3], A["mla_q_norm_2"][0].rearrange("(t p) -> p t", p=P))
                    sp.dma(d_w[0], gains[:, 3:5], A["mla_kv_norm_2"][0].rearrange("(t p) -> p t", p=P))
                    for half in range(2):
                        r = slice(64 * half, 64 * half + 64)
                        sp.dma(d_w[0], gains[r, 5:6], A["gqa_q_norm_2"][0].rearrange("(p a) -> p a", a=1))
                        t = sp.dma(d_w[0], gains[r, 6:7], A["gqa_k_norm_2"][0].rearrange("(p a) -> p a", a=1))
                for e in (pe, act, dve):
                    e.wait(t)
                tq, tkv = [], []
                for j in range(3):
                    tq += project_T(cq[j][:], lambda k, j=j: wx[:, k, j * P:(j + 1) * P], KT, hT, (0, 1), P)
                for j in range(2):
                    tkv += project_T(ckv[j][:], lambda k, j=j: wx[:, k, 384 + j * P:384 + (j + 1) * P], KT, hT, (2, 3), P)
                act.wait(*tq, *tkv)
                feature_norm([c[:] for c in cq], sq, s_sq, ones, 384, [gains[:, j:j + 1] for j in range(3)], (4, 5))
                tkv = feature_norm([c[:] for c in ckv], sq, s_sq, ones, 256, [gains[:, 3 + j:4 + j] for j in range(2)], (6, 7))
                tr = []
                for (a, z), b in zip(spans(), (0, 1)):
                    pe.take(B[b])
                    renew(B[b])
                    t = mm_acc(PS[64:96, b, 0:z - a], [(wx[:, k, 640:672], hT[:, k, a:z]) for k in range(KT)])
                    t = act(S.copy, kr[64:96, a:z], PS[64:96, b, 0:z - a], after=[t])
                    B[b].got(t)
                    tr.append(t)
                rope(kr, 64, 96, mcos, msin, pair, tmp_, s_tmp_, (2, 3), tr, k0=64)
                tk = project_T(kb[:], lambda k: wx[:, k, 672:800], KT, hT, (0, 1), P)
                act.wait(*tk)
                tk = feature_norm([kb[:]], sq, s_sq, hsum, 64, [gains[:, 6:7]], (4, 5))
                tk = rope(kb, 0, P, gcos, gsin, pair, tmp_, s_tmp_, (2, 3), tk)
                for kv in range(2):
                    r = slice(64 * kv, 64 * kv + 64)
                    dve(V.tensor_copy, kz[r, kv, kv, :], kb[r, :], after=tk)
                for kv in range(2):
                    o = 64 * (1 - kv)
                    sp.dma(d_g, kz[o:o + 64, kv, 1 - kv, :], kb[64 * kv:64 * kv + 64, :], after=tk)
                pe.wait(*tkv)
                for n in range(NT):
                    b = 4 + n % 4
                    pe.take(B[b])
                    renew(B[b])
                    t = mm_acc(PS[:, b, :], [(ckv[k][:, n * P:(n + 1) * P], wv[:, k, :]) for k in range(2)])
                    t = act(S.copy, va[:, n, :], PS[:, b, :], after=[t])
                    B[b].got(t)
                for n in range(NT):
                    b = n % 4
                    pe.take(B[b])
                    renew(B[b])
                    t = mm_acc(PS[:, b, 0:P], [(hT[:, k, n * P:(n + 1) * P], wx[:, k, 800:928]) for k in range(KT)])
                    t = act(S.copy, vb[:, n, :], PS[:, b, 0:P], after=[t])
                    B[b].got(t)
                p.barrier()
            bufs = softmax_bufs(st, ALLT)
            stage = stages(bufs, [[0, 1], [2, 3]], [4, 5], 6, 64)
            with ExitStack() as sh:
                wqu = [sb(sh, f"wqu{n}", [P, 3, 96]) for n in range(2)]
                wku = [sb(sh, f"wku{n}", [P, 2, 64]) for n in range(2)]
                s_wu = [Slot(p, f"wqku{n}") for n in range(2)]
                qT = [sb(sh, f"aqT{n}", [96, ALLT]) for n in range(2)]
                kT = [sb(sh, f"akT{n}", [96, ALLT]) for n in range(2)]
                s_qT, s_kT = [Slot(p, f"aqT{n}") for n in range(2)], [Slot(p, f"akT{n}") for n in range(2)]

                def load(e, m):
                    sp.take(s_wu[m])
                    renew(s_wu[m])
                    sp.dma(d_qkv[m], wqu[m][:], w_cols(A["mla_w_q_up_2"][0], e * 96, 96))
                    s_wu[m].put(sp.dma(d_qkv[m], wku[m][:], w_cols(A["mla_w_kv_up_2"][0], e * P, 64)))

                def project(e, m, ahead):
                    def q_step(a, z):
                        pe.need(s_wu[m])
                        if a == 0:
                            act.take(s_qT[m])
                            renew(s_qT[m])
                        pe.take(B[7])
                        renew(B[7])
                        t = mm_acc(PS[0:96, 7, 0:NSPAN], [(wqu[m][:, k, :], cq[k][:, a:z]) for k in range(3)])
                        s_wu[m].got(t)
                        t = act(S.copy, qT[m][:, a:z], PS[0:96, 7, 0:NSPAN], after=[t])
                        B[7].got(t)
                        s_qT[m].put(t)

                    def k_step(a, z):
                        if a == 0:
                            act.take(s_kT[m])
                            dve.take(s_kT[m])
                            renew(s_kT[m])
                            s_kT[m].put(dve(V.tensor_copy, kT[m][64:96, :], kr[64:96, :]))
                        pe.take(B[7])
                        renew(B[7])
                        t = mm_acc(PS[0:64, 7, 0:NSPAN], [(wku[m][:, k, :], ckv[k][:, a:z]) for k in range(2)])
                        s_wu[m].got(t)
                        t = act(S.copy, kT[m][0:64, a:z], PS[0:64, 7, 0:NSPAN], after=[t])
                        B[7].got(t)
                        s_kT[m].put(t)
                        if a and ahead is not None:
                            load(ahead, m)

                    def rope_step():
                        s_qT[m].put(*rope(qT[m], 64, 96, mcos, msin, pair, tmp_, s_tmp_, (7, 7), s_qT[m].fill))

                    (a0, z0), (a1, z1) = spans()
                    return dealt(-3, 1, [lambda: q_step(a0, z0), lambda: q_step(a1, z1), rope_step,
                                         lambda: k_step(a0, z0), lambda: k_step(a1, z1)])

                def units(e, m):
                    return lat_and_ctx_units(
                        qT[m], kT[m], lambda j: va[:, j, bass.ds(e * 64, 64)], 96 ** -0.5,
                        lambda tl: OT[:, tl, bass.ds(e * 64, 64)]), [s_qT[m], s_kT[m]], []

                pipeline("mla", 8, 2, load, project, units, NT, stage)
            with ExitStack() as sh:
                wg = [sb(sh, f"wgq{m}", [P, KT, P]) for m in range(2)]
                s_wg = [Slot(p, f"wgq{m}") for m in range(2)]
                qT = [sb(sh, f"gqT{m}", [P, ALLT]) for m in range(2)]
                s_qT = [Slot(p, f"gqT{m}") for m in range(2)]

                def load(e, m):
                    sp.take(s_wg[m])
                    renew(s_wg[m])
                    s_wg[m].put(sp.dma(d_qkv[m], wg[m][:], w_cols(w_ab, e * P + 672, P)))

                def project(e, m, ahead):
                    def q_step(a, z):
                        pe.need(s_wg[m])
                        if a == 0:
                            act.take(s_qT[m])
                            renew(s_qT[m])
                        pe.take(B[7])
                        renew(B[7])
                        t = mm_acc(PS[:, 7, 0:z - a], [(wg[m][:, k, :], hT[:, k, a:z]) for k in range(KT)])
                        s_wg[m].got(t)
                        t = act(S.copy, qT[m][:, a:z], PS[:, 7, 0:z - a], after=[t])
                        B[7].got(t)
                        s_qT[m].put(t)
                        if a and ahead is not None:
                            load(ahead, m)

                    def norm_step():
                        act.wait(*s_qT[m].fill)
                        s_qT[m].put(*feature_norm([qT[m][:]], sq, s_sq, hsum, 64, [gains[:, 5:6]], (7, 7)))

                    def rope_step():
                        s_qT[m].put(*rope(qT[m], 0, P, gcos, gsin, pair, tmp_, s_tmp_, (7, 7), s_qT[m].fill))

                    (a0, z0), (a1, z1) = spans()
                    return dealt(-3, 7, [lambda: q_step(a0, z0), lambda: q_step(a1, z1), norm_step, rope_step])

                def units(e, m):
                    kv = e // 2
                    out_ = []
                    for hh in range(2):
                        out_ += lat_and_ctx_units(
                            qT[m], kz4[:, bass.ds(kv * 2 + hh, 1), :],
                            lambda j: vb[:, j, bass.ds(kv * 64, 64)], 64 ** -0.5,
                            lambda tl, hh=hh: OT[:, tl, bass.ds(e * P + (512 + 64 * hh), 64)])
                    return out_, [s_qT[m]], []

                kz4 = kz[:].rearrange("p a b c -> p (a b) c")
                pipeline("gqa", 4, 2, load, project, units, 2 * NT, stage)
        with ExitStack() as st:
            rg = row_gates(st, 0, 0, True)
            gate_and_project(st, A["ab_w_out_2"][0], None, list(range(NT)), rg)

        def moe(layer, tiles):
            n_t = len(tiles)
            with ExitStack() as st:
                E = expert_buffers(st, layer)
                for e in range(2):
                    for w in range(3):
                        load_w(E, w, e, e % 2)
                modulated_T(layer, 1, A["norm_ffn_2"][layer], tiles, to_dram=h_dram)
                idx = sb(st, "idx", [P, NBLK], U32)
                rows = sb(st, "rows", [P, 2, NT], U32)
                wts = sb(st, "wts", [P, 2, NT])
                n_ov = sb(st, "n_ov", [P, 1], U32)
                ov_e = sb(st, "ov_e", [P, 16], U32)
                route(st, layer, n_t, idx, rows, wts, n_ov, ov_e)
                experts(E, layer, idx, n_ov, ov_e)
                g2 = row_gates(st, layer, 1, 0 in tiles)
                yr = [[OT[:, 2 * a + b, :] for b in range(2)] for a in range(2)]
                s_yr = [Slot(p, f"yr{a}") for a in range(2)]
                for j, tl in enumerate(tiles):
                    y, s = yr[j % 2], s_yr[j % 2]
                    pool.take(s)
                    renew(s)
                    for b in range(2):
                        t = d_yg[j % 2].counted(G.indirect_dma_start(
                            y[b][:], None, y_dram, bass.IndirectOffsetOnAxis(ap=rows[:, b, j:j + 1], axis=0)))
                    s.put(t)
                    t = dve(V.tensor_scalar, y[0][:], y[0][:], wts[:, 0, j:j + 1], None, ALU.mult, after=[t])
                    t = dve(V.scalar_tensor_tensor, y[0][:], y[1][:], wts[:, 1, j:j + 1], y[0][:], ALU.mult,
                            ALU.add, after=[t])
                    t = dve(V.tensor_tensor, y[0][:], y[0][:], g2(tl), ALU.mult, after=[t])
                    t = dve(V.tensor_tensor, X[:, tl, :], X[:, tl, :], y[0][:], ALU.add, after=[t])
                    s.got(t)
                p.barrier(ahead=True)

        def route(st, layer, n_t, idx, rows, wts, n_ov, ov_e):
            with ExitStack() as s:
                wr = sb(s, "wr", [P, KT, 36])
                br = sb(s, "br", [P, 36])
                L = sb(s, "L", [P, NT, 36])
                io = sb(s, "io", [P, 32])
                tri = sb(s, "tri", [P, P])
                ids = sb(s, "ids", [P, NT], U32)
                with nc.allow_non_contiguous_dma("router weights"):
                    sp.dma(d_bc, wr[:, :, 0:4], A["moe_w_rg_2"][layer].rearrange("(t p) m -> p t m", p=P))
                    sp.dma(d_bc, wr[:, :, 4:36], A["moe_w_re_2"][layer].rearrange("(t p) m -> p t m", p=P))
                sp.dma(d_bc, br[:, 0:4], bcast(A["moe_b_rg_2"][layer], 4))
                sp.dma(d_bc, br[:, 4:36], bcast(A["moe_b_re_2"][layer], 32))
                sp.dma(d_bc, io[:], A["c_iota32"])
                sp.dma(d_bc, tri[:], A["c_before"])
                sp.dma(d_bc, ids[:], A["c_token_ids"])
                t = sp.dma(d_bc, table[layer].rearrange("(p b) a -> p (b a)", p=P), A["c_zero_table"])
                for e in (pe, dve, pool):
                    e.wait(t)
                for n in range(n_t):
                    t = mm_acc(PS[:, 0, n * 36:(n + 1) * 36], [(hT[:, k, n * P:(n + 1) * P], wr[:, k, :]) for k in range(KT)])
                d = lambda *a, **k: dve(*a, after=[last_dve()], **k)

                def last_dve():
                    return Token(dve.ctr, None, 0, dve.ctr.count)

                def bc(ap, shape):
                    return ap[:].to_broadcast(shape)

                def tile(name, w, dt=F32):
                    return sb(s, "r_" + name, [P, n_t, w], dt)

                dve.wait(t)
                d(V.tensor_tensor, L[:, 0:n_t, :], PS[:, 0, 0:36 * n_t].rearrange("p (n m) -> p n m", m=36),
                  bc(br[:].unsqueeze(1), [P, n_t, 36]), ALU.add)
                lg, le = L[:, 0:n_t, 0:4], L[:, 0:n_t, 4:36]

                def first_max(src, w, mx, oh, cand):
                    d(V.tensor_reduce, mx[:, :, 0], src, AX, ALU.max)
                    d(V.tensor_tensor, cand, src, bc(mx, [P, n_t, w]), ALU.is_equal)
                    d(V.tensor_scalar, cand, cand, -1000.0, None, ALU.mult)
                    d(V.tensor_tensor, cand, cand, bc(io[:, 0:w].unsqueeze(1), [P, n_t, w]), ALU.add)
                    d(V.tensor_reduce, red[:, :, 0], cand, AX, ALU.min)
                    d(V.tensor_tensor, oh, cand, bc(red, [P, n_t, w]), ALU.is_equal)

                red, m0, m1, m2 = tile("red", 1), tile("m0", 1), tile("m1", 1), tile("m2", 1)
                oh4, c4, c32 = tile("oh4", 4), tile("c4", 4), tile("c32", 32)
                O = [tile("o1", 32), tile("o2", 32)]
                first_max(lg, 4, m0, oh4[:], c4[:])
                d(V.tensor_tensor, c4[:], lg, bc(m0, [P, n_t, 4]), ALU.subtract)
                t = act(S.activation, c4[:], c4[:], ACT.Exp, after=[last_dve()])
                dve.wait(t)
                pg = tile("pg", 1)
                d(V.tensor_reduce, pg[:, :, 0], c4[:], AX, ALU.add)
                d(V.reciprocal, pg[:], pg[:])
                d(V.tensor_scalar, oh4[:], oh4[:], -NEG, NEG, ALU.mult, ALU.add)
                for n in range(n_t):
                    d(V.tensor_tensor, L[:, n, 4:36].rearrange("p (g e) -> p g e", g=4),
                      L[:, n, 4:36].rearrange("p (g e) -> p g e", g=4),
                      bc(oh4[:, n, :].unsqueeze(2), [P, 4, 8]), ALU.add)
                first_max(le, 32, m1, O[0][:], c32[:])
                d(V.scalar_tensor_tensor, le, O[0][:], 3 * NEG, le, ALU.mult, ALU.add)
                first_max(le, 32, m2, O[1][:], c32[:])
                e2 = tile("e2", 1)
                d(V.tensor_tensor, e2[:], m2[:], m1[:], ALU.subtract)
                t = act(S.activation, e2[:], e2[:], ACT.Exp, after=[last_dve()])
                dve.wait(t)
                d(V.tensor_scalar, m0[:], e2[:], 1.0, None, ALU.add)
                d(V.reciprocal, m0[:], m0[:])
                d(V.tensor_tensor, wts[:, 0, 0:n_t], m0[:, :, 0], pg[:, :, 0], ALU.mult)
                d(V.tensor_tensor, wts[:, 1, 0:n_t], wts[:, 0, 0:n_t], e2[:, :, 0], ALU.mult)
                C = tile("C", 32)
                t = d(V.tensor_tensor, C[:], O[0][:], O[1][:], ALU.add)
                pe.wait(t)
                for n in range(n_t):
                    mm_acc(PS[:, 1, n * 32:(n + 1) * 32],
                           [(tri[:], C[:, n, :])] + [(ones[:], C[:, m, :]) for m in range(n)], sig=False)
                t = mm_acc(PS[:, 2, 0:32], [(ones[:], C[:, m, :]) for m in range(n_t)])
                dve.wait(t)
                R = tile("R", 32)
                d(V.tensor_copy, R[:], PS[:, 1, 0:32 * n_t].rearrange("p (n m) -> p n m", m=32))
                cnt, nov, oend, ost = (sb(s, f"r_{n}", [P, 32]) for n in ("cnt", "nov", "oend", "ost"))
                d(V.tensor_copy, cnt[:], PS[:, 2, 0:32])
                d(V.tensor_scalar, nov[:], cnt[:], float(P), None, ALU.is_gt)
                for j in range(2, MAXJ + 1):
                    d(V.scalar_tensor_tensor, nov[:], cnt[:], float(P * j), nov[:], ALU.is_gt, ALU.add)
                d(V.tensor_tensor_scan, oend[:], ones[:, 0:32], nov[:], 0.0, ALU.mult, ALU.add)
                d(V.tensor_tensor, ost[:], oend[:], nov[:], ALU.subtract)
                d(V.tensor_copy, n_ov[:], oend[:, 31:32])
                oe = sb(s, "r_oe", [P, 16])
                for b in range(NBLK - NEXP):
                    d(V.tensor_scalar, cnt[:], oend[:], float(b), None, ALU.is_le)
                    d(V.tensor_reduce, oe[:, b:b + 1], cnt[:], AX, ALU.add)
                d(V.tensor_scalar, oe[:, 0:NBLK - NEXP], oe[:, 0:NBLK - NEXP], float(NEXP - 1), None, ALU.min)
                d(V.tensor_copy, ov_e[:, 0:NBLK - NEXP], oe[:, 0:NBLK - NEXP])
                rk, ee, oo, jj, bb, pos = (tile(x, 1) for x in ("rk", "ee", "oo", "jj", "bb", "pos"))
                posu = [tile("pu0", 1, U32), tile("pu1", 1, U32)]
                for c in range(2):
                    for dst, src in ((rk, R[:]), (ee, bc(io[:].unsqueeze(1), [P, n_t, 32])),
                                     (oo, bc(ost[:].unsqueeze(1), [P, n_t, 32]))):
                        d(V.tensor_tensor, c32[:], O[c][:], src, ALU.mult)
                        d(V.tensor_reduce, dst[:, :, 0], c32[:], AX, ALU.add)
                    d(V.tensor_scalar, jj[:], rk[:], float(P), None, ALU.is_ge)
                    for j in range(2, MAXJ + 1):
                        d(V.scalar_tensor_tensor, jj[:], rk[:], float(P * j), jj[:], ALU.is_ge, ALU.add)
                    d(V.tensor_tensor, bb[:], oo[:], jj[:], ALU.add)
                    d(V.tensor_tensor, bb[:], bb[:], ee[:], ALU.subtract)
                    d(V.tensor_scalar, bb[:], bb[:], float(NEXP - 1), None, ALU.add)
                    d(V.tensor_scalar, pos[:], jj[:], 0.0, None, ALU.is_gt)
                    d(V.tensor_tensor, bb[:], bb[:], pos[:], ALU.mult)
                    d(V.tensor_tensor, bb[:], bb[:], ee[:], ALU.add)
                    d(V.scalar_tensor_tensor, rk[:], jj[:], -float(P), rk[:], ALU.mult, ALU.add)
                    d(V.scalar_tensor_tensor, pos[:], bb[:], float(P), rk[:], ALU.mult, ALU.add)
                    d(V.tensor_copy, rows[:, c, 0:n_t], pos[:, :, 0])
                    d(V.scalar_tensor_tensor, pos[:], rk[:], float(NBLK), bb[:], ALU.mult, ALU.add)
                    t = d(V.tensor_copy, posu[c][:], pos[:])
                pool.wait(t)
                for c in range(2):
                    for n in range(n_t):
                        t = d_idx.counted(G.indirect_dma_start(
                            table[layer], bass.IndirectOffsetOnAxis(ap=posu[c][:, n, :], axis=0),
                            ids[:, n:n + 1], None))
                sp.dma(d_bc, idx[:], table[layer].rearrange("(p b) a -> p (b a)", p=P), after=[t])
                p.barrier()

        def expert_buffers(st, layer):
            E = {"dram": [A[f"moe_w_{n}_2"][layer] for n in ("gate", "up", "down")]}
            shapes = ([P, KT, DEXP], [P, KT, DEXP], [P, DEXP // P, D])
            E["W"] = [[sb(st, f"W{w}{n}", shapes[w]) for n in range(2)] for w in range(3)]
            E["sW"] = [[Slot(p, f"W{w}{n}") for n in range(2)] for w in range(3)]
            E["ic"] = [sb(st, f"e_ic{j}", [P, 1], U32) for j in range(2)]
            E["aT"] = [sb(st, "e_aT", [P, DEXP])]
            E["xe"], E["y"] = [OT[:, j, :] for j in range(2)], [OT[:, 2 + j, :] for j in range(2)]
            E["xT"] = [OT[:, 4, :].rearrange("p (k c) -> p k c", k=KT)]
            E["sg"] = [OT[:, 5, j * DEXP:(j + 1) * DEXP] for j in range(2)]
            for name in ("ic", "aT", "xe", "y", "xT", "sg"):
                E["s" + name] = [Slot(p, f"e_{name}{j}") for j in range(len(E[name]))]
            return E

        def load_w(E, w, e, n, stream=None):
            sp.take(E["sW"][w][n])
            renew(E["sW"][w][n])
            order = "a (p t) m -> p (a t) m" if w < 2 else "a (t p) m -> p (a t) m"
            E["sW"][w][n].put(sp.dma(stream or d_e[w][n], E["W"][w][n][:],
                                     E["dram"][w][bass.ds(e, 1)].rearrange(order, p=P)))

        def fetch(E, block, n, idx, stream=None):
            dve.take(E["sic"][n])
            renew(E["sic"][n])
            t = dve(V.tensor_copy, E["ic"][n][:], idx[:, bass.ds(block, 1)])
            E["sic"][n].put(t)
            pool.take(E["sxe"][n])
            renew(E["sxe"][n])
            pool.wait(t)
            E["sxe"][n].put((stream or d_x[n]).counted(G.indirect_dma_start(
                E["xe"][n], None, h_dram, bass.IndirectOffsetOnAxis(ap=E["ic"][n][:, 0:1], axis=0))))

        def up_half(E, n, then=None):
            xe, sxe, xT, sxT = E["xe"][n], E["sxe"][n], E["xT"][0], E["sxT"][0]
            sg, ssg = E["sg"][n], E["ssg"][n]
            then = then or (lambda what: None)
            pe.need(sxe)
            act.take(sxT)
            dve.take(sxT)
            renew(sxT)
            x3 = xe.rearrange("s (p t) -> s p t", t=KT)
            for b in range(2):
                pe.take(B[b])
                renew(B[b])
                for j in range(4):
                    t = pe(T.transpose, PS[:, b, j * P:(j + 1) * P], x3[:, :, 4 * b + j], ident[:], sig=(j == 3))
                sxe.got(t)
                E["sic"][n].got(t)
                ev, cp = (act, S.copy) if b else (dve, V.tensor_copy)
                t = ev(cp, xT[:, 4 * b:4 * b + 4, :], PS[:, b, :].rearrange("p (j c) -> p j c", j=4), after=[t])
                B[b].got(t)
                sxT.put(t)
            then("rows")
            bg, bu = 2 + 2 * n, 3 + 2 * n
            pe.need(sxT)
            toks = []
            for w, b in ((0, bg), (1, bu)):
                pe.need(E["sW"][w][n])
                pe.take(B[b])
                renew(B[b])
                t = mm_acc(PS[:, b, :], [(xT[:, k, :], E["W"][w][n][:, k, :]) for k in range(KT)])
                B[b].put(t)
                E["sW"][w][n].got(t)
                toks.append(t)
                then(w)
            sxT.got(t)
            act.take(ssg)
            renew(ssg)
            t = act(S.activation, sg, PS[:, bg, :], ACT.Exp, scale=-1.0, after=[toks[0]])
            t = dve(V.tensor_scalar, sg, sg, 1.0, None, ALU.add, after=[t])
            t = dve(V.reciprocal, sg, sg, after=[t])
            t = dve(V.tensor_tensor, sg, sg, PS[:, bg, :], ALU.mult, after=[t])
            B[bg].got(t)
            t = dve(V.tensor_tensor, sg, sg, PS[:, bu, :], ALU.mult, after=[t, toks[1]])
            B[bu].got(t)
            ssg.put(t)

        def down_half(E, n, block, then=None, stream=None):
            sg, ssg, aT, saT = E["sg"][n], E["ssg"][n], E["aT"][0], E["saT"][0]
            y, sy = E["y"][n], E["sy"][n]
            pe.need(ssg)
            pe.take(B[0])
            renew(B[0])
            for j in range(4):
                t = pe(T.transpose, PS[:, 0, j * P:(j + 1) * P], sg[:, j * P:(j + 1) * P], ident[:], sig=(j == 3))
            ssg.got(t)
            act.take(saT)
            renew(saT)
            t = act(S.copy, aT[:], PS[:, 0, :], after=[t])
            B[0].got(t)
            saT.put(t)
            pe.wait(t)
            pe.need(E["sW"][2][n])
            pe.take(B[6], B[7])
            renew(B[6], B[7])
            act.take(sy)
            dve.take(sy)
            renew(sy)
            for c in range(2):
                t = mm_acc(PS[:, 6 + c, :], [(aT[:, j * P:(j + 1) * P],
                                              E["W"][2][n][:, j, c * 512:c * 512 + 512]) for j in range(4)])
                B[6 + c].put(t)
                ev, cp = (act, S.copy) if c else (dve, V.tensor_copy)
                a = ev(cp, y[:, c * 512:c * 512 + 512], PS[:, 6 + c, :], after=[t])
                B[6 + c].got(a)
                sy.put(a)
            saT.got(t)
            E["sW"][2][n].got(t)
            if then:
                then(2)
            sp.need(sy)
            sy.got(sp.dma(stream or d_y[n], y_dram[bass.ds(block * P, P), :], y))

        def experts(E, layer, idx, n_ov, ov_e):
            def step(e, first=False, more=True, n=None):
                n = e % 2 if n is None else n

                def then(what):
                    if what == "rows":
                        if more:
                            fetch(E, e + 2, n, idx)
                    elif more:
                        load_w(E, what, e + 2, n)
                up_half(E, n, then)
                if not first:
                    down_half(E, 1 - n, e - 1, lambda w: load_w(E, w, e + 1, 1 - n))

            for e in range(2):
                fetch(E, e, e, idx)
            step(0, first=True)
            rounds = (NEXP - 4) // 2
            with p.repeat(f"experts{layer}", rounds) as i:
                step(i * 2 + 1, n=1)
                step(i * 2 + 2, n=0)
            step(NEXP - 3)
            up_half(E, 0)
            down_half(E, 1, NEXP - 3, lambda w: load_w(E, w, NEXP - 1, 1))
            up_half(E, 1)
            down_half(E, 0, NEXP - 2)
            down_half(E, 1, NEXP - 1)
            p.barrier(ahead=True)
            gathers, weights, stores = d_over[layer]
            count = nc.values_load(n_ov[0:1, 0:1], min_val=0, max_val=NBLK - NEXP)
            with p.own_counters(f"over{layer}"):
                with p.repeat(f"overflow{layer}", NBLK - NEXP) as i:
                    with p.while_rounds_left(count > i):
                        e = nc.values_load(ov_e[0:1, bass.ds(i, 1)], engines=(mybir.EngineType.SP,),
                                           min_val=0, max_val=NEXP - 1)
                        for w in range(3):
                            load_w(E, w, e, 0, weights[w])
                        fetch(E, i + NEXP, 0, idx, gathers)
                        up_half(E, 0)
                        down_half(E, 0, i + NEXP, stream=stores)

        moe(0, list(range(NT)))

        modulated_T(1, 0, A["norm_mix_2"][1], range(NT))
        w_na = A["na_w_in_2"][0]
        with ExitStack() as st:
            NH, NR = 16, 15
            bias_t = sb(st, "bias", [P, NH, NR, 64])
            with ExitStack() as s:
                pick = sb(s, "pick", [64, 64 * P])
                rp = sb(s, "rp", [P, 2, 32])
                rT = sb(s, "rT", [64, NH * NR])
                sp.dma(d_bc, pick[:], A["c_na_pick"])
                half = NH * NR // 2
                t = dve(V.memset, rp[:], NEG)
                sp.wait(t)
                flat = A["na_rpb_2"][0].rearrange("h r c -> (h r) c")
                for j in range(2):
                    t = sp.dma(d_bc, rp[0:half, j, 0:31], flat[j * half:(j + 1) * half, :])
                pe.wait(t)
                for j in range(2):
                    t = pe(T.transpose, PS[0:32, 0, j * half:(j + 1) * half], rp[0:half, j, :], ident[0:half, 0:half])
                t = act(S.copy, rT[0:32, :], PS[0:32, 0, 0:2 * half], after=[t])
                t0 = dve(V.memset, rT[32:64, :], 0.0)
                r3 = rT[:].rearrange("x (h r) -> x h r", h=NH)
                t = sp.dma(d_bc, r3[32:64, :, 1:NR], r3[0:32, :, 0:NR - 1], after=[t, t0])
                pe.wait(t)
                s_b = Slot(p, "bias_fill")
                for kc in range(64):
                    b = kc % 8
                    if kc:
                        pe.take(B[b])
                    renew(B[b])
                    t = mm_acc(PS[:, b, 0:NH * NR], [(pick[:, kc * P:(kc + 1) * P], rT[:])])
                    ev, cp = (dve, V.tensor_copy) if kc % 2 else (act, S.copy)
                    t = ev(cp, bias_t[:, :, :, kc], PS[:, b, 0:NH * NR].rearrange("p (h r) -> p h r", h=NH), after=[t])
                    B[b].got(t)
                p.barrier()
            ws = [sb(st, f"ws{n}", [P, KT, 3, P]) for n in range(2)]
            s_ws = [Slot(p, f"ws{n}") for n in range(2)]
            qT = [sb(st, f"nqT{m}", [P, SEQ]) for m in range(2)]
            kz = [sb(st, f"nkz{m}", [P, 2, ALLT]) for m in range(2)]
            vv = [sb(st, f"nv{m}", [P, NT, P]) for m in range(2)]
            s_q, s_k, s_v = ([Slot(p, f"{n}{m}") for m in range(2)] for n in ("nq", "nk", "nv"))
            bufs = softmax_bufs(st, ALLT, 4)
            for m in range(2):
                s_k[m].put(dve(V.memset, kz[m][:], 0.0))

            def load(e, m):
                sp.take(s_ws[m])
                renew(s_ws[m])
                for j in range(3):
                    t = sp.dma(d_qkv[m], ws[m][:, :, j, :], w_cols(w_na, e * P + j * D, P))
                s_ws[m].put(t)

            def project(e, m, ahead):
                w = ws[m]

                def q_step():
                    pe.need(s_ws[m])
                    pe.take(B[7])
                    renew(B[7])
                    t = mm_acc(PS[:, 7, :], [(w[:, k, 0, :], hT[:, k, CTX:ALLT]) for k in range(KT)])
                    s_ws[m].got(t)
                    act.take(s_q[m])
                    renew(s_q[m])
                    t = act(S.activation, qT[m][:], PS[:, 7, :], ACT.Copy, scale=64 ** -0.5, after=[t])
                    B[7].got(t)
                    s_q[m].put(t)

                def k_step(a, z, first):
                    if first:
                        act.take(s_k[m])
                        dve.take(s_k[m])
                        renew(s_k[m])
                    pe.take(B[7])
                    renew(B[7])
                    t = mm_acc(PS[:, 7, 0:z - a], [(w[:, k, 1, :], hT[:, k, a:z]) for k in range(KT)])
                    s_ws[m].got(t)
                    t1 = dve(V.tensor_copy, kz[m][0:64, 0, a:z], PS[0:64, 7, 0:z - a], after=[t])
                    t2 = act(S.copy, kz[m][64:P, 1, a:z], PS[64:P, 7, 0:z - a], after=[t])
                    B[7].got(t1, t2)
                    s_k[m].put(t1, t2)

                def v_step(g0):
                    if g0 == 0:
                        act.take(s_v[m])
                        renew(s_v[m])
                    pe.take(B[7])
                    renew(B[7])
                    for n in range(3):
                        t = mm_acc(PS[:, 7, n * P:(n + 1) * P],
                                   [(hT[:, k, (g0 + n) * P:(g0 + n + 1) * P], w[:, k, 2, :]) for k in range(KT)])
                    s_ws[m].got(t)
                    t = act(S.copy, vv[m][:, g0:g0 + 3, :].rearrange("p a b -> p (a b)"), PS[:, 7, 0:3 * P], after=[t])
                    B[7].got(t)
                    s_v[m].put(t)
                    if g0 and ahead is not None:
                        load(ahead, m)

                (a0, z0), (a1, z1) = spans()
                return dealt(-3, 3, [q_step, lambda: k_step(a0, z0, True), lambda: k_step(a1, z1, False)]) + \
                    dealt(0, 5, [lambda: v_step(0), lambda: v_step(3)])

            def units(e, m):
                out_ = []
                for hh in range(2):
                    for n in range(LT):
                        def scores(o, n=n, hh=hh):
                            q = qT[m][:, n * P:(n + 1) * P]
                            pe(T.matmul, o[:, 0:SEQ], q, kz[m][:, hh, CTX:ALLT], start=True, stop=True, sig=False)
                            return pe(T.matmul, o[:, SEQ:ALLT], q, kz[m][:, hh, 0:CTX], start=True, stop=True)

                        def bias(src, dst, toks, n=n, hh=hh):
                            b4 = bias_t[:].rearrange("p h r c -> p h (r c)")[
                                :, bass.ds(e * 2 + hh, 1), (7 - 2 * n) * 64:(15 - 2 * n) * 64]
                            return [dve(V.tensor_tensor, src[:, 0:SEQ].unsqueeze(1), src[:, 0:SEQ].unsqueeze(1),
                                        b4, ALU.add, after=toks)]

                        out_.append(dict(
                            n=ALLT, scale=1.0, in_place=True, scores=scores, bias=bias,
                            v=lambda j, hh=hh: vv[m][:, (j + CT) % NT, hh * 64:hh * 64 + 64],
                            out=OT[:, CT + n, bass.ds(e * P + hh * 64, 64)]))
                return out_, [s_q[m], s_k[m]], [s_v[m]]

            pipeline("neighbours", NH // 2, 2, load, project, units, 2 * LT,
                     stages(bufs, [[0, 1], [2, 3]], [4, 5], 6, 64))
        with ExitStack() as st:
            rg = row_gates(st, 1, 0, False)
            gate_and_project(st, A["na_w_out_2"][0], None, list(range(CT, NT)), rg)
        moe(1, list(range(CT, NT)))

        with ExitStack() as st:
            norm_rows(st, A["norm_final_2"], range(CT, NT), lambda tl: OT[:, tl, :])
            t = sp.dma(d_st, out[0].rearrange("(t p) d -> p t d", p=P), OT[:, CT:, :])
            sp.wait(t)
            sp.wait(*p.everything())
        return p.found


_NAMES = ["x", "mem", "mem_norm_w", "norm_w", "w_memkv", "w_out", "w_in_a", "w_gate_up", "b_gate", "gla_norm_w",
          "w_in_b", "final_norm_w", "c_2", "ctx_2", "c_ctx_2", "w_ada_2", "b_ada_2", "norm_mix_2", "norm_ffn_2",
          "norm_final_2", "ab_w_in_2", "ab_w_out_2", "mla_q_norm_2", "mla_w_q_up_2", "mla_kv_norm_2",
          "mla_w_kv_up_2", "gqa_q_norm_2", "gqa_k_norm_2", "na_w_in_2", "na_w_out_2", "na_rpb_2", "moe_w_rg_2",
          "moe_b_rg_2", "moe_w_re_2", "moe_b_re_2", "moe_w_gate_2", "moe_w_up_2", "moe_w_down_2"]


def kernel(**inputs):
    import concourse.bacc as _bacc
    from concourse.bass_utils import run_bass_kernel_spmd as _run

    arrays = {f"in_{n}": np.ascontiguousarray(inputs[n]) for n in _NAMES}
    arrays.update({f"in_c_{n}": a for n, a in shape_constants().items()})

    def assemble(plan):
        nc = _bacc.Bacc("TRN2", target_bir_lowering=False, num_devices=1)
        aps = {n[3:]: nc.dram_tensor(n, a.shape, mybir.dt.from_np(a.dtype), kind="ExternalInput").ap()
               for n, a in arrays.items()}
        out = nc.dram_tensor("out", (1, SEQ, D), F32, kind="ExternalOutput").ap()
        return nc, build(nc, aps, out, plan)

    _, plan = assemble(None)
    nc, _ = assemble(plan)
    r = _run(nc, [arrays], core_ids=[0])
    return r.results[0]["out"]
```
